# Optimizing a Trainium2 kernel written in Bass

```python
import jax, jax.numpy as jnp
from jax import lax
import numpy as np

D_MODEL = 1024
BATCH = 1
SEQ = 1024
DEPTH = 1

D_CONV = D_MODEL
CONV_A_WIDTH = 31
D_RNN = 1536
N_RNN_HEADS = 16
RNN_HEAD_DIM = D_RNN // N_RNN_HEADS
CONV_B_WIDTH = 4
LRU_C = 8.0
D_FF = 4 * D_MODEL
EPS = 1e-6

SPLITS = (D_CONV, D_CONV, D_RNN, D_RNN, D_MODEL, D_MODEL)
D_IN = sum(SPLITS)


def rms_norm(x, g):
    xf = x.astype(jnp.float32)
    y = xf * lax.rsqrt(jnp.mean(xf * xf, axis=-1, keepdims=True) + EPS)
    return (y * g.astype(jnp.float32)).astype(x.dtype)

def layer_norm(x, g, b):
    xf = x.astype(jnp.float32)
    mu = jnp.mean(xf, axis=-1, keepdims=True)
    xc = xf - mu
    y = xc * lax.rsqrt(jnp.mean(xc * xc, axis=-1, keepdims=True) + EPS)
    return (y * g.astype(jnp.float32) + b.astype(jnp.float32)).astype(x.dtype)

def causal_depthwise_conv(u, w, b):
    k = w.shape[0]
    y = lax.conv_general_dilated(
        u, w[:, None, :].astype(u.dtype), window_strides=(1,), padding=[(k - 1, 0)],
        dimension_numbers=("NWC", "WIO", "NWC"), feature_group_count=u.shape[-1])
    return y + b

def block_diag_linear(x, w, b):
    bsz, s, c = x.shape
    xh = x.reshape(bsz, s, N_RNN_HEADS, RNN_HEAD_DIM)
    y = jnp.einsum("bshi,hij->bshj", xh, w).reshape(bsz, s, c)
    return y + b

def rg_lru(x, w_a, b_a, w_x, b_x, lam):
    s = x.shape[1]
    r = jax.nn.sigmoid(block_diag_linear(x, w_a, b_a).astype(jnp.float32))
    i = jax.nn.sigmoid(block_diag_linear(x, w_x, b_x).astype(jnp.float32))
    log_a = -LRU_C * r * jax.nn.softplus(-lam.astype(jnp.float32))
    a = jnp.exp(log_a)
    mult = jnp.sqrt(-jnp.expm1(2.0 * log_a))
    is_start = (jnp.arange(s) == 0)[None, :, None]
    mult = jnp.where(is_start, 1.0, mult)
    bterm = mult * i * x.astype(jnp.float32)

    def combine(left, right):
        a_l, b_l = left
        a_r, b_r = right
        return a_r * a_l, a_r * b_l + b_r

    _, h = lax.associative_scan(combine, (a, bterm), axis=1)
    return h.astype(x.dtype)

def first_inputs(seed: int = 0) -> dict:
    key = jax.random.key(seed)
    ks = jax.random.split(key, 32)
    f32 = jnp.float32
    L = DEPTH

    def nrm(k, shape, scale):
        return jax.random.normal(k, shape, f32) * scale

    x = jax.random.normal(ks[0], (BATCH, SEQ, D_MODEL), f32)
    g_mix = 1.0 + nrm(ks[1], (L, D_MODEL), 0.02)
    w_in = nrm(ks[2], (L, D_MODEL, D_IN), D_MODEL ** -0.5)
    b_in = nrm(ks[3], (L, D_IN), 0.02)
    conv_a_w = nrm(ks[4], (L, CONV_A_WIDTH, D_CONV), CONV_A_WIDTH ** -0.5)
    conv_a_b = nrm(ks[5], (L, D_CONV), 0.02)
    ln_g = 1.0 + nrm(ks[6], (L, D_CONV), 0.02)
    ln_b = nrm(ks[7], (L, D_CONV), 0.02)
    w_a_out = nrm(ks[8], (L, D_CONV, D_MODEL), D_CONV ** -0.5)
    conv_b_w = nrm(ks[9], (L, CONV_B_WIDTH, D_RNN), CONV_B_WIDTH ** -0.5)
    conv_b_b = nrm(ks[10], (L, D_RNN), 0.02)
    w_rg_a = nrm(ks[11], (L, N_RNN_HEADS, RNN_HEAD_DIM, RNN_HEAD_DIM), RNN_HEAD_DIM ** -0.5)
    b_rg_a = nrm(ks[12], (L, D_RNN), 0.02)
    w_rg_x = nrm(ks[13], (L, N_RNN_HEADS, RNN_HEAD_DIM, RNN_HEAD_DIM), RNN_HEAD_DIM ** -0.5)
    b_rg_x = nrm(ks[14], (L, D_RNN), 0.02)
    a0 = jax.random.uniform(ks[15], (L, D_RNN), f32, 0.9, 0.999)
    s0 = a0 ** (1.0 / LRU_C)
    lam = jnp.log(s0) - jnp.log1p(-s0)
    w_b_out = nrm(ks[16], (L, D_RNN, D_MODEL), D_RNN ** -0.5)
    w_o = nrm(ks[17], (L, D_MODEL, D_MODEL), D_MODEL ** -0.5)
    g_mlp = 1.0 + nrm(ks[18], (L, D_MODEL), 0.02)
    w_1 = nrm(ks[19], (L, D_MODEL, D_FF), D_MODEL ** -0.5)
    w_2 = nrm(ks[20], (L, D_FF, D_MODEL), D_FF ** -0.5)
    g_final = 1.0 + nrm(ks[21], (D_MODEL,), 0.02)
    return {"x": x, "g_mix": g_mix, "w_in": w_in, "b_in": b_in,
            "conv_a_w": conv_a_w, "conv_a_b": conv_a_b, "ln_g": ln_g, "ln_b": ln_b,
            "w_a_out": w_a_out, "conv_b_w": conv_b_w, "conv_b_b": conv_b_b,
            "w_rg_a": w_rg_a, "b_rg_a": b_rg_a, "w_rg_x": w_rg_x, "b_rg_x": b_rg_x,
            "lam": lam, "w_b_out": w_b_out, "w_o": w_o, "g_mlp": g_mlp,
            "w_1": w_1, "w_2": w_2, "g_final": g_final}

def first_block(x, g_mix, w_in, b_in, conv_a_w, conv_a_b, ln_g, ln_b, w_a_out,
              conv_b_w, conv_b_b, w_rg_a, b_rg_a, w_rg_x, b_rg_x, lam, w_b_out,
              w_o, g_mlp, w_1, w_2, g_final):
    cuts = np.cumsum(SPLITS)[:-1].tolist()
    for l in range(DEPTH):
        h = rms_norm(x, g_mix[l])
        z = jnp.einsum("bsd,de->bse", h, w_in[l]) + b_in[l]
        va, ga, xb, gb, sa, sb = jnp.split(z, cuts, axis=-1)

        u = va * jax.nn.sigmoid(ga)
        u = causal_depthwise_conv(u, conv_a_w[l], conv_a_b[l])
        u = jax.nn.silu(layer_norm(u, ln_g[l], ln_b[l]))
        y_a = jnp.einsum("bsc,cd->bsd", u, w_a_out[l])

        v = causal_depthwise_conv(xb, conv_b_w[l], conv_b_b[l])
        v = rg_lru(v, w_rg_a[l], b_rg_a[l], w_rg_x[l], b_rg_x[l], lam[l])
        y_b = jnp.einsum("bsc,cd->bsd", v * jax.nn.gelu(gb), w_b_out[l])

        m = jax.nn.sigmoid(sa) * y_a + jax.nn.sigmoid(sb) * y_b
        x = x + jnp.einsum("bsd,de->bse", m, w_o[l])

        h = rms_norm(x, g_mlp[l])
        f = jnp.square(jax.nn.relu(jnp.einsum("bsd,df->bsf", h, w_1[l])))
        x = x + jnp.einsum("bsf,fd->bsd", f, w_2[l])
    return rms_norm(x, g_final)


CHUNK = 64
GROUP_W = 512
N_GROUPS = 3
D_MIX = N_GROUPS * GROUP_W
H_A = 4
DH_A = GROUP_W // H_A
CONV_K = 4
POOL_WINDOWS = (2, 4, 8, 16)
N_POOL = len(POOL_WINDOWS)
DC_B = GROUP_W // N_POOL
H_C = 4
DH_C = GROUP_W // H_C
N_MEM = 256

_SIZES = (2 * GROUP_W, GROUP_W, GROUP_W, GROUP_W, 2 * H_A, GROUP_W, GROUP_W, GROUP_W, GROUP_W)
N_IN = sum(_SIZES)
_OFFS = tuple(int(v) for v in np.cumsum(_SIZES)[:-1])


def rmsnorm(x, g):
    xf = x.astype(jnp.float32)
    y = xf * lax.rsqrt(jnp.mean(xf * xf, axis=-1, keepdims=True) + EPS)
    return (y * g.astype(jnp.float32)).astype(x.dtype)

def causal_dwconv(x, w, b):
    S = x.shape[1]
    xp = jnp.pad(x, ((0, 0), (CONV_K - 1, 0), (0, 0)))
    return b + sum(xp[:, j:j + S] * w[j] for j in range(CONV_K))

def mlstm_chunkwise(q, k, v, ig, logf):
    B, S, H, D = q.shape
    NC, L = S // CHUNK, CHUNK
    to_c = lambda a: a.reshape(B, NC, L, H, D).transpose(0, 3, 1, 2, 4)
    q, k, v = to_c(q), to_c(k), to_c(v)
    ig = ig.reshape(B, NC, L, H).transpose(0, 3, 1, 2)
    logf = logf.reshape(B, NC, L, H).transpose(0, 3, 1, 2)
    b = jnp.cumsum(logf, axis=-1)
    bL = b[..., -1]
    g = bL[..., None] - b + ig
    gmax = jnp.max(g, axis=-1)
    w = jnp.exp(g - gmax[..., None])
    kv_loc = jnp.einsum('bhcld,bhcle->bhcde', k * w[..., None], v)
    n_loc = jnp.einsum('bhcld,bhcl->bhcd', k, w)

    def step(carry, inp):
        C, n, m = carry
        kv_c, n_c, bL_c, gmax_c = inp
        m_new = jnp.maximum(bL_c + m, gmax_c)
        a = jnp.exp(bL_c + m - m_new)
        bc = jnp.exp(gmax_c - m_new)
        C_new = a[..., None, None] * C + bc[..., None, None] * kv_c
        n_new = a[..., None] * n + bc[..., None] * n_c
        return (C_new, n_new, m_new), (C, n, m)

    init = (jnp.zeros((B, H, D, D), jnp.float32), jnp.zeros((B, H, D), jnp.float32),
            jnp.zeros((B, H), jnp.float32))
    mv = lambda a: jnp.moveaxis(a, 2, 0)
    _, (C_prev, n_prev, m_prev) = lax.scan(step, init, (mv(kv_loc), mv(n_loc), mv(bL), mv(gmax)))
    C_prev = jnp.moveaxis(C_prev, 0, 2)
    n_prev = jnp.moveaxis(n_prev, 0, 2)
    m_prev = jnp.moveaxis(m_prev, 0, 2)

    causal = jnp.tril(jnp.ones((L, L), dtype=bool))
    dmat = jnp.where(causal, b[..., :, None] - b[..., None, :] + ig[..., None, :], -jnp.inf)
    inter = b + m_prev[..., None]
    m_t = jnp.maximum(inter, jnp.max(dmat, axis=-1))
    s = jnp.einsum('bhcld,bhcsd->bhcls', q, k) * jnp.exp(dmat - m_t[..., None])
    a_t = jnp.exp(inter - m_t)
    num = a_t[..., None] * jnp.einsum('bhcld,bhcde->bhcle', q, C_prev) + jnp.einsum('bhcls,bhcse->bhcle', s, v)
    den = a_t * jnp.einsum('bhcld,bhcd->bhcl', q, n_prev) + jnp.sum(s, axis=-1)
    h = num / jnp.maximum(jnp.abs(den), jnp.exp(-m_t))[..., None]
    return h.transpose(0, 2, 3, 1, 4).reshape(B, S, H, D)

def mlstm_branch(qk_raw, v, o, ig, fg, conv_w, conv_b, norm_g):
    B, S, _ = v.shape
    f32 = jnp.float32
    qk = jax.nn.silu(causal_dwconv(qk_raw, conv_w, conv_b))
    q, k = jnp.split(qk, 2, axis=-1)
    q = q.astype(f32).reshape(B, S, H_A, DH_A)
    k = k.astype(f32).reshape(B, S, H_A, DH_A) * (DH_A ** -0.5)
    vh = v.astype(f32).reshape(B, S, H_A, DH_A)
    h = mlstm_chunkwise(q, k, vh, ig.astype(f32), jax.nn.log_sigmoid(fg.astype(f32)))
    h = jax.nn.sigmoid(o.astype(f32)).reshape(B, S, H_A, DH_A) * h
    h = h * lax.rsqrt(jnp.mean(h * h, axis=-1, keepdims=True) + EPS)
    h = h * norm_g.astype(f32).reshape(H_A, DH_A)
    return h.reshape(B, S, GROUP_W).astype(v.dtype)

def pool_branch(u, w, scale):
    B, S, _ = u.shape
    uf = u.astype(jnp.float32).reshape(B, S, N_POOL, DC_B)
    cs = jnp.cumsum(uf, axis=1)
    t1 = jnp.arange(1, S + 1, dtype=jnp.float32)
    pooled = []
    for gi, win in enumerate(POOL_WINDOWS):
        c = cs[:, :, gi]
        lo = jnp.pad(c, ((0, 0), (win, 0), (0, 0)))[:, :S]
        cnt = jnp.minimum(t1, float(win))[None, :, None]
        pooled.append((c - lo) / cnt)
    p = (jnp.stack(pooled, axis=2) - uf).astype(u.dtype)
    y = jnp.einsum('bsgc,gcd->bsgd', p, w).reshape(B, S, GROUP_W)
    return y * scale

def mem_attn_branch(qc, mem, mem_norm_g, w_kv):
    B, S, _ = qc.shape
    mn = rmsnorm(mem, mem_norm_g)
    kv = mn @ w_kv
    km, vm = jnp.split(kv, 2, axis=-1)
    km = km.reshape(B, N_MEM, H_C, DH_C)
    vm = vm.reshape(B, N_MEM, H_C, DH_C)
    q = qc.reshape(B, S, H_C, DH_C)
    s = jnp.einsum('bshd,bmhd->bhsm', q, km).astype(jnp.float32) * (DH_C ** -0.5)
    p = jax.nn.softmax(s, axis=-1).astype(vm.dtype)
    return jnp.einsum('bhsm,bmhd->bshd', p, vm).reshape(B, S, GROUP_W)

def second_inputs(seed: int = 0) -> dict:
    key = jax.random.key(seed)
    ks = jax.random.split(key, 16)
    nrm = jax.random.normal
    f32 = jnp.float32
    x = nrm(ks[0], (BATCH, SEQ, D_MODEL), f32)
    mem = nrm(ks[1], (BATCH, N_MEM, D_MODEL), f32)
    norm_g = 1.0 + 0.1 * nrm(ks[2], (DEPTH, D_MODEL), f32)
    w_in = nrm(ks[3], (DEPTH, D_MODEL, N_IN), f32) * D_MODEL ** -0.5
    b_i = 0.1 * nrm(ks[4], (DEPTH, H_A), f32)
    b_f = jnp.linspace(3.0, 6.0, H_A, dtype=f32)[None, :] + 0.1 * nrm(ks[5], (DEPTH, H_A), f32)
    b_gates = jnp.concatenate([b_i, b_f], axis=-1)
    conv_w = nrm(ks[6], (DEPTH, CONV_K, 2 * GROUP_W), f32) * CONV_K ** -0.5
    conv_b = 0.02 * nrm(ks[7], (DEPTH, 2 * GROUP_W), f32)
    mlstm_norm_g = 1.0 + 0.1 * nrm(ks[8], (DEPTH, GROUP_W), f32)
    pool_w = nrm(ks[9], (DEPTH, N_POOL, DC_B, DC_B), f32) * DC_B ** -0.5
    pool_scale = 1.0 + 0.1 * nrm(ks[10], (DEPTH, GROUP_W), f32)
    mem_norm_g = 1.0 + 0.1 * nrm(ks[11], (DEPTH, D_MODEL), f32)
    w_mem_kv = nrm(ks[12], (DEPTH, D_MODEL, 2 * GROUP_W), f32) * D_MODEL ** -0.5
    w_out = nrm(ks[13], (DEPTH, D_MIX, D_MODEL), f32) * D_MIX ** -0.5
    final_norm_g = 1.0 + 0.1 * nrm(ks[14], (D_MODEL,), f32)
    return {"x": x, "mem": mem, "norm_g": norm_g, "w_in": w_in, "b_gates": b_gates,
            "conv_w": conv_w, "conv_b": conv_b, "mlstm_norm_g": mlstm_norm_g,
            "pool_w": pool_w, "pool_scale": pool_scale, "mem_norm_g": mem_norm_g,
            "w_mem_kv": w_mem_kv, "w_out": w_out, "final_norm_g": final_norm_g}

def second_block(x, mem, norm_g, w_in, b_gates, conv_w, conv_b, mlstm_norm_g, pool_w, pool_scale,
              mem_norm_g, w_mem_kv, w_out, final_norm_g):
    for l in range(DEPTH):
        h = rmsnorm(x, norm_g[l])
        proj = h @ w_in[l]
        qk_raw, v, o, z_a, gates, u, z_b, qc, z_c = jnp.split(proj, _OFFS, axis=-1)
        gates = gates + b_gates[l]
        ig, fg = gates[..., :H_A], gates[..., H_A:]
        y_a = mlstm_branch(qk_raw, v, o, ig, fg, conv_w[l], conv_b[l], mlstm_norm_g[l]) * jax.nn.silu(z_a)
        y_b = pool_branch(u, pool_w[l], pool_scale[l]) * jax.nn.silu(z_b)
        y_c = mem_attn_branch(qc, mem, mem_norm_g[l], w_mem_kv[l]) * jax.nn.silu(z_c)
        x = x + jnp.concatenate([y_a, y_b, y_c], axis=-1) @ w_out[l]
    return rmsnorm(x, final_norm_g)


def setup_inputs(seed=0):
    out = dict(first_inputs(seed))
    for name, value in second_inputs(seed + 1).items():
        if name != "x":
            out[name + "_2"] = value
    return out


def reference(
    x, g_mix, w_in, b_in, conv_a_w, conv_a_b, ln_g, ln_b, w_a_out, conv_b_w, conv_b_b, w_rg_a,
    b_rg_a, w_rg_x, b_rg_x, lam, w_b_out, w_o, g_mlp, w_1, w_2, g_final, mem_2, norm_g_2,
    w_in_2, b_gates_2, conv_w_2, conv_b_2, mlstm_norm_g_2, pool_w_2, pool_scale_2, mem_norm_g_2,
    w_mem_kv_2, w_out_2, final_norm_g_2,
):
    x = first_block(
        x, g_mix, w_in, b_in, conv_a_w, conv_a_b, ln_g, ln_b, w_a_out, conv_b_w, conv_b_b,
        w_rg_a, b_rg_a, w_rg_x, b_rg_x, lam, w_b_out, w_o, g_mlp, w_1, w_2, g_final,
    )
    return second_block(
        x, mem_2, norm_g_2, w_in_2, b_gates_2, conv_w_2, conv_b_2, mlstm_norm_g_2, pool_w_2,
        pool_scale_2, mem_norm_g_2, w_mem_kv_2, w_out_2, final_norm_g_2,
    )


_drawn_inputs = setup_inputs


def setup_inputs(seed=0):
    import zlib

    import numpy as np

    out = dict(_drawn_inputs(seed))
    spreads = {}
    factors = {'g_mix': 4.681,
     'conv_a_b': 3.622,
     'ln_g': 16.255,
     'ln_b': 26.858,
     'b_rg_a': 8.0,
     'b_rg_x': 8.0,
     'g_mlp': 3.041,
     'conv_b_2': 40.015,
     'mem_norm_g_2': 8.0,
     'mlstm_norm_g_2': 4.378,
     'pool_scale_2': 4.824}
    for name, (base, spread) in spreads.items():
        noise = np.random.default_rng([zlib.crc32(name.encode()), seed]).standard_normal(out[name].shape)
        drawn = base * np.exp(spread * noise) if base else spread * noise
        out[name] = __import__('jax').numpy.asarray(drawn.astype(out[name].dtype))
    for name, factor in factors.items():
        out[name] = (out[name] * factor).astype(out[name].dtype)
    return out
```

```python
import concourse.bass as bass
from concourse import mybir
from contextlib import ExitStack

F32 = mybir.dt.float32
F32R = mybir.dt.float32r
ALU = mybir.AluOpType
ACT = mybir.ActivationFunctionType

P = 128
HALF = 512
KB = 1024

SEQ = 1024
D = 1024
D_RNN = 1536
HEADS, HEAD = 16, 96
TAPS_A, TAPS_B = 31, 4
D_FF = 4096
EPS = 1e-6
LRU_C = 8.0
GROUP = 512
HD = 128
NH = GROUP // HD
TAPS_C = 4
N_MEM = 256
WINDOWS = (2, 4, 8, 16)
NT = SEQ // P
DT = D // P
BIG = 3.0e38

Z_VA, Z_GA, Z_XB, Z_GB, Z_SA, Z_SB = 0, D, 2 * D, 2 * D + D_RNN, 2 * D + 2 * D_RNN, 3 * D + 2 * D_RNN
Y_QK, Y_V, Y_O, Y_ZA = 0, 2 * GROUP, 3 * GROUP, 4 * GROUP
Y_G = 5 * GROUP
Y_U = Y_G + 2 * NH
Y_ZB, Y_QC, Y_ZC = Y_U + GROUP, Y_U + 2 * GROUP, Y_U + 3 * GROUP

PARAMS = [("g_mix", 8), ("b_in", 56), ("conv_a_b", 8), ("ln_g", 8), ("ln_b", 8), ("conv_b_b", 12),
          ("b_rg_a", 12), ("b_rg_x", 12), ("lam", 12), ("conv_b_w", 48), ("conv_a_w", 248), ("g_mlp", 8),
          ("g_final", 8), ("norm_g_2", 8), ("conv_w_2", 32), ("conv_b_2", 8), ("mlstm_norm_g_2", 4),
          ("pool_scale_2", 4), ("mem_norm_g_2", 8)]
ROWS = sum(n for _, n in PARAMS)
assert ROWS == 4 * P


class Queue:

    def __init__(self, sem):
        self.sem, self.count, self.program = sem, 0, []

    def op(self, make, *waits, inc=True):
        self.program.append((list(flat(waits)), make, (self.sem, 1) if inc else None))
        self.count += inc
        return self.sem, self.count

    def dma(self, make, landing, *waits):
        landing.count += 16
        self.program.append((list(flat(waits)), make, (landing.sem, 16)))
        return landing.sem, landing.count

    def wait(self, *waits):
        self.program.append((list(flat(waits)), None, None))

    def play(self, engine):
        passed = {}
        for waits, make, signal in self.program:
            for sem, value in waits:
                if passed.get(id(sem), 0) < value:
                    engine.wait_ge(sem, value)
                    passed[id(sem)] = value
            if make is None:
                continue
            instruction = make(engine)
            if signal:
                instruction.then_inc(*signal)


class Landing:

    def __init__(self, sem):
        self.sem, self.count = sem, 0


def flat(waits):
    for w in waits:
        if isinstance(w, list):
            yield from flat(w)
        elif w is not None:
            yield w


def build_program(nc, A, out, stop=None):
    ctx = ExitStack()
    with ctx:
        sem = lambda name: ctx.enter_context(nc.semaphore(name))
        pe, act, dve, pool, sp = (Queue(sem(f"{n}_done")) for n in ("pe", "act", "dve", "pool", "sp"))
        landing = lambda name: Landing(sem(f"landed_{name}"))

        base = (nc.sbuf_base + 31) // 32 * 32
        sizes = [("const", 6656), ("raw", 8 * KB), ("split", 24 * KB), ("h", 64 * KB), ("y", 32 * KB), ("g", 74272)]
        region, at = {}, base
        for name, size in sizes:
            region[name] = at
            at += size
        assert at <= nc.sbuf_usable_end, (at, nc.sbuf_usable_end)
        ends = dict(zip([n for n, _ in sizes], [region[n] + s for n, s in sizes]))

        def sb(name, where, offset, shape, dt=F32):
            n = 4
            for s in shape[1:]:
                n *= s
            assert region[where] + offset + n <= ends[where], name
            return nc.alloc_sbuf_tensor_at(name, shape, dt, offset=region[where] + offset)

        par = sb("par", "const", 0, [P, ROWS])
        parh = sb("parh", "const", 2048, [P, ROWS])
        ident = sb("ident", "const", 4096, [P, P])
        ones = sb("ones", "const", 4608, [P, 8])
        sp4 = sb("sp4", "const", 4640, [P, 16])
        nsp4 = sb("nsp4", "const", 4704, [P, 16])
        stat = sb("stat", "const", 4768, [P, 32])
        small = sb("small", "const", 4896, [P, 192])
        xcol = sb("xcol", "const", 5664, [P, 32])
        mprev = sb("mprev", "const", 5792, [P, 32])
        wcol = sb("wcol", "const", 5920, [P, 32])
        acol = sb("acol", "const", 6048, [P, 32])
        gcol = sb("gcol", "const", 6176, [P, 16])
        rcnt = sb("rcnt", "const", 6240, [P, 64])
        half_q = sb("half_q", "const", 6496, [P, 16])

        offsets, at = {}, 0
        for name, rows in PARAMS:
            offsets[name] = at
            at += rows
        C = lambda name, j: par[:, offsets[name] + j:offsets[name] + j + 1]
        CH = lambda name, j: parh[:, offsets[name] + j:offsets[name] + j + 1]

        banks = [ctx.enter_context(nc.psum_tensor(f"bank{i}", [P, HALF], F32)) for i in range(8)]
        NB = 7
        free = [[] for _ in range(NB)]
        turn = [0]

        def bank():
            i = turn[0] % NB
            turn[0] += 1
            was = free[i]
            assert was is not None, "the bank's reader isn't known yet"
            free[i] = None
            return i, banks[i], was

        stat_bank = banks[7]
        stat_free = [[]]

        raw = [sb(f"raw{i}", "raw", 4096 * i, [P, 1024]) for i in range(2)]
        whi = [sb(f"whi{i}", "split", 8192 * i, [P, 1024], F32R) for i in range(3)]
        wlo = [sb(f"wlo{i}", "split", 8192 * i + 4096, [P, 1024], F32R) for i in range(3)]
        raw_landed = [landing(f"raw{i}") for i in range(2)]
        raw_free = [None, None]
        split_free = [None, None, None]
        plan = []
        ready = {}
        at_use = [0]

        def load(i):
            key, pieces, kt, cols, clear = plan[i]
            r, n = i % 2, kt * cols
            waits = [raw_free[r]]
            if clear:
                waits = [pool.op(lambda e: e.memset(raw[r][:], 0.0), waits)]
            view = raw[r][:, 0:n].rearrange("p (k c) -> p k c", k=kt)
            for where, src in pieces:
                got = sp.dma(lambda e, d=view[:, :, where[0]:where[1]], s=src: e.dma_start(d, s), raw_landed[r], waits)
            return got

        loads = {}

        def split(i):
            key, pieces, kt, cols, clear = plan[i]
            r, s, n = i % 2, i % 3, kt * cols
            if i not in loads:
                loads[i] = load(i)
            hi = act.op(lambda e: e.activation(whi[s][:, 0:n], raw[r][:, 0:n], ACT.Copy), loads[i], split_free[s])
            lo = dve.op(lambda e: e.tensor_tensor(wlo[s][:, 0:n], raw[r][:, 0:n], whi[s][:, 0:n].bitcast(F32),
                                                  ALU.subtract), hi, split_free[s])
            raw_free[r] = [hi, lo]
            ready[i] = (whi[s][:, 0:n].rearrange("p (k c) -> p k c", k=kt),
                        wlo[s][:, 0:n].rearrange("p (k c) -> p k c", k=kt), [hi, lo])
            if i + 1 < len(plan):
                loads[i + 1] = load(i + 1)

        def weights(key):
            i = at_use[0]
            assert plan[i][0] == key, (plan[i][0], key)
            at_use[0] += 1
            for j in range(i, min(i + 3, len(plan))):
                if j not in ready:
                    if j >= 3 and split_free[j % 3] is None:
                        break
                    split(j)
            assert i in ready
            split_free[i % 3] = None
            return ready[i], i % 3

        def need(key, src, row0, kt, col0, cols):
            piece = src[row0:row0 + kt * P, col0:col0 + cols].rearrange("(k p) c -> p k c", p=P)
            plan.append((key, [((0, cols), piece)], kt, cols, False))

        def product(target, terms, waits, start=True, stop=True):
            last = len(terms) - 1
            done = None
            for n, (lh, ll, rh, rl, tokens) in enumerate(terms):
                for m, (l, r) in enumerate(((lh, rh), (lh, rl), (ll, rh))):
                    first, end = start and n == 0 and m == 0, n == last and m == 2
                    done = pe.op(lambda e, l=l, r=r, a=first, b=end and stop: e.matmul(target, l, r, start=a, stop=b,
                                                                                skip_group_check=True),
                                 waits if n == 0 and m == 0 else [], tokens if m == 0 else [], inc=end)
            return done

        def pair(name, where, offset, n, width=SEQ):
            return ([sb(f"{name}_hi{i}", where, offset + 8 * width * i, [P, width], F32R) for i in range(n)],
                    [sb(f"{name}_lo{i}", where, offset + 8 * width * i + 4 * width, [P, width], F32R) for i in range(n)])

        cut = lambda half: slice(half * HALF, (half + 1) * HALF)

        def split_value(hi, lo, value, waits, over=()):
            a = act.op(lambda e: e.activation(hi, value, ACT.Copy), waits, list(over))
            b = dve.op(lambda e: e.tensor_tensor(lo, value, hi.bitcast(F32), ALU.subtract), a, waits, list(over))
            return [a, b]

        def outputs(key, kt, cols, rhs, tokens, consume, k0=0):
            (hi, lo, got), slot = weights(key)
            for c in range(cols // P):
                for half in range(2):
                    i, b, was = bank()
                    terms = [(hi[:, k, c * P:(c + 1) * P], lo[:, k, c * P:(c + 1) * P], rhs[0][k0 + k][:, cut(half)],
                              rhs[1][k0 + k][:, cut(half)], tokens[k0 + k][half]) for k in range(kt)]
                    done = product(b[:], terms, [was, got])
                    split_free[slot] = done
                    free[i] = [consume(c, half, b, done)]
            return done

        x_rows = A["x"].rearrange("b (t p) d -> p (b t) d", p=P)
        x_in = sb("x_in", "g", 0, [P, NT, D])
        square_out = sb("square_out", "g", 32 * KB, [P, D])
        rows_in = [sb(f"rows_in{i}", "g", 36 * KB + 512 * i, [P, P]) for i in range(4)]
        l_rows, l_x, l_const = landing("rows"), [landing(f"x{t}") for t in range(NT)], landing("const")
        got_ident = sp.dma(lambda e: e.dma_start(ident[:], A["ident"]), l_const)
        got_x = [sp.dma(lambda e, t=t: e.dma_start(x_in[:, t, :], x_rows[:, t, :]), l_x[t]) for t in range(NT)]
        for name, rows in PARAMS:
            a = A[name]
            flat_rows = a.rearrange("l (k p) -> (l k) p", p=P) if len(a.shape) == 2 else (
                a.rearrange("(k p) -> k p", p=P) if len(a.shape) == 1 else a.rearrange("l t (k p) -> (l t k) p", p=P))
            done = 0
            while done < rows:
                at = offsets[name] + done
                n = min(rows - done, P - at % P)
                got_rows = sp.dma(lambda e, at=at, n=n, s=flat_rows[done:done + n, :]: e.dma_start(
                    rows_in[at // P][at % P:at % P + n, :], s), l_rows)
                done += n
        got_consts = dve.op(lambda e: e.memset(ones[:], 1.0))

        i, b, was = bank()
        for s in range(4):
            turned = pe.op(lambda e, s=s: e.transpose(b[:, s * P:(s + 1) * P], rows_in[s][:], ident[:]), got_rows, got_ident)
        got_par = dve.op(lambda e: e.tensor_copy(par[:], b[:]), turned)
        free[i] = [got_par]
        got_parh = dve.op(lambda e: e.tensor_scalar(parh[:], par[:], 0.5, None, ALU.mult), got_par)

        def rstd_of(columns, inv_n, waits):
            v = stat[:, columns]
            t = dve.op(lambda e: e.tensor_scalar(v, v, inv_n, EPS, ALU.mult, ALU.add), waits)
            t = act.op(lambda e: e.activation(v, v, ACT.Sqrt), t)
            return dve.op(lambda e: e.reciprocal(v, v), t)

        h = pair("h", "h", 0, DT)
        h_got = [[None, None] for _ in range(DT)]
        normed = []
        for t in range(NT):
            s = act.op(lambda e, t=t: e.activation(square_out[:], x_in[:, t, :], ACT.Square, accum_out=stat[:, t:t + 1]),
                       got_x[t], (act.sem, act.count) if t else None)
            r = rstd_of(slice(t, t + 1), 1.0 / D, s)
            normed.append(dve.op(lambda e, t=t: e.tensor_scalar(x_in[:, t, :], x_in[:, t, :], stat[:, t:t + 1], None,
                                                                ALU.mult), r))

        def evacuate_split(hi, lo, source, scale, waits):
            a = act.op(lambda e: e.activation(hi, source, ACT.Copy, scale=scale), waits)
            b = dve.op(lambda e: e.scalar_tensor_tensor(lo, source, scale, hi.bitcast(F32), ALU.mult, ALU.subtract), a, waits)
            return [a, b]

        for half in range(2):
            for j in range(DT):
                i, b, was = bank()
                for q in range(4):
                    t = half * 4 + q
                    turned = pe.op(lambda e, t=t, q=q, j=j, b=b: e.transpose(b[:, q * P:(q + 1) * P],
                                   x_in[:, t, j * P:(j + 1) * P], ident[:]), normed[t], was, got_ident)
                h_got[j][half] = evacuate_split(h[0][j][:, cut(half)], h[1][j][:, cut(half)], b[:], C("g_mix", j),
                                                [turned, got_par])
                free[i] = h_got[j][half]
        x_in_read = turned

        w_in = A["w_in"][0]
        w_b_out, w_a_out, w_o = A["w_b_out"][0], A["w_a_out"][0], A["w_o"][0]
        NG, GT = D_RNN // (3 * P), 3

        def plan_xb(g):
            for t in range(GT):
                need(("xb", g, t), w_in, 0, DT, Z_XB + (g * GT + t) * P, P)

        def plan_gb(g):
            for t in range(GT):
                need(("gb", g, t), w_in, 0, DT, Z_GB + (g * GT + t) * P, P)

        plan_xb(0)
        for g in range(NG):
            plan_gb(g)
            if g + 1 < NG:
                plan_xb(g + 1)
            for c in range(4):
                need(("yb", g, c), w_b_out, g * GT * P, GT, c * 2 * P, 2 * P)
        for j in range(DT):
            need(("va", j), w_in, 0, DT, Z_VA + j * P, P)
            need(("ga", j), w_in, 0, DT, Z_GA + j * P, P)
        for j in range(DT):
            need(("sb", j), w_in, 0, DT, Z_SB + j * P, P)
        for j in range(DT):
            need(("sa", j), w_in, 0, DT, Z_SA + j * P, P)
        for j in range(DT):
            need(("ya", j), w_a_out, 0, DT, j * P, P)
        for j in range(DT):
            need(("wo", j), w_o, 0, DT, j * P, P)
        w_1, w_2 = A["w_1"][0], A["w_2"][0]
        FC = D_FF // D
        for f in range(FC):
            for j in range(DT):
                need(("w1", f, j), w_1, 0, DT, (f * DT + j) * P, P)
            for j in range(DT):
                need(("w2", f, j), w_2, f * D, DT, j * P, P)

        yb = [sb(f"yb{j}", "y", 4096 * j, [P, SEQ]) for j in range(DT)]
        o = 0
        xb_in = sb("xb_in", "g", o, [P, SEQ + 8]); o += 4 * (SEQ + 8)
        v = [sb(f"v{t}", "g", o + 4096 * t, [P, SEQ]) for t in range(GT)]; o += 4096 * GT
        G = [sb(f"gelu{t}", "g", o + 4096 * t, [P, SEQ]) for t in range(GT)]; o += 4096 * GT
        vg = pair("vg", "g", o, GT); o += 8192 * GT
        T1, T2, T3 = (sb(f"lru{i}", "g", o + 4096 * i, [P, SEQ]) for i in range(3)); o += 3 * 4096
        PAD_B = TAPS_B - 1

        PAIRS = [(0, 0), (1, 0), (0, 1), (1, 1), (2, 1), (1, 2), (2, 2)]
        gate_w = [sb(f"gate_w{n}", "g", o + 3584 * n, [P, len(PAIRS), P]) for n in range(2)]
        l_gate = [landing(f"gate{n}") for n in range(2)]
        gate_read = [[None], [None]]
        start_gates = [pool.op(lambda e, n=n: e.memset(gate_w[n][:], 0.0), x_in_read) for n in range(2)]

        def load_gates(g):
            got = []
            for n, w in enumerate((A["w_rg_a"][0], A["w_rg_x"][0])):
                for a, c in PAIRS:
                    for q in range(4):
                        r0, r1 = max(q * HEAD, a * P), min((q + 1) * HEAD, (a + 1) * P)
                        c0, c1 = max(q * HEAD, c * P), min((q + 1) * HEAD, (c + 1) * P)
                        if r0 < r1 and c0 < c1:
                            t = sp.dma(lambda e, n=n, a=a, c=c, w=w, q=q, r0=r0, r1=r1, c0=c0, c1=c1: e.dma_start(
                                gate_w[n][r0 - a * P:r1 - a * P, PAIRS.index((a, c)), c0 - c * P:c1 - c * P],
                                w[4 * g + q, r0 - q * HEAD:r1 - q * HEAD, c0 - q * HEAD:c1 - q * HEAD]),
                                l_gate[n], start_gates[n], gate_read[n])
                got.append(t)
            return got

        NR = D_RNN // P
        lam = par[:, offsets["lam"]:offsets["lam"] + NR]
        la, lb, lc, ld = (small[:, 16 * n:16 * n + NR] for n in range(4))
        t = dve.op(lambda e: e.tensor_scalar(la, lam, -1.0, None, ALU.mult), got_par)
        t = dve.op(lambda e: e.tensor_tensor(lb, la, lam, ALU.min), t)
        t = act.op(lambda e: e.activation(lc, lb, ACT.Exp), t)
        t = dve.op(lambda e: e.tensor_scalar(lb, lc, 2.0, None, ALU.add), t)
        t = dve.op(lambda e: e.reciprocal(lb, lb), t)
        t = dve.op(lambda e: e.tensor_tensor(lb, lb, lc, ALU.mult), t)
        t = dve.op(lambda e: e.tensor_tensor(lc, lb, lb, ALU.mult), t)
        t = dve.op(lambda e: e.memset(ld, 1.0 / 17), t)
        for m in (15, 13, 11, 9, 7, 5, 3, 1):
            t = dve.op(lambda e: e.tensor_tensor(ld, ld, lc, ALU.mult), t)
            t = dve.op(lambda e, m=m: e.tensor_scalar(ld, ld, 1.0 / m, None, ALU.add), t)
        t = dve.op(lambda e: e.tensor_tensor(ld, ld, lb, ALU.mult), t)
        t = dve.op(lambda e: e.tensor_scalar(la, la, 0.0, None, ALU.max), t)
        t = dve.op(lambda e: e.scalar_tensor_tensor(la, ld, 2.0, la, ALU.mult, ALU.add), t)
        t = dve.op(lambda e: e.tensor_scalar(sp4[:, 0:NR], la, LRU_C / 2, None, ALU.mult), t)
        got_sp4 = dve.op(lambda e: e.tensor_scalar(nsp4[:, 0:NR], la, -LRU_C / 2, None, ALU.mult), t)

        v_got, v_read = [None] * GT, [[x_in_read]] * GT
        xb_read = [dve.op(lambda e: e.memset(xb_in[:, 0:PAD_B], 0.0), x_in_read)]

        def xb_tiles(g):
            for t in range(GT):
                j = g * GT + t
                evac = []

                def take(c, half, b, done, j=j, evac=evac):
                    evac.append(act.op(lambda e: e.activation(xb_in[:, PAD_B + half * HALF:PAD_B + (half + 1) * HALF], b[:],
                                                              ACT.Identity, bias=C("b_in", Z_XB // P + j)), done, xb_read[0], got_par))
                    return evac[-1]

                outputs(("xb", g, t), DT, P, h, h_got, take)
                for m in range(TAPS_B):
                    w, src = C("conv_b_w", m * NR + j), xb_in[:, m:m + SEQ]
                    if m == 0:
                        d = dve.op(lambda e, w=w, src=src, t=t, j=j: e.tensor_scalar(v[t][:], src, w, C("conv_b_b", j),
                                   ALU.mult, ALU.add), evac, v_read[t])
                    else:
                        d = dve.op(lambda e, w=w, src=src, t=t: e.scalar_tensor_tensor(v[t][:], src, w, v[t][:], ALU.mult,
                                   ALU.add), d)
                xb_read[0], v_got[t] = d, d

        G_got, G_read, T1_read = [None] * GT, [[x_in_read]] * GT, [x_in_read]

        def gb_tiles(g):
            for t in range(GT):
                j = g * GT + t
                evac = []

                def take(c, half, b, done, j=j, t=t, evac=evac):
                    evac.append(act.op(lambda e: e.activation(G[t][:, cut(half)], b[:], ACT.Identity,
                                                              bias=C("b_in", Z_GB // P + j)), done, G_read[t], got_par))
                    return evac[-1]

                outputs(("gb", g, t), DT, P, h, h_got, take)
                s = act.op(lambda e, t=t: e.activation(T1[:], G[t][:], ACT.Square), evac, T1_read[0])
                s = dve.op(lambda e: e.tensor_scalar(T1[:], T1[:], 0.044715, 1.0, ALU.mult, ALU.add), s)
                s = dve.op(lambda e, t=t: e.tensor_tensor(T1[:], T1[:], G[t][:], ALU.mult), s)
                s = act.op(lambda e: e.activation(T1[:], T1[:], ACT.Tanh, scale=0.7978845608028654), s)
                s = dve.op(lambda e, t=t: e.scalar_tensor_tensor(G[t][:], T1[:], 1.0, G[t][:], ALU.add, ALU.mult), s)
                G_got[t], T1_read[0] = s, s

        vg_got, vg_read = [[None, None] for _ in range(GT)], [x_in_read]
        T2_read, T3_read = [x_in_read], [x_in_read]

        def gates(g, got_w):
            for c in range(GT):
                j = g * GT + c
                out_banks = {}
                for n in range(2):
                    rows = [a for a, cc in PAIRS if cc == c]
                    for half in range(2):
                        i, b, was = bank()
                        for m, a in enumerate(rows):
                            done = pe.op(lambda e, n=n, a=a, c=c, m=m, half=half, b=b, rows=rows: e.matmul(
                                b[:], gate_w[n][:, PAIRS.index((a, c)), :], v[a][:, cut(half)], start=m == 0,
                                stop=m == len(rows) - 1), was, got_w[n], v_got[a], inc=m == len(rows) - 1)
                        out_banks[n, half] = (i, b, done)
                        gate_read[n] = done
                tr, ti = [], []
                for half in range(2):
                    i, b, done = out_banks[0, half]
                    tr.append(act.op(lambda e, half=half, b=b, j=j: e.activation(T1[:, cut(half)], b[:], ACT.Tanh,
                              bias=CH("b_rg_a", j), scale=0.5), done, T1_read[0], got_parh))
                for half in range(2):
                    i, b, done = out_banks[1, half]
                    ti.append(act.op(lambda e, half=half, b=b, j=j: e.activation(T3[:, cut(half)], b[:], ACT.Tanh,
                              bias=CH("b_rg_x", j), scale=0.5), done, T3_read[0], got_parh))
                    free[i] = [ti[-1]]
                a_got = act.op(lambda e, j=j: e.activation(T2[:], T1[:], ACT.Exp, scale=nsp4[:, j:j + 1], bias=nsp4[:, j:j + 1]),
                               tr, T2_read[0], got_sp4)
                th = act.op(lambda e, j=j: e.activation(T1[:], T1[:], ACT.Tanh, scale=sp4[:, j:j + 1], bias=sp4[:, j:j + 1]), a_got)
                mm = []
                for half in range(2):
                    i, b, done = out_banks[0, half]
                    q = dve.op(lambda e, half=half, b=b: e.tensor_tensor(b[:], T2[:, cut(half)], T2[:, cut(half)], ALU.mult),
                               a_got, tr)
                    q = dve.op(lambda e, half=half, b=b: e.scalar_tensor_tensor(T1[:, cut(half)], b[:], 1.0, T1[:, cut(half)],
                               ALU.add, ALU.mult), q, th)
                    free[i] = [q]
                    mm.append(q)
                s = act.op(lambda e: e.activation(T1[:], T1[:], ACT.Sqrt), mm)
                s = dve.op(lambda e: e.memset(T1[:, 0:1], 1.0), s)
                q = dve.op(lambda e, c=c: e.scalar_tensor_tensor(T3[:], T3[:], 1.0, v[c][:], ALU.add, ALU.mult), ti)
                v_read[c] = [q, gate_read[0], gate_read[1]]
                q = dve.op(lambda e: e.scalar_tensor_tensor(T3[:], T1[:], 0.5, T3[:], ALU.mult, ALU.mult), s, q)
                q = dve.op(lambda e: e.tensor_tensor_scan(T1[:], T2[:], T3[:], 0.0, ALU.mult, ALU.add), q)
                T2_read[0] = T3_read[0] = q
                q = dve.op(lambda e, c=c: e.scalar_tensor_tensor(T1[:], T1[:], 0.5, G[c][:], ALU.mult, ALU.mult), q, G_got[c])
                G_read[c] = q
                s = split_value(vg[0][c][:], vg[1][c][:], T1[:], [q], [vg_read[0]])
                vg_got[c] = [s, s]
                T1_read[0] = s
            for t in range(GT):
                v_read[t] = [v_read[t], gate_read[0], gate_read[1]]

        yb_got = [[None, None] for _ in range(DT)]

        def yb_tiles(g):
            for c4 in range(4):
                def take(c, half, b, done, c4=c4):
                    j = c4 * 2 + c
                    dst = yb[j][:, cut(half)]
                    if g == 0:
                        yb_got[j][half] = dve.op(lambda e: e.tensor_copy(dst, b[:]), done)
                    else:
                        yb_got[j][half] = dve.op(lambda e: e.tensor_tensor(dst, dst, b[:], ALU.add), done, yb_got[j][half])
                    return yb_got[j][half]
                vg_read[0] = outputs(("yb", g, c4), GT, 2 * P, vg, vg_got, take)

        xb_tiles(0)
        for g in range(NG):
            got_w = load_gates(g)
            gb_tiles(g)
            gates(g, got_w)
            if g + 1 < NG:
                xb_tiles(g + 1)
            yb_tiles(g)

        stage_b = [dve.sem and (dve.sem, dve.count), (act.sem, act.count), (pe.sem, pe.count)]
        uc = [sb(f"uc{j}", "g", 4096 * j, [P, SEQ]) for j in range(DT)]
        sa = [sb(f"sa{j}", "g", 32 * KB + 4096 * j, [P, SEQ]) for j in range(DT)]
        PAD_A = TAPS_A - 1
        u_in = [sb(f"u_in{n}", "g", 64 * KB + 4224 * n, [P, PAD_A + SEQ + 2]) for n in range(2)]
        u_read = [[dve.op(lambda e, n=n: e.memset(u_in[n][:, 0:PAD_A], 0.0), stage_b)] for n in range(2)]
        uc_got = [None] * DT

        def conv_a(j, got):
            src = u_in[j % 2]
            d = got
            for m in range(TAPS_A):
                w, s = C("conv_a_w", m * DT + j), src[:, m:m + SEQ]
                if m == 0:
                    d = dve.op(lambda e, w=w, s=s: e.tensor_scalar(uc[j][:], s, w, C("conv_a_b", j), ALU.mult, ALU.add), d)
                else:
                    d = dve.op(lambda e, w=w, s=s: e.scalar_tensor_tensor(uc[j][:], s, w, uc[j][:], ALU.mult, ALU.add), d)
                yield
            uc_got[j] = d
            u_read[j % 2] = [d]

        todo = []

        def taps(n):
            while n and todo:
                try:
                    next(todo[0])
                    n -= 1
                except StopIteration:
                    todo.pop(0)

        for j in range(DT):
            while len(todo) > 1:
                taps(1)
            if j >= 2 and uc_got[j - 2] is None:
                while uc_got[j - 2] is None:
                    taps(1)
            va_banks = []

            def hold(c, half, b, done):
                va_banks.append((b, done))
                return None
            i0 = turn[0]
            outputs(("va", j), DT, P, h, h_got, hold)
            evac, u_got = [], []

            def take(c, half, b, done, j=j, evac=evac, va_banks=va_banks):
                t = act.op(lambda e: e.activation(uc[j][:, cut(half)], b[:], ACT.Tanh, bias=CH("b_in", Z_GA // P + j), scale=0.5),
                           done, stage_b, got_parh)
                s = dve.op(lambda e: e.tensor_scalar(uc[j][:, cut(half)], uc[j][:, cut(half)], 0.5, 0.5, ALU.mult, ALU.add), t)
                vb, vdone = va_banks[half]
                s = dve.op(lambda e: e.scalar_tensor_tensor(u_in[j % 2][:, PAD_A + half * HALF:PAD_A + (half + 1) * HALF], vb[:],
                           C("b_in", Z_VA // P + j), uc[j][:, cut(half)], ALU.add, ALU.mult), s, vdone, u_read[j % 2])
                u_got.append(s)
                free[(i0 + half) % NB] = [s]
                return t
            outputs(("ga", j), DT, P, h, h_got, take)
            todo.append(conv_a(j, u_got))
            taps(16)
        m_got = [[None, None] for _ in range(DT)]
        for j in range(DT):
            def take(c, half, b, done, j=j):
                t = act.op(lambda e: e.activation(sa[j][:, cut(half)], b[:], ACT.Tanh, bias=CH("b_in", Z_SB // P + j), scale=0.5),
                           done, stage_b)
                s = dve.op(lambda e: e.tensor_scalar(sa[j][:, cut(half)], sa[j][:, cut(half)], 0.5, 0.5, ALU.mult, ALU.add), t)
                m_got[j][half] = dve.op(lambda e: e.tensor_tensor(yb[j][:, cut(half)], yb[j][:, cut(half)], sa[j][:, cut(half)],
                                                                  ALU.mult), s, yb_got[j][half])
                return t
            outputs(("sb", j), DT, P, h, h_got, take)
            taps(8)
        sa_got = [[None, None] for _ in range(DT)]
        for j in range(DT):
            def take(c, half, b, done, j=j):
                t = act.op(lambda e: e.activation(sa[j][:, cut(half)], b[:], ACT.Tanh, bias=CH("b_in", Z_SA // P + j), scale=0.5),
                           done, m_got[j][half])
                sa_got[j][half] = dve.op(lambda e: e.tensor_scalar(sa[j][:, cut(half)], sa[j][:, cut(half)], 0.5, 0.5, ALU.mult,
                                                                   ALU.add), t)
                return t
            h_last = outputs(("sa", j), DT, P, h, h_got, take)
            taps(8)
        while todo:
            taps(1)

        def column_sums(tiles, got, rhs, width, col0=0):
            done = None
            for j in range(len(tiles)):
                for t in range(NT):
                    done = pe.op(lambda e, j=j, t=t: e.matmul(stat_bank[:, width * t:width * (t + 1)],
                                 tiles[j][:, t * P:(t + 1) * P], rhs(j), start=j == 0 and t == 0, stop=j == len(tiles) - 1,
                                 skip_group_check=True), got[j], stat_free[0] if j == 0 else [], inc=t == NT - 1)
            return done

        def spread(column, waits, half):
            i, b, was = bank()
            for q in range(4):
                t = half * 4 + q
                done = pe.op(lambda e, t=t, q=q: e.matmul(b[:, q * P:(q + 1) * P], stat[:, column + t:column + t + 1].broadcast_to([P, P]),
                             ident[:], start=True, stop=True), waits, was, inc=q == 3)
            return i, b, done

        done = column_sums(uc, uc_got, lambda j: ones[:, 0:1], 1)
        t = dve.op(lambda e: e.tensor_scalar(stat[:, 0:NT], stat_bank[:, 0:NT], 1.0 / D, None, ALU.mult), done)
        stat_free[0] = [t]
        centred = [[None, None] for _ in range(DT)]
        sq = [sb(f"sq{n}", "g", 64 * KB + 4224 * n, [P, SEQ]) for n in range(2)]
        for half in range(2):
            i, b, done = spread(0, t, half)
            for j in range(DT):
                centred[j][half] = dve.op(lambda e, j=j, b=b, half=half: e.tensor_tensor(uc[j][:, cut(half)], uc[j][:, cut(half)], b[:],
                                          ALU.subtract), done)
            free[i] = [centred[DT - 1][half]]
        sums = None
        sq_read = [u_read[0], u_read[1]]
        for j in range(DT):
            s = act.op(lambda e, j=j: e.activation(sq[j % 2][:], uc[j][:], ACT.Square), centred[j], sq_read[j % 2], uc_got)
            for t in range(NT):
                done = pe.op(lambda e, j=j, t=t: e.matmul(stat_bank[:, t:t + 1], sq[j % 2][:, t * P:(t + 1) * P], ones[:, 0:1],
                             start=j == 0 and t == 0, stop=j == DT - 1, skip_group_check=True), s, stat_free[0] if j == 0 else [],
                             inc=t == NT - 1)
            sq_read[j % 2] = done
        t = dve.op(lambda e: e.tensor_copy(stat[:, 8:16], stat_bank[:, 0:NT]), done)
        stat_free[0] = [t]
        r = rstd_of(slice(8, 16), 1.0 / D, t)
        un = pair("un", "h", 0, DT)
        un_got = [[None, None] for _ in range(DT)]
        lnz = [sb(f"lnz{n}", "g", 64 * KB + 4224 * n, [P, HALF]) for n in range(2)]
        lnt = [sb(f"lnt{n}", "g", 64 * KB + 4224 * n + 2048, [P, HALF]) for n in range(2)]
        lnz_read = [sq_read, sq_read]
        for half in range(2):
            i, b, done = spread(8, r, half)
            for j in range(DT):
                n = j % 2
                z = dve.op(lambda e, j=j, n=n, b=b, half=half: e.scalar_tensor_tensor(lnz[n][:], uc[j][:, cut(half)], C("ln_g", j),
                           b[:], ALU.mult, ALU.mult), done, lnz_read[n], centred[j][half])
                t = act.op(lambda e, j=j, n=n: e.activation(lnt[n][:], lnz[n][:], ACT.Tanh, bias=CH("ln_b", j), scale=0.5), z,
                           lnz_read[n])
                z = act.op(lambda e, j=j, n=n: e.activation(lnz[n][:], lnz[n][:], ACT.Identity, bias=CH("ln_b", j), scale=0.5), t)
                z = dve.op(lambda e, n=n: e.scalar_tensor_tensor(lnz[n][:], lnt[n][:], 1.0, lnz[n][:], ALU.add, ALU.mult), z)
                un_got[j][half] = split_value(un[0][j][:, cut(half)], un[1][j][:, cut(half)], lnz[n][:], [z], [h_last])
                lnz_read[n] = un_got[j][half]
            free[i] = [z]

        mx = pair("mx", "g", 0, DT)
        mx_got = [[None, None] for _ in range(DT)]
        uc_done = [un_got[j][half] for j in range(DT) for half in range(2)]
        gated = []
        for j in range(DT):
            def take(c, half, b, done, j=j):
                s = dve.op(lambda e: e.tensor_tensor(sa[j][:, cut(half)], sa[j][:, cut(half)], b[:], ALU.mult), done, sa_got[j][half])
                s = dve.op(lambda e: e.tensor_tensor(yb[j][:, cut(half)], yb[j][:, cut(half)], sa[j][:, cut(half)], ALU.add), s,
                           m_got[j][half])
                gated.append(s)
                return s
            un_last = outputs(("ya", j), DT, P, un, un_got, take)
            s = split_value(mx[0][j][:], mx[1][j][:], yb[j][:], gated[-2:], uc_done)
            mx_got[j] = [s, s]

        x1 = [sb(f"x1_{j}", "y", 4096 * j, [P, SEQ]) for j in range(DT)]
        x1_got = [[None, None] for _ in range(DT)]
        xcols = [sb(f"xcols{n}", "g", 64 * KB + 4224 * n, [P, NT, P]) for n in range(2)]
        l_xc = [landing(f"xc{n}") for n in range(2)]
        xc_read = [lnz_read[0], lnz_read[1]]
        for j in range(DT):
            n = j % 2
            got = sp.dma(lambda e, n=n, j=j: e.dma_start(xcols[n][:], x_rows[:, :, j * P:(j + 1) * P]), l_xc[n], xc_read[n], uc_done)
            (hi, lo, wgot), slot = weights(("wo", j))
            for half in range(2):
                i, b, was = bank()
                terms = [(hi[:, k, :], lo[:, k, :], mx[0][k][:, cut(half)], mx[1][k][:, cut(half)], mx_got[k][half])
                         for k in range(DT)]
                split_free[slot] = product(b[:], terms, [was, wgot], stop=False)
                for q in range(4):
                    done = pe.op(lambda e, q=q, b=b, n=n, half=half: e.matmul(b[:, q * P:(q + 1) * P], xcols[n][:, half * 4 + q, :],
                                 ident[:], start=False, stop=q == 3, skip_group_check=True), got, inc=q == 3)
                x1_got[j][half] = act.op(lambda e, b=b, j=j, half=half: e.activation(x1[j][:, cut(half)], b[:], ACT.Copy), done, mx_got[j])
                free[i] = [x1_got[j][half]]
            xc_read[n] = done
        mx_last = done

        def square_sums(tiles, got, rhs, width, buffers, waits):
            read = list(waits)
            for j in range(len(tiles)):
                s = act.op(lambda e, j=j: e.activation(buffers[j % 2][:], tiles[j][:], ACT.Square), got[j], read[j % 2])
                for t in range(NT):
                    done = pe.op(lambda e, j=j, t=t: e.matmul(stat_bank[:, width * t:width * (t + 1)],
                                 buffers[j % 2][:, t * P:(t + 1) * P], rhs(j), start=j == 0 and t == 0, stop=j == len(tiles) - 1,
                                 skip_group_check=True), s, stat_free[0] if j == 0 else [], inc=t == NT - 1)
                read[j % 2] = done
            return done, read

        done, sq_read = square_sums(x1, x1_got, lambda j: ones[:, 0:1], 1, sq, xc_read)
        t = dve.op(lambda e: e.tensor_copy(stat[:, 0:8], stat_bank[:, 0:NT]), done)
        stat_free[0] = [t]
        r = rstd_of(slice(0, 8), 1.0 / D, t)
        h2 = pair("h2", "h", 0, DT)
        h2_got = [[None, None] for _ in range(DT)]
        tmp = [sb(f"tmp{n}", "g", 64 * KB + 2048 * n, [P, HALF]) for n in range(4)]
        tmp_read = [list(sq_read) for _ in range(4)]
        turns = [0]

        def temporary():
            n = turns[0] % 4
            turns[0] += 1
            return n, tmp[n], tmp_read[n]

        def scaled(hl, got, source, source_got, column, gain, r, over):
            for half in range(2):
                i, b, done = spread(column, r, half)
                for j in range(DT):
                    n, tt, was = temporary()
                    z = dve.op(lambda e, j=j, tt=tt, b=b, half=half: e.scalar_tensor_tensor(tt[:], source[j][:, cut(half)], gain(j), b[:],
                               ALU.mult, ALU.mult), done, was, source_got[j][half])
                    got[j][half] = split_value(hl[0][j][:, cut(half)], hl[1][j][:, cut(half)], tt[:], [z], over)
                    tmp_read[n] = got[j][half]
                free[i] = [z]

        scaled(h2, h2_got, x1, x1_got, 0, lambda j: C("g_mlp", j), r, [un_last])
        ff = pair("ff", "g", 0, DT)
        ff_got = [[None, None] for _ in range(DT)]
        ff_read = [mx_last]
        GG, GF2 = small[:, 64:72], gcol[:, :].rearrange("p (j n) -> p j n", n=2)
        g_final, norm_g = (par[:, offsets[n]:offsets[n] + DT] for n in ("g_final", "norm_g_2"))
        t = dve.op(lambda e: e.memset(gcol[:], 1.0))
        gf_got = dve.op(lambda e: e.tensor_tensor(GF2[:, :, 1], g_final, g_final, ALU.mult), t)
        gg_got = dve.op(lambda e: e.tensor_tensor(GG, g_final, norm_g, ALU.mult), got_par)
        NM = N_MEM // P
        mem_in = sb("mem_in", "h", 0, [P, NM, D])
        mem_sq = sb("mem_sq", "h", 8 * KB, [P, D])
        mn = pair("mn", "h", 12 * KB, DT, N_MEM)
        km = sb("km", "g", 0, [P, NH, N_MEM])
        vm = sb("vm", "g", 4 * KB, [P, NM, GROUP])
        l_mem = landing("mem")
        sqm = [sb(f"sqm{n}", "h", 32 * KB + 4096 * n, [P, SEQ]) for n in range(2)]
        sqm_read = [None, None]
        w_in2, w_kv, w_out2 = A["w_in_2"][0], A["w_mem_kv_2"][0], A["w_out_2"][0]
        for c in range(2 * GROUP // P):
            need(("kv", c), w_kv, 0, DT, c * P, P)
        gate_cols = lambda c: w_in2[:, c:c + NH].rearrange("(k p) c -> p k c", p=P)
        plan.append((("gates",), [((0, NH), gate_cols(Y_G)), ((32, 32 + NH), gate_cols(Y_G + NH))], DT, P, True))
        for g in range(NH):
            need(("u", g), w_in2, 0, DT, Y_U + g * P, P)
            need(("zb", g), w_in2, 0, DT, Y_ZB + g * P, P)
            need(("pw", g), A["pool_w_2"][0, g], 0, 1, 0, P)
        for c in range(4):
            need(("ob", c), w_out2, GROUP, NH, c * 2 * P, 2 * P)
        for g in range(NH):
            need(("qc", g), w_in2, 0, DT, Y_QC + g * P, P)
            need(("zc", g), w_in2, 0, DT, Y_ZC + g * P, P)
        for c in range(4):
            need(("oc", c), w_out2, 2 * GROUP, NH, c * 2 * P, 2 * P)
        for j in range(2 * NH):
            need(("qk", j), w_in2, 0, DT, Y_QK + j * P, P)
        for g in range(NH):
            need(("v", g), w_in2, 0, DT, Y_V + g * P, P)
        for g in range(NH):
            need(("o", g), w_in2, 0, DT, Y_O + g * P, P)
        for g in range(NH):
            need(("za", g), w_in2, 0, DT, Y_ZA + g * P, P)
        for c in range(4):
            need(("oa", c), w_out2, 0, NH, c * 2 * P, 2 * P)

        def stat_tile(j, n_last, rhs, width, buffer, over, got):
            s = act.op(lambda e: e.activation(buffer[:], x1[j][:], ACT.Square), got, over)
            for t in range(NT):
                done = pe.op(lambda e, t=t: e.matmul(stat_bank[:, width * t:width * (t + 1)], buffer[:, t * P:(t + 1) * P], rhs,
                             start=j == 0 and t == 0, stop=j == n_last, skip_group_check=True), s,
                             stat_free[0] if j == 0 else [], gf_got, inc=t == NT - 1)
            return done

        for f in range(FC):
            for j in range(DT):
                def take(c, half, b, done, j=j):
                    n, tt, was = temporary()
                    z = act.op(lambda e: e.activation(tt[:], b[:], ACT.Relu), done, was)
                    z2 = dve.op(lambda e: e.tensor_tensor(tt[:], tt[:], tt[:], ALU.mult), z)
                    ff_got[j][half] = split_value(ff[0][j][:, cut(half)], ff[1][j][:, cut(half)], tt[:], [z2], [ff_read[0]])
                    tmp_read[n] = ff_got[j][half]
                    return z
                h2_last = outputs(("w1", f, j), DT, P, h2, h2_got, take)
            if f == FC - 1:
                mem_got = sp.dma(lambda e: e.dma_start(mem_in[:], A["mem_2"][0].rearrange("(t p) d -> p t d", p=P)), l_mem, h2_last)
            for j in range(DT):
                def take(c, half, b, done, j=j):
                    x1_got[j][half] = dve.op(lambda e: e.tensor_tensor(x1[j][:, cut(half)], x1[j][:, cut(half)], b[:], ALU.add), done,
                                             x1_got[j][half])
                    return x1_got[j][half]
                last = outputs(("w2", f, j), DT, P, ff, ff_got, take)
                if f == FC - 1 and j:
                    sqm_read[(j - 1) % 2] = stat_tile(j - 1, DT - 1, GF2[:, j - 1, :], 2, sqm[(j - 1) % 2], [sqm_read[(j - 1) % 2], h2_last],
                                                      x1_got[j - 1])
                if f == FC - 1 and j in (1, 2):
                    t = j - 1
                    s = act.op(lambda e, t=t: e.activation(mem_sq[:], mem_in[:, t, :], ACT.Square, accum_out=stat[:, 16 + t:17 + t]),
                               mem_got, (act.sem, act.count), h2_last)
                    r = rstd_of(slice(16 + t, 17 + t), 1.0 / D, s)
                    mem_normed = dve.op(lambda e, t=t: e.tensor_scalar(mem_in[:, t, :], mem_in[:, t, :], stat[:, 16 + t:17 + t], None,
                                                                       ALU.mult), r)
            ff_read[0] = last
        ff_last = last

        if stop == "first":
            l_out = landing("out")
            for j in range(DT):
                fin = sp.dma(lambda e, j=j: e.dma_start(out[j], x1[j][:]), l_out, x1_got[j])
            sp.wait(fin)
            finish(nc, ctx, pe, act, dve, pool, sp)
            return

        mn_got = [[None, None] for _ in range(DT)]
        for j in range(0, DT, 2):
            i, b, was = bank()
            for q in range(4):
                done = pe.op(lambda e, q=q, j=j, b=b: e.transpose(b[:, q * P:(q + 1) * P], mem_in[:, q % 2, (j + q // 2) * P:(j + q // 2 + 1) * P],
                             ident[:]), mem_normed, was, inc=q == 3)
            for q in range(2):
                was = evacuate_split(mn[0][j + q][:], mn[1][j + q][:], b[:, q * N_MEM:(q + 1) * N_MEM], C("mem_norm_g_2", j + q),
                                     [done, was if q else None])
                mn_got[j + q] = [was, was]
            free[i] = [mn_got[j], mn_got[j + 1]]
        done = stat_tile(DT - 1, DT - 1, GF2[:, DT - 1, :], 2, sqm[(DT - 1) % 2], [sqm_read[(DT - 1) % 2]], x1_got[DT - 1])
        sums = stat_bank[:, 0:2 * NT].rearrange("p (t n) -> p t n", n=2)
        t = dve.op(lambda e: e.tensor_copy(stat[:, 0:NT], sums[:, :, 0]), done)
        t2 = dve.op(lambda e: e.tensor_copy(stat[:, 8:16], sums[:, :, 1]), done)
        stat_free[0] = [t, t2]
        r1 = rstd_of(slice(0, 8), 1.0 / D, t)
        t = dve.op(lambda e: e.tensor_tensor(small[:, 72:80], stat[:, 0:8], stat[:, 0:8], ALU.mult), r1)
        t = dve.op(lambda e: e.tensor_tensor(stat[:, 8:16], stat[:, 8:16], small[:, 72:80], ALU.mult), t)
        r2 = rstd_of(slice(8, 16), 1.0 / D, t)
        r12 = dve.op(lambda e: e.tensor_tensor(stat[:, 8:16], stat[:, 8:16], stat[:, 0:8], ALU.mult), r2)

        km_got = [None] * NH
        vm_got = []
        for c in range(2 * NH):
            (hi, lo, wgot), slot = weights(("kv", c))
            i, b, was = bank()
            if c < NH:
                terms = [(hi[:, k, :], lo[:, k, :], mn[0][k][:], mn[1][k][:], mn_got[k]) for k in range(DT)]
                split_free[slot] = done = product(b[:, 0:N_MEM], terms, [was, wgot])
                km_got[c] = act.op(lambda e, c=c, b=b: e.activation(km[:, c, :], b[:, 0:N_MEM], ACT.Copy), done, ff_last)
                free[i] = [km_got[c]]
            else:
                for q in range(NM):
                    terms = [(mn[0][k][:, q * P:(q + 1) * P], mn[1][k][:, q * P:(q + 1) * P], hi[:, k, :], lo[:, k, :], mn_got[k])
                             for k in range(DT)]
                    split_free[slot] = done = product(b[:, q * P:(q + 1) * P], terms, [was, wgot])
                t = act.op(lambda e, c=c, b=b: e.activation(vm[:, :, (c - NH) * P:(c - NH + 1) * P],
                           b[:, 0:NM * P].rearrange("p (q d) -> p q d", q=NM), ACT.Copy), done, ff_last)
                vm_got.append(t)
                free[i] = [t]
        mem_last = [done, sqm_read]

        h3 = pair("h3", "h", 0, DT)
        h3_got = [[None, None] for _ in range(DT)]
        scaled(h3, h3_got, x1, x1_got, 8, lambda j: GG[:, j:j + 1], [r12, gg_got], mem_last)
        y1, y1_got = x1, [[None, None] for _ in range(DT)]
        for half in range(2):
            i, b, done = spread(0, r1, half)
            for j in range(DT):
                y1_got[j][half] = dve.op(lambda e, j=j, b=b, half=half: e.scalar_tensor_tensor(y1[j][:, cut(half)], x1[j][:, cut(half)],
                                         C("g_final", j), b[:], ALU.mult, ALU.mult), done, h3_got[j][half])
            free[i] = [y1_got[DT - 1][half]]

        row = [sb(f"row{n}", "g", (8 + 17 + 8) * KB + 4096 * n, [P, SEQ]) for n in range(5)]
        bias = small[:, 80:82]
        l_bias = landing("bias")
        bias_got = sp.dma(lambda e: e.dma_start(bias[0:NH, 0:1], A["b_gates_2"][:, 0:NH].rearrange("l n -> n l")), l_bias)
        bias_got = sp.dma(lambda e: e.dma_start(bias[32:32 + NH, 0:1], A["b_gates_2"][:, NH:2 * NH].rearrange("l n -> n l")), l_bias)
        gate_evac = []

        def take(c, half, b, done):
            a = act.op(lambda e: e.activation(row[0][0:NH, cut(half)], b[0:NH, :], ACT.Identity, bias=bias[0:NH, 0:1]), done, bias_got,
                       ff_last)
            f = act.op(lambda e: e.activation(row[1][32:32 + NH, cut(half)], b[32:32 + NH, :], ACT.Identity, bias=bias[32:32 + NH, 0:1]),
                       done, bias_got)
            gate_evac.extend([a, f])
            return [a, f]
        outputs(("gates",), DT, P, h3, h3_got, take)
        R = lambda n: row[n][0:NH, :]
        chunks = lambda n: row[n][0:NH, :].rearrange("p (c t) -> p c t", t=P)
        t = act.op(lambda e: e.activation(R(2), row[1][32:32 + NH, :], ACT.Copy), gate_evac)
        f_got = t
        t = dve.op(lambda e: e.scalar_tensor_tensor(R(3), R(2), -1.0, R(2), ALU.mult, ALU.min), t)
        t = act.op(lambda e: e.activation(R(3), R(3), ACT.Exp), t)
        t = act.op(lambda e: e.activation(R(3), R(3), ACT.Ln, bias=1.0), t)
        t = dve.op(lambda e: e.scalar_tensor_tensor(R(2), R(2), 0.0, R(3), ALU.min, ALU.subtract), t)
        u = dve.op(lambda e: e.memset(R(4), 1.0), ff_last)
        u = dve.op(lambda e: e.memset(chunks(4)[:, :, 0:1], 0.0), u)
        t = dve.op(lambda e: e.tensor_tensor_scan(R(3), R(4), R(2), 0.0, ALU.mult, ALU.add), t, u)
        x_got = dve.op(lambda e: e.tensor_tensor(R(0), R(0), R(3), ALU.subtract), t, gate_evac)
        u = dve.op(lambda e: e.memset(R(4), BIG), t)
        u = dve.op(lambda e: e.memset(chunks(4)[:, :, 0:1], -BIG), u)
        t = dve.op(lambda e: e.tensor_tensor_scan(R(2), R(4), R(0), -BIG, ALU.min, ALU.max), x_got, u)
        mm4, mp4 = small[0:NH, 84:92], small[0:NH, 92:100]
        t = dve.op(lambda e: e.tensor_tensor_scan(mm4, chunks(2)[:, :, P - 1], chunks(3)[:, :, P - 1], 0.0, ALU.max, ALU.add), t)
        u = dve.op(lambda e: e.memset(mp4, 0.0))
        t = dve.op(lambda e: e.tensor_copy(mp4[:, 1:NT], mm4[:, 0:NT - 1]), t, u)
        m_row = dve.op(lambda e: e.tensor_tensor(chunks(1), chunks(2), mp4.unsqueeze(2).broadcast_to([NH, NT, P]), ALU.max), t, f_got)
        nb_row = dve.op(lambda e: e.scalar_tensor_tensor(R(4), R(3), -1.0, R(1), ALU.mult, ALU.subtract), m_row)
        rows_dram = nc.dram_tensor("rows_dram", (2, NH, SEQ), F32).ap()
        mp_dram = nc.dram_tensor("mp_dram", (NH, NT), F32).ap()
        sz_dram = nc.dram_tensor("sz_dram", (NH, P, SEQ), F32).ap()
        l_rowout, l_mb, l_nb, l_mp = landing("rowout"), landing("mb"), landing("nb"), landing("mp")
        rows_out = [sp.dma(lambda e: e.dma_start(rows_dram[0], R(1)), l_rowout, m_row),
                    sp.dma(lambda e: e.dma_start(rows_dram[1], R(4)), l_rowout, nb_row),
                    sp.dma(lambda e: e.dma_start(mp_dram, mp4), l_rowout, m_row)][-1]
        mp_got = sp.dma(lambda e: e.dma_start(mprev[:].rearrange("p (h c) -> p h c", h=NH), mp_dram.partition_broadcast(P)), l_mp, rows_out)
        i, b, was = bank()
        for c in range(NT):
            done = pe.op(lambda e, c=c, b=b: e.transpose(b[:, c * NH:(c + 1) * NH], row[0][0:NH, c * P:(c + 1) * P], ident[0:NH, 0:NH]),
                         x_got, was, inc=c == NT - 1)
        xcol_got = dve.op(lambda e, b=b: e.tensor_copy(xcol[:], b[:, 0:NH * NT]), done)
        free[i] = [xcol_got]
        rows_read = [xcol_got, rows_out, nb_row]

        def silu2(dst, b, done, over, scratch, scratch_read):
            t = act.op(lambda e: e.activation(scratch, b, ACT.Tanh, scale=0.5), done, scratch_read)
            return dve.op(lambda e: e.scalar_tensor_tensor(dst, scratch, 1.0, b, ALU.add, ALU.mult), t, over)

        def add_outputs(key, hl, got):
            for c4 in range(4):
                def take(c, half, b, done, c4=c4):
                    j = c4 * 2 + c
                    y1_got[j][half] = dve.op(lambda e: e.tensor_tensor(y1[j][:, cut(half)], y1[j][:, cut(half)], b[:], ALU.add), done,
                                             y1_got[j][half])
                    return y1_got[j][half]
                last = outputs((key, c4), NH, 2 * P, hl, got, take)
            return last

        PAD_U = 16
        uw = [sb(f"uw{n}", "g", 8 * KB + 4224 * n, [P, PAD_U + SEQ]) for n in range(3)]
        zb = sb("zb", "g", 8 * KB + 4224 * 3, [P, SEQ])
        yp = pair("yp", "g", 25 * KB, NH)
        l_rcnt = landing("rcnt")
        rcnt_got = sp.dma(lambda e: e.dma_start(rcnt[:], A["rcnt"]), l_rcnt)
        yp_got = [[None, None] for _ in range(NH)]
        uw_read = [dve.op(lambda e, n=n: e.memset(uw[n][:, 0:PAD_U], 0.0), ff_last) for n in range(3)]
        zb_read = [ff_last]
        for g, window in enumerate(WINDOWS):
            evac = []

            def take(c, half, b, done):
                evac.append(act.op(lambda e: e.activation(uw[0][:, PAD_U + half * HALF:PAD_U + (half + 1) * HALF], b[:], ACT.Copy), done,
                                   uw_read))
                return evac[-1]
            outputs(("u", g), DT, P, h3, h3_got, take)
            src, step, at = 0, 1, 1
            t = evac
            while step < window:
                dst = 1 if src != 1 else 2
                t = dve.op(lambda e, src=src, dst=dst, step=step, at=at: e.tensor_tensor(uw[dst][:, at:], uw[src][:, at:],
                           uw[src][:, at - step:PAD_U + SEQ - step], ALU.add), t, uw_read)
                src, step = dst, step * 2
                at += step
            t = dve.op(lambda e, src=src, g=g, w=window: e.tensor_tensor(uw[src][:, PAD_U:PAD_U + w], uw[src][:, PAD_U:PAD_U + w],
                       rcnt[:, 16 * g:16 * g + w], ALU.mult), t, rcnt_got)
            t = dve.op(lambda e, src=src, w=window: e.scalar_tensor_tensor(uw[src][:, PAD_U:], uw[src][:, PAD_U:], 1.0 / w,
                       uw[0][:, PAD_U:], ALU.mult, ALU.subtract), t)
            s = split_value(yp[0][g][:], yp[1][g][:], uw[src][:, PAD_U:], [t], [rows_read, ff_last])
            uw_read = s

            def take(c, half, b, done):
                n, tt, was = temporary()
                t = silu2(zb[:, cut(half)], b[:], done, zb_read, tt[:], was)
                tmp_read[n] = t
                zb_got.append(t)
                return t
            zb_got = []
            outputs(("zb", g), DT, P, h3, h3_got, take)
            (hi, lo, wgot), slot = weights(("pw", g))
            held = []
            for half in range(2):
                i, b, was = bank()
                done = product(b[:], [(hi[:, 0, :], lo[:, 0, :], yp[0][g][:, cut(half)], yp[1][g][:, cut(half)], s)], [was, wgot])
                held.append((i, b, done))
            split_free[slot] = done
            zb_read = []
            for half, (i, b, done) in enumerate(held):
                n, tt, was = temporary()
                t = dve.op(lambda e, g=g, tt=tt, b=b, half=half: e.scalar_tensor_tensor(tt[:], b[:], CH("pool_scale_2", g), zb[:, cut(half)],
                           ALU.mult, ALU.mult), done, was, zb_got)
                free[i] = [t]
                zb_read.append(t)
                yp_got[g][half] = split_value(yp[0][g][:, cut(half)], yp[1][g][:, cut(half)], tt[:], [t], [done])
                tmp_read[n] = yp_got[g][half]
        yp_last = add_outputs("ob", yp, yp_got)

        qc = sb("qc", "g", 8 * KB, [P, SEQ])
        zc = sb("zc", "g", 12 * KB, [P, SEQ])
        pr = [sb(f"pr{n}", "g", 16 * KB + 2048 * n, [P, 2, N_MEM]) for n in range(2)]
        pt = sb("pt", "g", 20 * KB, [P, NM, SEQ])
        yc = pair("yc", "g", 28 * KB, NH)
        yc_got = [[None, None] for _ in range(NH)]
        SCALE = float(HD) ** -0.5
        qc_read = zc_read = pt_read = [uw_read, zb_read]
        pr_read = [[uw_read, zb_read], [uw_read, zb_read]]
        for g in range(NH):
            q_got = []

            def take(c, half, b, done):
                q_got.append(act.op(lambda e: e.activation(qc[:, cut(half)], b[:], ACT.Copy), done, qc_read))
                return q_got[-1]
            outputs(("qc", g), DT, P, h3, h3_got, take)
            pt_got = []
            for tp in range(NT // 2):
                n = tp % 2
                i, b, was = bank()
                for q in range(2):
                    done = pe.op(lambda e, q=q, tp=tp, g=g, b=b: e.matmul(b[:, q * N_MEM:(q + 1) * N_MEM], qc[:, (2 * tp + q) * P:(2 * tp + q + 1) * P],
                                 km[:, g, :], start=True, stop=True), was, q_got, km_got[g], inc=q == 1)
                scores = b[:].rearrange("p (q m) -> p q m", q=2)
                top, total = small[:, 100 + 4 * n:102 + 4 * n], small[:, 102 + 4 * n:104 + 4 * n]
                t = dve.op(lambda e, s=scores, top=top: e.tensor_reduce(top, s, mybir.AxisListType.X, ALU.max), done, pr_read[n])
                t = dve.op(lambda e, top=top: e.tensor_scalar(top, top, -SCALE, None, ALU.mult), t)
                for q in range(2):
                    t2 = act.op(lambda e, q=q, n=n, s=scores, top=top, total=total: e.activation(pr[n][:, q, :], s[:, q, :], ACT.Exp,
                                bias=top[:, q:q + 1], scale=SCALE, accum_out=total[:, q:q + 1]), t, pr_read[n])
                free[i] = [t2]
                t = dve.op(lambda e, total=total: e.reciprocal(total, total), t2)
                for q in range(2):
                    t = dve.op(lambda e, q=q, n=n, total=total: e.tensor_scalar(pr[n][:, q, :], pr[n][:, q, :], total[:, q:q + 1], None,
                                                                              ALU.mult), t, t2)
                i, b, was = bank()
                for mt in range(NM):
                    for q in range(2):
                        done = pe.op(lambda e, mt=mt, q=q, n=n, b=b: e.transpose(b[:, (mt * 2 + q) * P:(mt * 2 + q + 1) * P],
                                     pr[n][:, q, mt * P:(mt + 1) * P], ident[:]), was, t, inc=(mt, q) == (NM - 1, 1))
                pr_read[n] = done
                pt_got.append(act.op(lambda e, b=b, tp=tp: e.activation(pt[:, :, tp * 2 * P:(tp + 1) * 2 * P],
                              b[:].rearrange("p (m t) -> p m t", m=NM), ACT.Copy), done, pt_read))
                free[i] = [pt_got[-1]]
            qc_read = done
            zc_got = []

            def take(c, half, b, done):
                n, tt, was = temporary()
                zc_got.append(silu2(zc[:, cut(half)], b[:], done, zc_read, tt[:], was))
                tmp_read[n] = zc_got[-1]
                return zc_got[-1]
            outputs(("zc", g), DT, P, h3, h3_got, take)
            zc_read = []
            for half in range(2):
                i, b, was = bank()
                for mt in range(NM):
                    done = pe.op(lambda e, mt=mt, g=g, b=b, half=half: e.matmul(b[:], vm[:, mt, g * P:(g + 1) * P], pt[:, mt, cut(half)],
                                 start=mt == 0, stop=mt == NM - 1), was, pt_got, vm_got, inc=mt == NM - 1)
                n, tt, was = temporary()
                t = dve.op(lambda e, tt=tt, b=b, half=half: e.scalar_tensor_tensor(tt[:], b[:], 0.5, zc[:, cut(half)], ALU.mult, ALU.mult),
                           done, was, zc_got)
                free[i] = [t]
                zc_read.append(t)
                yc_got[g][half] = split_value(yc[0][g][:, cut(half)], yc[1][g][:, cut(half)], tt[:], [t], [yp_last])
                tmp_read[n] = yc_got[g][half]
            pt_read = done
        yc_last = add_outputs("oc", yc, yc_got)

        q_all = sb("q_all", "g", 0, [P, NH, SEQ])
        k_all = sb("k_all", "g", 16 * KB, [P, NH, SEQ])
        v_tok = sb("v_tok", "g", 32 * KB, [P, NT, NH, P])
        o_all = sb("o_all", "g", 48 * KB, [P, NH, SEQ])
        work = [sb(f"work{n}", "g", 64 * KB + 4224 * n, [P, SEQ + 8]) for n in range(2)]
        before = [yc_last, pt_read, zc_read, yc_got[NH - 1], tmp_read]
        PAD_C = TAPS_C - 1
        work_read = [[dve.op(lambda e, n=n: e.memset(work[n][:, 0:PAD_C], 0.0), before)] for n in range(2)]
        q_got, k_got = [None] * NH, [None] * NH
        for j in range(2 * NH):
            dst = (q_all if j < NH else k_all)[:, j % NH, :]
            evac, w0 = [], work[0]

            def take(c, half, b, done, w0=w0):
                evac.append(act.op(lambda e: e.activation(w0[:, PAD_C + half * HALF:PAD_C + (half + 1) * HALF], b[:], ACT.Copy), done,
                                   work_read[0]))
                return evac[-1]
            outputs(("qk", j), DT, P, h3, h3_got, take)
            t = evac
            for m in range(TAPS_C):
                w, s = CH("conv_w_2", m * 2 * NH + j), w0[:, m:m + SEQ]
                if m == 0:
                    t = dve.op(lambda e, w=w, s=s, j=j, dst=dst: e.tensor_scalar(dst, s, w, CH("conv_b_2", j), ALU.mult, ALU.add), t, before)
                else:
                    t = dve.op(lambda e, w=w, s=s, dst=dst: e.scalar_tensor_tensor(dst, s, w, dst, ALU.mult, ALU.add), t)
            work_read[0] = [t]
            s = act.op(lambda e, dst=dst: e.activation(work[1][:, PAD_C:PAD_C + SEQ], dst, ACT.Tanh), t, work_read[1])
            t = dve.op(lambda e, dst=dst: e.scalar_tensor_tensor(dst, work[1][:, PAD_C:PAD_C + SEQ], 1.0, dst, ALU.add, ALU.mult), s)
            work_read[1] = [t]
            if j >= NH:
                t = dve.op(lambda e, dst=dst: e.tensor_scalar(dst, dst, SCALE, None, ALU.mult), t)
            (q_got if j < NH else k_got)[j % NH] = t
        v_got = []
        for g in range(NH):
            w0, evac, n = work[g % 2], [], g % 2

            def take(c, half, b, done, w0=w0):
                evac.append(act.op(lambda e: e.activation(w0[:, cut(half)], b[:], ACT.Copy), done, work_read[n]))
                return evac[-1]
            outputs(("v", g), DT, P, h3, h3_got, take)
            for half in range(2):
                i, b, was = bank()
                for q in range(4):
                    done = pe.op(lambda e, q=q, b=b, w0=w0, half=half: e.transpose(b[:, q * P:(q + 1) * P],
                                 w0[:, (half * 4 + q) * P:(half * 4 + q + 1) * P], ident[:]), was, evac, inc=q == 3)
                v_got.append(dve.op(lambda e, b=b, g=g, half=half: e.tensor_copy(v_tok[:, half * 4:half * 4 + 4, g, :],
                             b[:].rearrange("p (c d) -> p c d", c=4)), done, before))
                free[i] = [v_got[-1]]
            work_read[n] = [done]
        o_got = []
        for g in range(NH):
            def take(c, half, b, done):
                o_got.append(act.op(lambda e, g=g: e.activation(o_all[:, g, cut(half)], b[:], ACT.Tanh, scale=0.5), done, before))
                return o_got[-1]
            outputs(("o", g), DT, P, h3, h3_got, take)
        l_sz, l_szin = landing("sz"), landing("szin")
        sz_out = None
        for g in range(NH):
            w0, n, parts = work[g % 2], g % 2, []

            def take(c, half, b, done, w0=w0):
                t = act.op(lambda e: e.activation(w0[:, cut(half)], b[:], ACT.Tanh, scale=0.5), done, work_read[n])
                parts.append(dve.op(lambda e: e.scalar_tensor_tensor(w0[:, cut(half)], w0[:, cut(half)], 1.0, b[:], ALU.add, ALU.mult), t))
                return parts[-1]
            h3_last = outputs(("za", g), DT, P, h3, h3_got, take)
            sz_out = sp.dma(lambda e, g=g, w0=w0: e.dma_start(sz_dram[g], w0[:, 0:SEQ]), l_sz, parts)
            work_read[n] = [sz_out]

        mb = sb("mb", "h", 0, [P, NH, SEQ])
        nb = sb("nb", "h", 16 * KB, [P, NH, SEQ])
        mb_got = sp.dma(lambda e: e.dma_start(mb[:], rows_dram[0].partition_broadcast(P)), l_mb, h3_last, rows_out)
        nb_got = sp.dma(lambda e: e.dma_start(nb[:], rows_dram[1].partition_broadcast(P)), l_nb, h3_last, rows_out)
        o = 32 * KB
        names = ["arg", "dec", "qa", "pts", "kts", "dens", "sqs"]
        buf = {}
        for n in range(2):
            for name in names:
                buf[name, n] = sb(f"{name}{n}", "h", o, [P, NH, P]); o += 2048
        mask = sb("mask", "h", o, [P, P]); o += 512
        ones_sq = sb("ones_sq", "h", o, [P, P]); o += 512
        mean_sq = sb("mean_sq", "h", o, [P, P]); o += 512
        state = sb("state", "g", 64 * KB, [P, NH, P])
        nstate = sb("nstate", "g", 66 * KB, [P, 8])
        l_mask = landing("mask")
        mask_got = sp.dma(lambda e: e.dma_start(mask[:], A["mask"]), l_mask, h3_last)
        ones_got = dve.op(lambda e: e.memset(ones_sq[:], 1.0), h3_last)
        mean_got = dve.op(lambda e: e.memset(mean_sq[:], 1.0 / HD), h3_last)
        m_end = mb[:, :, P - 1::P]
        xc_view = xcol[:].rearrange("p (c h) -> p h c", h=NH)
        w_view, a_view = wcol[:].rearrange("p (h c) -> p h c", h=NH), acol[:].rearrange("p (h c) -> p h c", h=NH)
        mp_view = mprev[:].rearrange("p (h c) -> p h c", h=NH)
        t = dve.op(lambda e: e.tensor_tensor(w_view, xc_view, m_end, ALU.subtract), mb_got, xcol_got)
        w_ready = act.op(lambda e: e.activation(wcol[:], wcol[:], ACT.Exp), t)
        t = dve.op(lambda e: e.tensor_tensor(a_view, mp_view, m_end, ALU.subtract), mb_got, mp_got)
        a_ready = act.op(lambda e: e.activation(acol[:], acol[:], ACT.Exp), t)
        read = {k: [] for k in buf}
        state_got, state_read = [], [sz_out, work_read]
        v2_got = []
        for c in range(NT):
            n, tok = c % 2, slice(c * P, (c + 1) * P)
            B = lambda name: buf[name, n]
            mbc = mb[:, :, tok]
            t = dve.op(lambda e, n=n, mbc=mbc: e.tensor_tensor(buf["arg", n][:], mask[:].unsqueeze(1).broadcast_to([P, NH, P]), mbc,
                       ALU.subtract), mask_got, mb_got, read["arg", n])
            for g in range(NH):
                dec = act.op(lambda e, g=g, n=n, c=c: e.activation(buf["dec", n][:, g, :], buf["arg", n][:, g, :], ACT.Exp,
                             bias=xcol[:, c * NH + g:c * NH + g + 1]), t, read["dec", n])
            read["arg", n] = [dec]
            i, b, was = bank()
            for g in range(NH):
                done = pe.op(lambda e, g=g, b=b, tok=tok: e.matmul(b[:, g * P:(g + 1) * P], k_all[:, g, tok], q_all[:, g, tok],
                             start=True, stop=True), was, q_got, k_got, inc=g == NH - 1)
            p_got = dve.op(lambda e, n=n, b=b: e.tensor_tensor(buf["pts", n][:].rearrange("p h t -> p (h t)"), b[:],
                           buf["dec", n][:].rearrange("p h t -> p (h t)"), ALU.mult), done, dec, read["pts", n])
            free[i] = [p_got]
            read["dec", n] = [p_got]
            scores_done = done
            i, b, was = bank()
            for g in range(NH):
                done = pe.op(lambda e, g=g, b=b, tok=tok: e.transpose(b[:, g * P:(g + 1) * P], k_all[:, g, tok], ident[:]), was, k_got,
                             inc=g == NH - 1)
            for g in range(NH):
                kt_got = act.op(lambda e, g=g, n=n, b=b, c=c: e.activation(buf["kts", n][:, g, :], b[:, g * P:(g + 1) * P], ACT.Copy,
                                scale=wcol[:, g * NT + c:g * NT + c + 1]), done, w_ready, read["kts", n])
            free[i] = [kt_got]
            if c:
                for g in range(NH):
                    t = act.op(lambda e, g=g, n=n, c=c, mbc=mbc: e.activation(buf["qa", n][:, g, :], mbc[:, g, :], ACT.Exp, scale=-1.0,
                               bias=mprev[:, g * NT + c:g * NT + c + 1]), mb_got, mp_got, read["qa", n])
                qa_got = dve.op(lambda e, n=n, tok=tok: e.tensor_tensor(buf["qa", n][:], buf["qa", n][:], q_all[:, :, tok], ALU.mult), t,
                                q_got)
            i, b, was = bank()
            for g in range(NH):
                done = pe.op(lambda e, g=g, n=n, b=b, c=c: e.matmul(b[:, g * P:(g + 1) * P], v_tok[:, c, g, :], buf["pts", n][:, g, :],
                             start=True, stop=c == 0, skip_group_check=True), was, p_got, v_got, inc=g == NH - 1)
                if c:
                    done = pe.op(lambda e, g=g, n=n, b=b: e.matmul(b[:, g * P:(g + 1) * P], state[:, g, :], buf["qa", n][:, g, :],
                                 start=False, stop=True, skip_group_check=True), qa_got, state_got, inc=g == NH - 1)
            o_view = o_all[:, :, tok]
            sn = dve.op(lambda e, b=b, o_view=o_view: e.scalar_tensor_tensor(o_view, o_view, 1.0, b[:].rearrange("p (h t) -> p h t", h=NH),
                        ALU.add, ALU.mult), done, o_got)
            free[i] = [sn]
            i, b, was = bank()
            done = pe.op(lambda e, n=n, b=b, c=c: e.matmul(b[:], ones_sq[:], buf["pts", n][:].rearrange("p h t -> p (h t)"), start=True,
                         stop=c == 0, skip_group_check=True), was, p_got, ones_got)
            if c:
                for g in range(NH):
                    done = pe.op(lambda e, g=g, n=n, b=b: e.matmul(b[:, g * P:(g + 1) * P], nstate[:, g:g + 1].broadcast_to([P, P]),
                                 buf["qa", n][:, g, :], start=False, stop=g == NH - 1, skip_group_check=True), qa_got, state_got)
            read["pts", n] = read["qa", n] = [done]
            t = act.op(lambda e, n=n, tok=tok: e.activation(buf["dens", n][:], nb[:, :, tok], ACT.Exp), nb_got, read["dens", n])
            a = act.op(lambda e, b=b: e.activation(b[:], b[:], ACT.Abs), done)
            t = dve.op(lambda e, n=n, b=b: e.tensor_tensor(buf["dens", n][:].rearrange("p h t -> p (h t)"), b[:],
                       buf["dens", n][:].rearrange("p h t -> p (h t)"), ALU.max), t, a)
            free[i] = [t]
            t = act.op(lambda e, n=n: e.activation(buf["dens", n][:], buf["dens", n][:], ACT.Square, scale=2.0 * EPS ** 0.5), t)
            s = act.op(lambda e, n=n, o_view=o_view: e.activation(buf["sqs", n][:], o_view, ACT.Square), sn, read["sqs", n])
            i, b, was = bank()
            for g in range(NH):
                done = pe.op(lambda e, g=g, n=n, b=b, c=c: e.matmul(b[:, g * P:(g + 1) * P], buf["kts", n][:, g, :], v_tok[:, c, g, :],
                             start=True, stop=True), was, kt_got, v_got)
            for g in range(NH):
                done = pe.op(lambda e, g=g, n=n: e.matmul(stat_bank[:, g:g + 1], buf["kts", n][:, g, :], ones[:, 0:1],
                             start=True, stop=True), stat_free[0], inc=g == NH - 1)
            read["kts", n] = [done]
            updates = []
            for g in range(NH):
                if c == 0:
                    updates.append(dve.op(lambda e, g=g, b=b: e.tensor_copy(state[:, g, :], b[:, g * P:(g + 1) * P]), done, state_read))
                    updates.append(dve.op(lambda e, g=g: e.tensor_copy(nstate[:, g:g + 1], stat_bank[:, g:g + 1]), done, state_read))
                else:
                    col = acol[:, g * NT + c:g * NT + c + 1]
                    updates.append(dve.op(lambda e, g=g, b=b, col=col: e.scalar_tensor_tensor(state[:, g, :], state[:, g, :], col,
                                   b[:, g * P:(g + 1) * P], ALU.mult, ALU.add), done, a_ready, state_got))
                    updates.append(dve.op(lambda e, g=g, col=col: e.scalar_tensor_tensor(nstate[:, g:g + 1], nstate[:, g:g + 1], col,
                                   stat_bank[:, g:g + 1], ALU.mult, ALU.add), done, a_ready, state_got))
            free[i] = [updates]
            state_got = updates
            stat_free[0] = [updates]
            i, b, was = bank()
            done = pe.op(lambda e, n=n, b=b: e.matmul(b[:], mean_sq[:], buf["sqs", n][:].rearrange("p h t -> p (h t)"), start=True,
                         stop=True), was, s, mean_got)
            read["sqs", n] = [done]
            v2 = dve.op(lambda e, n=n, b=b, tok=tok: e.tensor_tensor(q_all[:, :, tok], b[:].rearrange("p (h t) -> p h t", h=NH),
                        buf["dens", n][:], ALU.add), done, t, scores_done, qa_got if c else None)
            free[i] = [v2]
            read["dens", n] = [v2]
            v2_got.append(v2)

        sz = sb("sz", "g", 32 * KB, [P, NH, SEQ])
        sz_in = sp.dma(lambda e: e.dma_start(sz[:], sz_dram.rearrange("h p t -> p h t")), l_szin, sz_out, updates, sn)
        ya = pair("ya", "h", 32 * KB, NH)
        ya_got = [[None, None] for _ in range(NH)]
        chunk_last = [read[k] for k in read] + [v2_got]
        roots = [act.op(lambda e, half=half: e.activation(q_all[:, :, cut(half)], q_all[:, :, cut(half)], ACT.Sqrt), v2_got)
                 for half in range(2)]
        for half in range(2):
            for g in range(NH):
                qv, ov = q_all[:, g, cut(half)], o_all[:, g, cut(half)]
                t = dve.op(lambda e, qv=qv: e.reciprocal(qv, qv), roots[half])
                t = dve.op(lambda e, qv=qv, ov=ov, g=g: e.scalar_tensor_tensor(ov, ov, CH("mlstm_norm_g_2", g), qv, ALU.mult, ALU.mult), t)
                t = dve.op(lambda e, ov=ov, g=g, half=half: e.tensor_tensor(ov, ov, sz[:, g, cut(half)], ALU.mult), t, sz_in)
                ya_got[g][half] = split_value(ya[0][g][:, cut(half)], ya[1][g][:, cut(half)], ov, [t], chunk_last)

        x3 = sb("x3", "h", 0, [P, NT, D])
        grow = sb("grow", "g", 64 * KB, [P, D])
        junk = sb("junk", "g", 68 * KB, [P, D])
        l_grow, l_out = landing("grow"), landing("out")
        grow_got = sp.dma(lambda e: e.dma_start(grow[:], A["final_norm_g_2"].partition_broadcast(P)), l_grow, updates, done)
        out_rows = out.rearrange("b (t p) d -> p (b t) d", p=P)
        x3_got = [[] for _ in range(NT)]
        for c in range(4):
            (hi, lo, wgot), slot = weights(("oa", c))
            for t in range(NT):
                half, tok = t // 4, slice(t * P, (t + 1) * P)
                i, b, was = bank()
                terms = [(ya[0][g][:, tok], ya[1][g][:, tok], hi[:, g, :], lo[:, g, :], ya_got[g][half]) for g in range(NH)]
                split_free[slot] = product(b[:, 0:2 * P], terms, [was, wgot], stop=False)
                for q in range(2):
                    j = 2 * c + q
                    done = pe.op(lambda e, q=q, j=j, b=b, tok=tok: e.matmul(b[:, q * P:(q + 1) * P], y1[j][:, tok], ident[:], start=False,
                                 stop=q == 1, skip_group_check=True), y1_got[j][half], inc=q == 1)
                x3_got[t].append(act.op(lambda e, b=b, c=c, t=t: e.activation(x3[:, t, c * 2 * P:(c + 1) * 2 * P], b[:, 0:2 * P], ACT.Copy),
                                        done, chunk_last))
                free[i] = [x3_got[t][-1]]
        stores = []
        for t in range(NT):
            s = act.op(lambda e, t=t: e.activation(junk[:], x3[:, t, :], ACT.Square, accum_out=stat[:, 24 + t:25 + t]), x3_got[t],
                       (act.sem, act.count), updates, done)
            r = rstd_of(slice(24 + t, 25 + t), 1.0 / D, s)
            z = dve.op(lambda e, t=t: e.scalar_tensor_tensor(x3[:, t, :], x3[:, t, :], stat[:, 24 + t:25 + t], grow[:], ALU.mult, ALU.mult),
                       r, grow_got)
            stores.append(sp.dma(lambda e, t=t: e.dma_start(out_rows[:, t, :], x3[:, t, :]), l_out, z))
        sp.wait(stores[-1])
        finish(nc, ctx, pe, act, dve, pool, sp)


def finish(nc, ctx, pe, act, dve, pool, sp):
    block = ctx.enter_context(nc.Block())
    block.sync(lambda e: sp.play(e))
    block.tensor(lambda e: pe.play(e))
    block.scalar(lambda e: act.play(e))
    block.vector(lambda e: dve.play(e))
    block.gpsimd(lambda e: pool.play(e))


def kernel(**inputs):
    import numpy as np
    import concourse.bacc as bacc
    from concourse.bass_utils import run_bass_kernel_spmd

    nc = bacc.Bacc("TRN2", target_bir_lowering=False, num_devices=1)
    arrays, A = {}, {}
    tokens = np.arange(P)
    rcnt = np.ones((P, 16 * NH), np.float32)
    for g, w in enumerate(WINDOWS):
        rcnt[:, 16 * g:16 * g + w] = w / np.arange(1, w + 1, dtype=np.float32)
    constants = {"ident": np.eye(P, dtype=np.float32),
                 "mask": np.where(tokens[:, None] <= tokens[None, :], 0.0, -1.0e30).astype(np.float32),
                 "rcnt": rcnt}
    for name, a in [*inputs.items(), *constants.items()]:
        a = np.ascontiguousarray(a)
        arrays[f"in_{name}"] = a
        A[name] = nc.dram_tensor(f"in_{name}", a.shape, mybir.dt.from_np(a.dtype), kind="ExternalInput").ap()
    out = nc.dram_tensor("out_0", (1, SEQ, D), F32, kind="ExternalOutput").ap()
    build_program(nc, A, out)
    result = run_bass_kernel_spmd(nc, [arrays], core_ids=[0])
    return result.results[0]["out_0"]
```

```python
import concourse.bass as bass
from concourse import mybir
from contextlib import ExitStack

F32 = mybir.dt.float32
F32R = mybir.dt.float32r
ALU = mybir.AluOpType
ACT = mybir.ActivationFunctionType

P = 128
HALF = 512
KB = 1024

SEQ = 1024
D = 1024
D_RNN = 1536
HEADS, HEAD = 16, 96
TAPS_A, TAPS_B = 31, 4
LAG = 1
D_FF = 4096
EPS = 1e-6
LRU_C = 8.0
GROUP = 512
HD = 128
NH = GROUP // HD
TAPS_C = 4
N_MEM = 256
WINDOWS = (2, 4, 8, 16)
NT = SEQ // P
DT = D // P
BIG = 3.0e38

Z_VA, Z_GA, Z_XB, Z_GB, Z_SA, Z_SB = 0, D, 2 * D, 2 * D + D_RNN, 2 * D + 2 * D_RNN, 3 * D + 2 * D_RNN
Y_QK, Y_V, Y_O, Y_ZA = 0, 2 * GROUP, 3 * GROUP, 4 * GROUP
Y_G = 5 * GROUP
Y_U = Y_G + 2 * NH
Y_ZB, Y_QC, Y_ZC = Y_U + GROUP, Y_U + 2 * GROUP, Y_U + 3 * GROUP

PARAMS = [("g_mix", 8), ("b_in", 56), ("conv_a_b", 8), ("ln_g", 8), ("ln_b", 8), ("conv_b_b", 12),
          ("b_rg_a", 12), ("b_rg_x", 12), ("lam", 12), ("conv_b_w", 48), ("conv_a_w", 248), ("g_mlp", 8),
          ("g_final", 8), ("norm_g_2", 8), ("conv_w_2", 32), ("conv_b_2", 8), ("mlstm_norm_g_2", 4),
          ("pool_scale_2", 4), ("mem_norm_g_2", 8)]
ROWS = sum(n for _, n in PARAMS)
assert ROWS == 4 * P


class Queue:

    def __init__(self, sem):
        self.sem, self.count, self.program = sem, 0, []

    def op(self, make, *waits, inc=True):
        self.program.append((list(flat(waits)), make, (self.sem, 1) if inc else None))
        self.count += inc
        return self.sem, self.count

    def dma(self, make, landing, *waits):
        landing.count += 16
        self.program.append((list(flat(waits)), make, (landing.sem, 16)))
        return landing.sem, landing.count

    def wait(self, *waits):
        self.program.append((list(flat(waits)), None, None))

    def play(self, engine):
        passed = {}
        for waits, make, signal in self.program:
            for sem, value in waits:
                if passed.get(id(sem), 0) < value:
                    engine.wait_ge(sem, value)
                    passed[id(sem)] = value
            if make is None:
                continue
            instruction = make(engine)
            if signal:
                instruction.then_inc(*signal)


class Landing:

    def __init__(self, sem):
        self.sem, self.count = sem, 0


def flat(waits):
    for w in waits:
        if isinstance(w, list):
            yield from flat(w)
        elif w is not None:
            yield w


def build_program(nc, A, out, stop=None):
    ctx = ExitStack()
    with ctx:
        sem = lambda name: ctx.enter_context(nc.semaphore(name))
        pe, act, dve, pool, sp = (Queue(sem(f"{n}_done")) for n in ("pe", "act", "dve", "pool", "sp"))
        landing = lambda name: Landing(sem(f"landed_{name}"))

        base = (nc.sbuf_base + 31) // 32 * 32
        sizes = [("const", 7168), ("raw", 8 * KB), ("split", 24 * KB), ("h", 64 * KB), ("y", 32 * KB), ("g", 74272)]
        region, at = {}, base
        for name, size in sizes:
            region[name] = at
            at += size
        assert at <= nc.sbuf_usable_end, (at, nc.sbuf_usable_end)
        ends = dict(zip([n for n, _ in sizes], [region[n] + s for n, s in sizes]))

        def sb(name, where, offset, shape, dt=F32):
            n = 4
            for s in shape[1:]:
                n *= s
            assert region[where] + offset + n <= ends[where], name
            return nc.alloc_sbuf_tensor_at(name, shape, dt, offset=region[where] + offset)

        par = sb("par", "const", 0, [P, ROWS])
        parh = sb("parh", "const", 2048, [P, ROWS])
        ident = sb("ident", "const", 4096, [P, P])
        ones = sb("ones", "const", 4608, [P, 8])
        sp4 = sb("sp4", "const", 4640, [P, 16])
        nsp4 = sb("nsp4", "const", 4704, [P, 16])
        stat = sb("stat", "const", 4768, [P, 32])
        small = sb("small", "const", 4896, [P, 192])
        xcol = sb("xcol", "const", 5664, [P, 32])
        mprev = sb("mprev", "const", 5792, [P, 32])
        wcol = sb("wcol", "const", 5920, [P, 32])
        acol = sb("acol", "const", 6048, [P, 32])
        gcol = sb("gcol", "const", 6176, [P, 16])
        rcnt = sb("rcnt", "const", 6240, [P, 64])
        mask = sb("mask", "const", 6528, [P, P])

        offsets, at = {}, 0
        for name, rows in PARAMS:
            offsets[name] = at
            at += rows
        C = lambda name, j: par[:, offsets[name] + j:offsets[name] + j + 1]
        CH = lambda name, j: parh[:, offsets[name] + j:offsets[name] + j + 1]

        banks = [ctx.enter_context(nc.psum_tensor(f"bank{i}", [P, HALF], F32)) for i in range(8)]
        NB = 7
        free = [[] for _ in range(NB)]
        turn = [0]

        def bank():
            i = turn[0] % NB
            turn[0] += 1
            was = free[i]
            assert was is not None, "the bank's reader isn't known yet"
            free[i] = None
            return i, banks[i], was

        stat_bank = banks[7]
        stat_free = [[]]

        raw = [sb(f"raw{i}", "raw", 4096 * i, [P, 1024]) for i in range(2)]
        whi = [sb(f"whi{i}", "split", 8192 * i, [P, 1024], F32R) for i in range(3)]
        wlo = [sb(f"wlo{i}", "split", 8192 * i + 4096, [P, 1024], F32R) for i in range(3)]
        raw_landed = [landing(f"raw{i}") for i in range(2)]
        raw_free = [None, None]
        split_free = [None, None, None]
        plan = []
        ready = {}
        at_use = [0]

        def load(i):
            key, pieces, kt, cols, clear = plan[i]
            r, n = i % 2, kt * cols
            waits = [raw_free[r]]
            if clear:
                waits = [pool.op(lambda e: e.memset(raw[r][:], 0.0), waits)]
            view = raw[r][:, 0:n].rearrange("p (k c) -> p k c", k=kt)
            for where, src in pieces:
                got = sp.dma(lambda e, d=view[:, :, where[0]:where[1]], s=src: e.dma_start(d, s), raw_landed[r], waits)
            return got

        loads = {}

        def split(i):
            key, pieces, kt, cols, clear = plan[i]
            r, s, n = i % 2, i % 3, kt * cols
            if i not in loads:
                loads[i] = load(i)
            hi = act.op(lambda e: e.activation(whi[s][:, 0:n], raw[r][:, 0:n], ACT.Copy), loads[i], split_free[s])
            lo = dve.op(lambda e: e.tensor_tensor(wlo[s][:, 0:n], raw[r][:, 0:n], whi[s][:, 0:n].bitcast(F32),
                                                  ALU.subtract), hi, split_free[s])
            raw_free[r] = [hi, lo]
            ready[i] = (whi[s][:, 0:n].rearrange("p (k c) -> p k c", k=kt),
                        wlo[s][:, 0:n].rearrange("p (k c) -> p k c", k=kt), [hi, lo])
            if i + 1 < len(plan):
                loads[i + 1] = load(i + 1)

        def weights(key):
            i = at_use[0]
            assert plan[i][0] == key, (plan[i][0], key)
            at_use[0] += 1
            for j in range(i, min(i + 3, len(plan))):
                if j not in ready:
                    if j >= 3 and split_free[j % 3] is None:
                        break
                    split(j)
            assert i in ready
            split_free[i % 3] = None
            return ready[i], i % 3

        def need(key, src, row0, kt, col0, cols):
            piece = src[row0:row0 + kt * P, col0:col0 + cols].rearrange("(k p) c -> p k c", p=P)
            plan.append((key, [((0, cols), piece)], kt, cols, False))

        def product(target, terms, waits, start=True, stop=True):
            last = len(terms) - 1
            done = None
            for n, (lh, ll, rh, rl, tokens) in enumerate(terms):
                for m, (l, r) in enumerate(((lh, rh), (lh, rl), (ll, rh))):
                    first, end = start and n == 0 and m == 0, n == last and m == 2
                    done = pe.op(lambda e, l=l, r=r, a=first, b=end and stop: e.matmul(target, l, r, start=a, stop=b,
                                                                                skip_group_check=True),
                                 waits if n == 0 and m == 0 else [], tokens if m == 0 else [], inc=end)
            return done

        def pair(name, where, offset, n, width=SEQ):
            return ([sb(f"{name}_hi{i}", where, offset + 8 * width * i, [P, width], F32R) for i in range(n)],
                    [sb(f"{name}_lo{i}", where, offset + 8 * width * i + 4 * width, [P, width], F32R) for i in range(n)])

        cut = lambda half: slice(half * HALF, (half + 1) * HALF)

        def split_value(hi, lo, value, waits, over=()):
            a = act.op(lambda e: e.activation(hi, value, ACT.Copy), waits, list(over))
            b = dve.op(lambda e: e.tensor_tensor(lo, value, hi.bitcast(F32), ALU.subtract), a, waits, list(over))
            return [a, b]

        def outputs(key, kt, cols, rhs, tokens, consume, k0=0):
            (hi, lo, got), slot = weights(key)
            for c in range(cols // P):
                for half in range(2):
                    i, b, was = bank()
                    terms = [(hi[:, k, c * P:(c + 1) * P], lo[:, k, c * P:(c + 1) * P], rhs[0][k0 + k][:, cut(half)],
                              rhs[1][k0 + k][:, cut(half)], tokens[k0 + k][half]) for k in range(kt)]
                    done = product(b[:], terms, [was, got])
                    split_free[slot] = done
                    read = consume(c, half, b, done)
                    free[i] = None if read is None else [read]
            return done

        x_rows = A["x"].rearrange("b (t p) d -> p (b t) d", p=P)
        x_in = sb("x_in", "g", 0, [P, NT, D])
        square_out = sb("square_out", "g", 32 * KB, [P, D])
        rows_in = [sb(f"rows_in{i}", "g", 36 * KB + 512 * i, [P, P]) for i in range(4)]
        l_rows, l_x, l_const = landing("rows"), [landing(f"x{t}") for t in range(NT)], landing("const")
        got_ident = sp.dma(lambda e: e.dma_start(ident[:], A["ident"]), l_const)
        mask_got = sp.dma(lambda e: e.dma_start(mask[:], A["mask"]), landing("mask"))
        got_x = [sp.dma(lambda e, t=t: e.dma_start(x_in[:, t, :], x_rows[:, t, :]), l_x[t]) for t in range(NT)]
        for name, rows in PARAMS:
            a = A[name]
            flat_rows = a.rearrange("l (k p) -> (l k) p", p=P) if len(a.shape) == 2 else (
                a.rearrange("(k p) -> k p", p=P) if len(a.shape) == 1 else a.rearrange("l t (k p) -> (l t k) p", p=P))
            done = 0
            while done < rows:
                at = offsets[name] + done
                n = min(rows - done, P - at % P)
                got_rows = sp.dma(lambda e, at=at, n=n, s=flat_rows[done:done + n, :]: e.dma_start(
                    rows_in[at // P][at % P:at % P + n, :], s), l_rows)
                done += n
        got_consts = dve.op(lambda e: e.memset(ones[:], 1.0))

        i, b, was = bank()
        for s in range(4):
            turned = pe.op(lambda e, s=s: e.transpose(b[:, s * P:(s + 1) * P], rows_in[s][:], ident[:]), got_rows, got_ident)
        got_par = dve.op(lambda e: e.tensor_copy(par[:], b[:]), turned)
        free[i] = [got_par]
        got_parh = dve.op(lambda e: e.tensor_scalar(parh[:], par[:], 0.5, None, ALU.mult), got_par)

        def rstd_of(columns, inv_n, waits):
            v = stat[:, columns]
            t = dve.op(lambda e: e.tensor_scalar(v, v, inv_n, EPS, ALU.mult, ALU.add), waits)
            t = act.op(lambda e: e.activation(v, v, ACT.Sqrt), t)
            return dve.op(lambda e: e.reciprocal(v, v), t)

        h = pair("h", "h", 0, DT)
        h_got = [[None, None] for _ in range(DT)]
        normed = []
        for t in range(NT):
            s = act.op(lambda e, t=t: e.activation(square_out[:], x_in[:, t, :], ACT.Square, accum_out=stat[:, t:t + 1]),
                       got_x[t], (act.sem, act.count) if t else None)
            r = rstd_of(slice(t, t + 1), 1.0 / D, s)
            normed.append(dve.op(lambda e, t=t: e.tensor_scalar(x_in[:, t, :], x_in[:, t, :], stat[:, t:t + 1], None,
                                                                ALU.mult), r))

        def evacuate_split(hi, lo, source, scale, waits):
            a = act.op(lambda e: e.activation(hi, source, ACT.Copy, scale=scale), waits)
            b = dve.op(lambda e: e.scalar_tensor_tensor(lo, source, scale, hi.bitcast(F32), ALU.mult, ALU.subtract), a, waits)
            return [a, b]

        for half in range(2):
            for j in range(DT):
                i, b, was = bank()
                for q in range(4):
                    t = half * 4 + q
                    turned = pe.op(lambda e, t=t, q=q, j=j, b=b: e.transpose(b[:, q * P:(q + 1) * P],
                                   x_in[:, t, j * P:(j + 1) * P], ident[:]), normed[t], was, got_ident)
                h_got[j][half] = evacuate_split(h[0][j][:, cut(half)], h[1][j][:, cut(half)], b[:], C("g_mix", j),
                                                [turned, got_par])
                free[i] = h_got[j][half]
        x_in_read = turned

        w_in = A["w_in"][0]
        w_b_out, w_a_out, w_o = A["w_b_out"][0], A["w_a_out"][0], A["w_o"][0]
        NG, GT = D_RNN // (3 * P), 3

        def plan_xb(g):
            for t in range(GT):
                need(("xb", g, t), w_in, 0, DT, Z_XB + (g * GT + t) * P, P)

        def plan_gb(g):
            for t in range(GT):
                need(("gb", g, t), w_in, 0, DT, Z_GB + (g * GT + t) * P, P)

        def plan_a(names, j):
            for name, col in (("va", Z_VA), ("ga", Z_GA), ("sb", Z_SB), ("sa", Z_SA)):
                if name in names:
                    need((name, j), w_in, 0, DT, col + j * P, P)

        plan_xb(0)
        for g in range(NG):
            plan_gb(g)
            if g + 1 < NG:
                plan_xb(g + 1)
            else:
                plan_a(("va", "ga"), 0)
                plan_a(("va", "ga"), 1)
            for c in range(4):
                need(("yb", g, c), w_b_out, g * GT * P, GT, c * 2 * P, 2 * P)
        for j in range(DT + LAG):
            if 2 <= j < DT:
                plan_a(("va", "ga"), j)
            if j >= LAG:
                plan_a(("sb", "sa"), j - LAG)
        for j in range(DT):
            need(("ya", j), w_a_out, 0, DT, j * P, P)
        for j in range(DT):
            need(("wo", j), w_o, 0, DT, j * P, P)
        w_1, w_2 = A["w_1"][0], A["w_2"][0]
        FC = D_FF // D
        for f in range(FC):
            for j in range(DT):
                need(("w1", f, j), w_1, 0, DT, (f * DT + j) * P, P)
            for j in range(DT):
                need(("w2", f, j), w_2, f * D, DT, j * P, P)

        yb = [sb(f"yb{j}", "y", 4096 * j, [P, SEQ]) for j in range(DT)]
        o = 0
        xb_in = sb("xb_in", "g", o, [P, SEQ + 32]); o += 4 * (SEQ + 32)
        v = [sb(f"v{t}", "g", o + 4096 * t, [P, SEQ]) for t in range(GT)]; o += 4096 * GT
        G = [sb(f"gelu{t}", "g", o + 4096 * t, [P, SEQ]) for t in range(GT)]; o += 4096 * GT
        vg = pair("vg", "g", o, GT); o += 8192 * GT
        T1, T2, T3 = (sb(f"lru{i}", "g", o + 4096 * i, [P, SEQ]) for i in range(3)); o += 3 * 4096
        PAD_B = TAPS_B - 1

        PAIRS = [(0, 0), (1, 0), (0, 1), (1, 1), (2, 1), (1, 2), (2, 2)]
        gate_w = [sb(f"gate_w{n}", "g", o + 3584 * n, [P, len(PAIRS), P]) for n in range(2)]
        l_gate = [landing(f"gate{n}") for n in range(2)]
        gate_read = [[None], [None]]
        start_gates = [pool.op(lambda e, n=n: e.memset(gate_w[n][:], 0.0), x_in_read) for n in range(2)]

        def load_gates(g):
            got = []
            for n, w in enumerate((A["w_rg_a"][0], A["w_rg_x"][0])):
                for a, c in PAIRS:
                    for q in range(4):
                        r0, r1 = max(q * HEAD, a * P), min((q + 1) * HEAD, (a + 1) * P)
                        c0, c1 = max(q * HEAD, c * P), min((q + 1) * HEAD, (c + 1) * P)
                        if r0 < r1 and c0 < c1:
                            t = sp.dma(lambda e, n=n, a=a, c=c, w=w, q=q, r0=r0, r1=r1, c0=c0, c1=c1: e.dma_start(
                                gate_w[n][r0 - a * P:r1 - a * P, PAIRS.index((a, c)), c0 - c * P:c1 - c * P],
                                w[4 * g + q, r0 - q * HEAD:r1 - q * HEAD, c0 - q * HEAD:c1 - q * HEAD]),
                                l_gate[n], start_gates[n], gate_read[n])
                got.append(t)
            return got

        NR = D_RNN // P
        lam = par[:, offsets["lam"]:offsets["lam"] + NR]
        la, lb, lc, ld = (small[:, 16 * n:16 * n + NR] for n in range(4))
        t = dve.op(lambda e: e.tensor_scalar(la, lam, -1.0, None, ALU.mult), got_par)
        t = dve.op(lambda e: e.tensor_tensor(lb, la, lam, ALU.min), t)
        t = act.op(lambda e: e.activation(lc, lb, ACT.Exp), t)
        t = dve.op(lambda e: e.tensor_scalar(lb, lc, 2.0, None, ALU.add), t)
        t = dve.op(lambda e: e.reciprocal(lb, lb), t)
        t = dve.op(lambda e: e.tensor_tensor(lb, lb, lc, ALU.mult), t)
        t = dve.op(lambda e: e.tensor_tensor(lc, lb, lb, ALU.mult), t)
        t = dve.op(lambda e: e.memset(ld, 1.0 / 17), t)
        for m in (15, 13, 11, 9, 7, 5, 3, 1):
            t = dve.op(lambda e: e.tensor_tensor(ld, ld, lc, ALU.mult), t)
            t = dve.op(lambda e, m=m: e.tensor_scalar(ld, ld, 1.0 / m, None, ALU.add), t)
        t = dve.op(lambda e: e.tensor_tensor(ld, ld, lb, ALU.mult), t)
        t = dve.op(lambda e: e.tensor_scalar(la, la, 0.0, None, ALU.max), t)
        t = dve.op(lambda e: e.scalar_tensor_tensor(la, ld, 2.0, la, ALU.mult, ALU.add), t)
        t = dve.op(lambda e: e.tensor_scalar(sp4[:, 0:NR], la, LRU_C / 2, None, ALU.mult), t)
        got_sp4 = dve.op(lambda e: e.tensor_scalar(nsp4[:, 0:NR], la, -LRU_C / 2, None, ALU.mult), t)

        v_got, v_read = [None] * GT, [[x_in_read]] * GT
        xb_read = [dve.op(lambda e: e.memset(xb_in[:, 0:PAD_B], 0.0), x_in_read)]

        def xb_tile(g, t):
            if g == NG:
                return
            j = g * GT + t
            evac = []

            def take(c, half, b, done, j=j, evac=evac):
                evac.append(act.op(lambda e: e.activation(xb_in[:, PAD_B + half * HALF:PAD_B + (half + 1) * HALF], b[:],
                                                          ACT.Identity, bias=C("b_in", Z_XB // P + j)), done, xb_read[0], got_par))
                return evac[-1]

            outputs(("xb", g, t), DT, P, h, h_got, take)
            for m in range(TAPS_B):
                w, src = C("conv_b_w", m * NR + j), xb_in[:, m:m + SEQ]
                if m == 0:
                    d = dve.op(lambda e, w=w, src=src, t=t, j=j: e.tensor_scalar(v[t][:], src, w, C("conv_b_b", j),
                               ALU.mult, ALU.add), evac, v_read[t])
                else:
                    d = dve.op(lambda e, w=w, src=src, t=t: e.scalar_tensor_tensor(v[t][:], src, w, v[t][:], ALU.mult,
                               ALU.add), d)
            xb_read[0], v_got[t] = d, d

        G_got, G_read, T1_read = [None] * GT, [[x_in_read]] * GT, [x_in_read]

        def gb_tiles(g):
            for t in range(GT):
                j = g * GT + t
                evac = []

                def take(c, half, b, done, j=j, t=t, evac=evac):
                    evac.append(act.op(lambda e: e.activation(G[t][:, cut(half)], b[:], ACT.Identity,
                                                              bias=C("b_in", Z_GB // P + j)), done, G_read[t], got_par))
                    return evac[-1]

                outputs(("gb", g, t), DT, P, h, h_got, take)
                s = act.op(lambda e, t=t: e.activation(T1[:], G[t][:], ACT.Square), evac, T1_read[0])
                s = dve.op(lambda e: e.tensor_scalar(T1[:], T1[:], 0.044715, 1.0, ALU.mult, ALU.add), s)
                s = dve.op(lambda e, t=t: e.tensor_tensor(T1[:], T1[:], G[t][:], ALU.mult), s)
                s = act.op(lambda e: e.activation(T1[:], T1[:], ACT.Tanh, scale=0.7978845608028654), s)
                s = dve.op(lambda e, t=t: e.scalar_tensor_tensor(G[t][:], T1[:], 1.0, G[t][:], ALU.add, ALU.mult), s)
                G_got[t], T1_read[0] = s, s

        vg_got, vg_read = [[None, None] for _ in range(GT)], [x_in_read]
        v_scaled = [None] * GT
        T2_read, T3_read = [x_in_read], [x_in_read]

        def gate_tile(g, c, got_w):
            j = g * GT + c
            out_banks = {}
            for n in range(2):
                rows = [a for a, cc in PAIRS if cc == c]
                for half in range(2):
                    i, b, was = bank()
                    for m, a in enumerate(rows):
                        done = pe.op(lambda e, n=n, a=a, c=c, m=m, half=half, b=b, rows=rows: e.matmul(
                            b[:], gate_w[n][:, PAIRS.index((a, c)), :], v[a][:, cut(half)], start=m == 0,
                            stop=m == len(rows) - 1), was, got_w[n], v_got[a], inc=m == len(rows) - 1)
                    out_banks[n, half] = (i, b, done)
                    gate_read[n] = done
            tr, ti = [], []
            for half in range(2):
                i, b, done = out_banks[0, half]
                tr.append(act.op(lambda e, half=half, b=b, j=j: e.activation(T1[:, cut(half)], b[:], ACT.Tanh,
                          bias=CH("b_rg_a", j), scale=0.5), done, T1_read[0], got_parh))
            for half in range(2):
                i, b, done = out_banks[1, half]
                ti.append(act.op(lambda e, half=half, b=b, j=j: e.activation(T3[:, cut(half)], b[:], ACT.Tanh,
                          bias=CH("b_rg_x", j), scale=0.5), done, T3_read[0], got_parh))
                free[i] = [ti[-1]]
            a_got = act.op(lambda e, j=j: e.activation(T2[:], T1[:], ACT.Exp, scale=nsp4[:, j:j + 1], bias=nsp4[:, j:j + 1]),
                           tr, T2_read[0], got_sp4)
            th = act.op(lambda e, j=j: e.activation(T1[:], T1[:], ACT.Tanh, scale=sp4[:, j:j + 1], bias=sp4[:, j:j + 1]), a_got)
            mm = []
            for half in range(2):
                i, b, done = out_banks[0, half]
                q = dve.op(lambda e, half=half, b=b: e.tensor_tensor(b[:], T2[:, cut(half)], T2[:, cut(half)], ALU.mult),
                           a_got, tr)
                q = dve.op(lambda e, half=half, b=b: e.scalar_tensor_tensor(T1[:, cut(half)], b[:], 1.0, T1[:, cut(half)],
                           ALU.add, ALU.mult), q, th)
                free[i] = [q]
                mm.append(q)
            s = act.op(lambda e: e.activation(T1[:], T1[:], ACT.Sqrt), mm)
            s = dve.op(lambda e: e.memset(T1[:, 0:1], 1.0), s)
            q = dve.op(lambda e, c=c: e.scalar_tensor_tensor(T3[:], T3[:], 1.0, v[c][:], ALU.add, ALU.mult), ti)
            v_scaled[c] = q
            q = dve.op(lambda e: e.scalar_tensor_tensor(T3[:], T1[:], 0.5, T3[:], ALU.mult, ALU.mult), s, q)
            q = dve.op(lambda e: e.tensor_tensor_scan(T1[:], T2[:], T3[:], 0.0, ALU.mult, ALU.add), q)
            T2_read[0] = T3_read[0] = q
            q = dve.op(lambda e, c=c: e.scalar_tensor_tensor(T1[:], T1[:], 0.5, G[c][:], ALU.mult, ALU.mult), q, G_got[c])
            G_read[c] = q
            s = split_value(vg[0][c][:], vg[1][c][:], T1[:], [q], [vg_read[0]])
            vg_got[c] = [s, s]
            T1_read[0] = s

        yb_got = [[None, None] for _ in range(DT)]

        def yb_tiles(g):
            for c4 in range(4):
                def take(c, half, b, done, c4=c4):
                    j = c4 * 2 + c
                    dst = yb[j][:, cut(half)]
                    if g == 0:
                        yb_got[j][half] = dve.op(lambda e: e.tensor_copy(dst, b[:]), done)
                    else:
                        yb_got[j][half] = dve.op(lambda e: e.tensor_tensor(dst, dst, b[:], ALU.add), done, yb_got[j][half])
                    taps(2)
                    return yb_got[j][half]
                vg_read[0] = outputs(("yb", g, c4), GT, 2 * P, vg, vg_got, take)

        stage_b = []
        over_u, over_uc = [None, None], [stage_b] * DT
        EDGE = [0, 4224 + 16 * 4096]
        uc = [sb(f"uc{j}", "g", 4224 + 4096 * j, [P, SEQ]) for j in range(DT)]
        sa = [sb(f"sa{j}", "g", 4224 + 4096 * (DT + j), [P, SEQ]) for j in range(DT)]
        PAD_A = TAPS_A - 1
        u_in = [sb(f"u_in{n}", "g", EDGE[n], [P, PAD_A + SEQ + 2]) for n in range(2)]
        u_read = [None, None]
        uc_got = [None] * DT

        def conv_a(j, got):
            src = u_in[j % 2]
            d = got
            for m in range(TAPS_A):
                w, s = C("conv_a_w", m * DT + j), src[:, m:m + SEQ]
                if m == 0:
                    d = dve.op(lambda e, w=w, s=s: e.tensor_scalar(uc[j][:], s, w, C("conv_a_b", j), ALU.mult, ALU.add), d)
                else:
                    d = dve.op(lambda e, w=w, s=s: e.scalar_tensor_tensor(uc[j][:], s, w, uc[j][:], ALU.mult, ALU.add), d)
                yield
            uc_got[j] = d
            u_read[j % 2] = [d]

        todo = []

        def taps(n):
            while n and todo:
                try:
                    next(todo[0])
                    n -= 1
                except StopIteration:
                    todo.pop(0)

        m_got = [[None, None] for _ in range(DT)]
        sa_got = [[None, None] for _ in range(DT)]

        def conv_input(j):
            n, u_half, u_got = j % 2, [], []

            def take(c, half, b, done):
                u_half.append(act.op(lambda e: e.activation(u_in[n][:, PAD_A + half * HALF:PAD_A + (half + 1) * HALF], b[:], ACT.Identity,
                                     bias=CH("b_in", Z_VA // P + j), scale=0.5), done, u_read[n], got_parh))
                return u_half[-1]
            outputs(("va", j), DT, P, h, h_got, take)

            def take(c, half, b, done):
                t = act.op(lambda e: e.activation(uc[j][:, cut(half)], b[:], ACT.Tanh, bias=CH("b_in", Z_GA // P + j), scale=0.5),
                           done, over_uc[j], got_parh)
                at = u_in[n][:, PAD_A + half * HALF:PAD_A + (half + 1) * HALF]
                u_got.append(dve.op(lambda e: e.scalar_tensor_tensor(at, uc[j][:, cut(half)], 1.0, at, ALU.add, ALU.mult), t,
                                    u_half[half]))
                return t
            outputs(("ga", j), DT, P, h, h_got, take)
            return u_got

        def mix_gates(j):
            def take(c, half, b, done):
                t = act.op(lambda e: e.activation(sa[j][:, cut(half)], b[:], ACT.Tanh, bias=CH("b_in", Z_SB // P + j), scale=0.5),
                           done, stage_b)
                m_got[j][half] = dve.op(lambda e: e.scalar_tensor_tensor(yb[j][:, cut(half)], sa[j][:, cut(half)], 1.0,
                                        yb[j][:, cut(half)], ALU.add, ALU.mult), t, yb_got[j][half])
                return t
            outputs(("sb", j), DT, P, h, h_got, take)
            taps(8)

            def take(c, half, b, done):
                sa_got[j][half] = act.op(lambda e: e.activation(sa[j][:, cut(half)], b[:], ACT.Tanh, bias=CH("b_in", Z_SA // P + j),
                                         scale=0.5), done, m_got[j][half])
                return sa_got[j][half]
            last = outputs(("sa", j), DT, P, h, h_got, take)
            taps(8)
            return last

        for t in range(GT):
            xb_tile(0, t)
        for g in range(NG):
            got_w = load_gates(g)
            gb_tiles(g)
            gate_tile(g, 0, got_w)
            gate_tile(g, 1, got_w)
            v_read[0] = [v_scaled[0], gate_read]
            xb_tile(g + 1, 0)
            gate_tile(g, 2, got_w)
            v_read[1:] = [v_scaled[1], gate_read], [v_scaled[2], gate_read]
            xb_tile(g + 1, 1)
            xb_tile(g + 1, 2)
            if g == NG - 1:
                for j in range(2):
                    over_u[j] = [xb_read[0]] if j == 0 else [gate_read]
                    u_read[j] = [dve.op(lambda e, j=j: e.memset(u_in[j][:, 0:PAD_A], 0.0), over_u[j])]
                    over_uc[j] = [v_read[j]]
                    todo.append(conv_a(j, conv_input(j)))
            yb_tiles(g)

        stage_b.extend([(dve.sem, dve.count), (act.sem, act.count), (pe.sem, pe.count)])
        for j in range(1, DT + LAG):
            if 2 <= j < DT:
                while uc_got[j - 2] is None:
                    taps(1)
                todo.append(conv_a(j, conv_input(j)))
                taps(8)
            if j >= LAG:
                h_last = mix_gates(j - LAG)
        while todo:
            taps(1)

        def column_sums(tiles, got, rhs, width, col0=0):
            done = None
            for j in range(len(tiles)):
                for t in range(NT):
                    done = pe.op(lambda e, j=j, t=t: e.matmul(stat_bank[:, width * t:width * (t + 1)],
                                 tiles[j][:, t * P:(t + 1) * P], rhs(j), start=j == 0 and t == 0, stop=j == len(tiles) - 1,
                                 skip_group_check=True), got[j], stat_free[0] if j == 0 else [], inc=t == NT - 1)
            return done

        def spread(column, waits, half):
            i, b, was = bank()
            for q in range(4):
                t = half * 4 + q
                done = pe.op(lambda e, t=t, q=q: e.matmul(b[:, q * P:(q + 1) * P], stat[:, column + t:column + t + 1].broadcast_to([P, P]),
                             ident[:], start=True, stop=True), waits, was, inc=q == 3)
            return i, b, done

        done = column_sums(uc, uc_got, lambda j: ones[:, 0:1], 1)
        t = dve.op(lambda e: e.tensor_scalar(stat[:, 0:NT], stat_bank[:, 0:NT], 1.0 / D, None, ALU.mult), done)
        stat_free[0] = [t]
        centred = [[None, None] for _ in range(DT)]
        sq = [sb(f"sq{n}", "g", EDGE[n], [P, SEQ]) for n in range(2)]
        for half in range(2):
            i, b, done = spread(0, t, half)
            for j in range(DT):
                centred[j][half] = dve.op(lambda e, j=j, b=b, half=half: e.tensor_tensor(uc[j][:, cut(half)], uc[j][:, cut(half)], b[:],
                                          ALU.subtract), done)
            free[i] = [centred[DT - 1][half]]
        sums = None
        sq_read = [u_read[0], u_read[1]]
        for j in range(DT):
            s = act.op(lambda e, j=j: e.activation(sq[j % 2][:], uc[j][:], ACT.Square), centred[j], sq_read[j % 2], uc_got)
            for t in range(NT):
                done = pe.op(lambda e, j=j, t=t: e.matmul(stat_bank[:, t:t + 1], sq[j % 2][:, t * P:(t + 1) * P], ones[:, 0:1],
                             start=j == 0 and t == 0, stop=j == DT - 1, skip_group_check=True), s, stat_free[0] if j == 0 else [],
                             inc=t == NT - 1)
            sq_read[j % 2] = done
        t = dve.op(lambda e: e.tensor_copy(stat[:, 8:16], stat_bank[:, 0:NT]), done)
        stat_free[0] = [t]
        r = rstd_of(slice(8, 16), 1.0 / D, t)
        un = pair("un", "h", 0, DT)
        un_got = [[None, None] for _ in range(DT)]
        lnt = [sb(f"lnt{n}", "g", EDGE[n // 2] + 2048 * (n % 2), [P, HALF]) for n in range(4)]
        lnt_read = [sq_read] * 4
        for half in range(2):
            i, b, done = spread(8, r, half)
            z_got, s_got = [None] * DT, [None] * DT
            for j in range(DT):
                z_got[j] = dve.op(lambda e, j=j, b=b, half=half: e.scalar_tensor_tensor(uc[j][:, cut(half)], uc[j][:, cut(half)],
                                  C("ln_g", j), b[:], ALU.mult, ALU.mult), done, sq_read)
            free[i] = [z_got[-1]]
            for j in range(DT + 1):
                if j < DT:
                    n = j % 4
                    t = act.op(lambda e, j=j, n=n, half=half: e.activation(lnt[n][:], uc[j][:, cut(half)], ACT.Tanh, bias=CH("ln_b", j),
                               scale=0.5), z_got[j], lnt_read[n])
                    z = act.op(lambda e, j=j, half=half: e.activation(uc[j][:, cut(half)], uc[j][:, cut(half)], ACT.Identity,
                               bias=CH("ln_b", j), scale=0.5), t)
                    s_got[j] = dve.op(lambda e, j=j, n=n, half=half: e.scalar_tensor_tensor(uc[j][:, cut(half)], lnt[n][:], 1.0,
                                      uc[j][:, cut(half)], ALU.add, ALU.mult), z)
                    lnt_read[n] = [s_got[j]]
                if j:
                    un_got[j - 1][half] = split_value(un[0][j - 1][:, cut(half)], un[1][j - 1][:, cut(half)], uc[j - 1][:, cut(half)],
                                                      [s_got[j - 1]], [h_last])

        mx = pair("mx", "g", 0, DT)
        mx_got = [[None, None] for _ in range(DT)]
        uc_done = [un_got[j][half] for j in range(DT) for half in range(2)]
        gated = []
        for j in range(DT):
            def take(c, half, b, done, j=j):
                s = dve.op(lambda e: e.scalar_tensor_tensor(sa[j][:, cut(half)], sa[j][:, cut(half)], 1.0, b[:], ALU.add, ALU.mult), done,
                           sa_got[j][half])
                s = dve.op(lambda e: e.tensor_tensor(yb[j][:, cut(half)], yb[j][:, cut(half)], sa[j][:, cut(half)], ALU.add), s,
                           m_got[j][half])
                gated.append(s)
                return s
            un_last = outputs(("ya", j), DT, P, un, un_got, take)
            s = act.op(lambda e, j=j: e.activation(mx[0][j][:], yb[j][:], ACT.Copy, scale=0.5), gated[-2:], uc_done)
            s = [s, dve.op(lambda e, j=j: e.scalar_tensor_tensor(mx[1][j][:], yb[j][:], 0.5, mx[0][j][:].bitcast(F32), ALU.mult,
                                                                 ALU.subtract), s)]
            mx_got[j] = [s, s]

        x1 = [sb(f"x1_{j}", "y", 4096 * j, [P, SEQ]) for j in range(DT)]
        x1_got = [[None, None] for _ in range(DT)]
        xcols = [sb(f"xcols{n}", "g", 64 * KB + 2048 * n, [P, NT // 2, P]) for n in range(2)]
        l_xc = [landing(f"xc{n}") for n in range(2)]
        xc_read = [gated, gated]
        squares = [sb(f"squares{n}", "g", 68 * KB + 2048 * n, [P, HALF]) for n in range(2)]
        squares_read = [gated, gated]

        def half_squares(j, half, rhs, width, buffer, over, got):
            s = act.op(lambda e: e.activation(buffer[:], x1[j][:, cut(half)], ACT.Square), got, over)
            for q in range(NT // 2):
                t = half * NT // 2 + q
                done = pe.op(lambda e, t=t, q=q: e.matmul(stat_bank[:, width * t:width * (t + 1)], buffer[:, q * P:(q + 1) * P], rhs,
                             start=j == 0 and t == 0, stop=j == DT - 1, skip_group_check=True), s,
                             stat_free[0] if j == 0 else [], inc=q == NT // 2 - 1)
            return done

        h2 = pair("h2", "h", 0, DT)
        h2_got = [[None, None] for _ in range(DT)]
        for j in range(DT):
            (hi, lo, wgot), slot = weights(("wo", j))
            for half in range(2):
                n = half
                got = sp.dma(lambda e, n=n, j=j, half=half: e.dma_start(xcols[n][:], x_rows[:, half * 4:half * 4 + 4, j * P:(j + 1) * P]),
                             l_xc[n], xc_read[n], uc_done)
                i, b, was = bank()
                terms = [(hi[:, k, :], lo[:, k, :], mx[0][k][:, cut(half)], mx[1][k][:, cut(half)], mx_got[k][half])
                         for k in range(DT)]
                split_free[slot] = product(b[:], terms, [was, wgot], stop=False)
                for q in range(4):
                    done = pe.op(lambda e, q=q, b=b, n=n: e.matmul(b[:, q * P:(q + 1) * P], xcols[n][:, q, :],
                                 ident[:], start=False, stop=q == 3, skip_group_check=True), got, inc=q == 3)
                xc_read[n] = done
                x1_got[j][half] = act.op(lambda e, b=b, j=j, half=half: e.activation(x1[j][:, cut(half)], b[:], ACT.Copy), done, mx_got[j])
                free[i] = [x1_got[j][half]]
                h2_got[j][half] = evacuate_split(h2[0][j][:, cut(half)], h2[1][j][:, cut(half)], x1[j][:, cut(half)], C("g_mlp", j),
                                                 [x1_got[j][half], un_last])
            if j:
                for half in range(2):
                    squares_read[half] = half_squares(j - 1, half, ones[:, 0:1], 1, squares[half], squares_read[half], x1_got[j - 1][half])
        mx_last = done
        factor = sb("factor", "g", 64 * KB, [P, SEQ])
        tmp = [sb(f"tmp{n}", "g", 68 * KB + 2048 * n, [P, HALF]) for n in range(2)]
        tmp_read, turns, factor_got = [None, None], [0], [None, None]

        def temporary():
            n = turns[0] % len(tmp)
            turns[0] += 1
            return n, tmp[n], tmp_read[n]

        def find_factor():
            for half in range(2):
                squares_read[half] = half_squares(DT - 1, half, ones[:, 0:1], 1, squares[half], squares_read[half], x1_got[DT - 1][half])
            tmp_read[:] = squares_read
            t = dve.op(lambda e: e.tensor_copy(stat[:, 0:8], stat_bank[:, 0:NT]), squares_read)
            stat_free[0] = [t]
            r = rstd_of(slice(0, 8), 1.0 / D, t)
            for half in range(2):
                i, b, done = spread(0, r, half)
                factor_got[half] = act.op(lambda e, b=b, half=half: e.activation(factor[:, cut(half)], b[:], ACT.Copy), done, xc_read)
                free[i] = [factor_got[half]]

        def scaled(hl, got, source, source_got, column, gain, r, over):
            held = [spread(column, r, half) for half in range(2)]
            for half, (i, b, done) in enumerate(held):
                for j in range(DT):
                    if j % 4 == 0:
                        yield
                    n, tt, was = temporary()
                    z = dve.op(lambda e, j=j, tt=tt, b=b, half=half: e.scalar_tensor_tensor(tt[:], source[j][:, cut(half)], gain(j), b[:],
                               ALU.mult, ALU.mult), done, was, source_got[j][half])
                    got[j][half] = split_value(hl[0][j][:, cut(half)], hl[1][j][:, cut(half)], tt[:], [z], over)
                    tmp_read[n] = got[j][half]
                free[i] = [z]

        ff = pair("ff", "g", 0, DT)
        ff_got = [[None, None] for _ in range(DT)]
        ff_read = [mx_last]
        GG, GF2 = small[:, 64:72], gcol[:, :].rearrange("p (j n) -> p j n", n=2)
        g_final, norm_g = (par[:, offsets[n]:offsets[n] + DT] for n in ("g_final", "norm_g_2"))
        t = dve.op(lambda e: e.memset(gcol[:], 1.0))
        gf_got = dve.op(lambda e: e.tensor_tensor(GF2[:, :, 1], g_final, g_final, ALU.mult), t)
        gg_got = dve.op(lambda e: e.tensor_tensor(GG, g_final, norm_g, ALU.mult), got_par)
        NM = N_MEM // P
        mem_in = sb("mem_in", "h", 0, [P, NM, D])
        mem_sq = sb("mem_sq", "h", 8 * KB, [P, D])
        mn = pair("mn", "g", 8 * KB, DT, N_MEM)
        km = sb("km", "g", 0, [P, NH, N_MEM])
        vm = sb("vm", "g", 4 * KB, [P, NM, GROUP])
        l_mem = landing("mem")
        sqm = [sb(f"sqm{n}", "h", 32 * KB + 4096 * n, [P, SEQ]) for n in range(2)]
        sqm_read = [None, None]
        w_in2, w_kv, w_out2 = A["w_in_2"][0], A["w_mem_kv_2"][0], A["w_out_2"][0]
        for c in range(2 * GROUP // P):
            need(("kv", c), w_kv, 0, DT, c * P, P)
        gate_cols = lambda c: w_in2[:, c:c + NH].rearrange("(k p) c -> p k c", p=P)
        plan.append((("gates",), [((0, NH), gate_cols(Y_G)), ((32, 32 + NH), gate_cols(Y_G + NH))], DT, P, True))
        for g in range(NH):
            need(("u", g), w_in2, 0, DT, Y_U + g * P, P)
            need(("zb", g), w_in2, 0, DT, Y_ZB + g * P, P)
            need(("pw", g), A["pool_w_2"][0, g], 0, 1, 0, P)
        for c in range(4):
            need(("ob", c), w_out2, GROUP, NH, c * 2 * P, 2 * P)
        for g in range(NH):
            need(("qc", g), w_in2, 0, DT, Y_QC + g * P, P)
            need(("zc", g), w_in2, 0, DT, Y_ZC + g * P, P)
        for c in range(4):
            need(("oc", c), w_out2, 2 * GROUP, NH, c * 2 * P, 2 * P)
        for j in range(2 * NH):
            need(("qk", j), w_in2, 0, DT, Y_QK + j * P, P)
        for g in range(NH):
            need(("v", g), w_in2, 0, DT, Y_V + g * P, P)
        for g in range(NH):
            need(("o", g), w_in2, 0, DT, Y_O + g * P, P)
        for g in range(NH):
            need(("za", g), w_in2, 0, DT, Y_ZA + g * P, P)
        for c in range(3):
            need(("oa", c), w_out2, 0, NH, c * 2 * P, 2 * P)

        def stat_tile(j, n_last, rhs, width, buffer, over, got):
            s = act.op(lambda e: e.activation(buffer[:], x1[j][:], ACT.Square), got, over)
            for t in range(NT):
                done = pe.op(lambda e, t=t: e.matmul(stat_bank[:, width * t:width * (t + 1)], buffer[:, t * P:(t + 1) * P], rhs,
                             start=j == 0 and t == 0, stop=j == n_last, skip_group_check=True), s,
                             stat_free[0] if j == 0 else [], gf_got, inc=t == NT - 1)
            return done

        def inner(j, half, b, done):
            n, tt, was = temporary()
            z = dve.op(lambda e: e.scalar_tensor_tensor(tt[:], b[:], 0.0, factor[:, cut(half)], ALU.max, ALU.mult), done, was,
                       factor_got[half])
            z2 = act.op(lambda e: e.activation(tt[:], tt[:], ACT.Square), z)
            ff_got[j][half] = split_value(ff[0][j][:, cut(half)], ff[1][j][:, cut(half)], tt[:], [z2], [ff_read[0]])
            tmp_read[n] = ff_got[j][half]
            return z

        for f in range(FC):
            for j in range(DT):
                if (f, j) == (0, 0):
                    first, held = turn[0], []
                    outputs(("w1", f, j), DT, P, h2, h2_got, lambda c, half, b, done: held.append((half, b, done)))
                    find_factor()
                    for half, b, done in held:
                        free[(first + half) % NB] = [inner(j, half, b, done)]
                else:
                    h2_last = outputs(("w1", f, j), DT, P, h2, h2_got, lambda c, half, b, done, j=j: inner(j, half, b, done))
            if f == FC - 1:
                mem_got = sp.dma(lambda e: e.dma_start(mem_in[:], A["mem_2"][0].rearrange("(t p) d -> p t d", p=P)), l_mem, h2_last)
            for j in range(DT):
                def take(c, half, b, done, j=j):
                    x1_got[j][half] = dve.op(lambda e: e.tensor_tensor(x1[j][:, cut(half)], x1[j][:, cut(half)], b[:], ALU.add), done,
                                             x1_got[j][half])
                    return x1_got[j][half]
                last = outputs(("w2", f, j), DT, P, ff, ff_got, take)
                if f == FC - 1 and j:
                    sqm_read[(j - 1) % 2] = stat_tile(j - 1, DT - 1, GF2[:, j - 1, :], 2, sqm[(j - 1) % 2], [sqm_read[(j - 1) % 2], h2_last],
                                                      x1_got[j - 1])
                if f == FC - 1 and j in (1, 2):
                    t = j - 1
                    s = act.op(lambda e, t=t: e.activation(mem_sq[:], mem_in[:, t, :], ACT.Square, accum_out=stat[:, 16 + t:17 + t]),
                               mem_got, (act.sem, act.count), h2_last)
                    r = rstd_of(slice(16 + t, 17 + t), 1.0 / D, s)
                    mem_normed = dve.op(lambda e, t=t: e.tensor_scalar(mem_in[:, t, :], mem_in[:, t, :], stat[:, 16 + t:17 + t], None,
                                                                       ALU.mult), r)
            ff_read[0] = last
        ff_last = last

        if stop == "first":
            l_out = landing("out")
            for j in range(DT):
                fin = sp.dma(lambda e, j=j: e.dma_start(out[j], x1[j][:]), l_out, x1_got[j])
            sp.wait(fin)
            finish(nc, ctx, pe, act, dve, pool, sp)
            return

        tmp[:] = [sb(f"tmp_2_{n}", "g", 64 * KB + 2048 * n, [P, HALF]) for n in range(4)]
        tmp_read[:] = [[ff_last, ff_got]] * 4
        mn_got = [[None, None] for _ in range(DT)]
        for j in range(0, DT, 2):
            i, b, was = bank()
            for q in range(4):
                turned = done = pe.op(lambda e, q=q, j=j, b=b: e.transpose(b[:, q * P:(q + 1) * P], mem_in[:, q % 2, (j + q // 2) * P:(j + q // 2 + 1) * P],
                             ident[:]), mem_normed, was, inc=q == 3)
            for q in range(2):
                was = evacuate_split(mn[0][j + q][:], mn[1][j + q][:], b[:, q * N_MEM:(q + 1) * N_MEM], C("mem_norm_g_2", j + q),
                                     [done, was if q else None, ff_last])
                mn_got[j + q] = [was, was]
            free[i] = [mn_got[j], mn_got[j + 1]]
        done = stat_tile(DT - 1, DT - 1, GF2[:, DT - 1, :], 2, sqm[(DT - 1) % 2], [sqm_read[(DT - 1) % 2]], x1_got[DT - 1])
        sums = stat_bank[:, 0:2 * NT].rearrange("p (t n) -> p t n", n=2)
        mem_last = [done, turned]
        t = dve.op(lambda e: e.tensor_copy(stat[:, 0:NT], sums[:, :, 0]), done)
        t2 = dve.op(lambda e: e.tensor_copy(stat[:, 8:16], sums[:, :, 1]), done)
        stat_free[0] = [t, t2]
        r1 = rstd_of(slice(0, 8), 1.0 / D, t)
        t = dve.op(lambda e: e.tensor_tensor(small[:, 72:80], stat[:, 0:8], stat[:, 0:8], ALU.mult), r1)
        t = dve.op(lambda e: e.tensor_tensor(stat[:, 8:16], stat[:, 8:16], small[:, 72:80], ALU.mult), t)
        r2 = rstd_of(slice(8, 16), 1.0 / D, t)
        r12 = dve.op(lambda e: e.tensor_tensor(stat[:, 8:16], stat[:, 8:16], stat[:, 0:8], ALU.mult), r2)

        h3 = pair("h3", "h", 0, DT)
        h3_got = [[None, None] for _ in range(DT)]

        km_got = [None] * NH
        vm_got = []
        for c in range(2 * NH):
            if c >= NH:
                if c == NH:
                    scaling = scaled(h3, h3_got, x1, x1_got, 8, lambda j: GG[:, j:j + 1], [r12, gg_got], mem_last)
                    next(scaling)
                next(scaling, None)
            (hi, lo, wgot), slot = weights(("kv", c))
            i, b, was = bank()
            if c < NH:
                terms = [(hi[:, k, :], lo[:, k, :], mn[0][k][:], mn[1][k][:], mn_got[k]) for k in range(DT)]
                split_free[slot] = done = product(b[:, 0:N_MEM], terms, [was, wgot])
                km_got[c] = act.op(lambda e, c=c, b=b: e.activation(km[:, c, :], b[:, 0:N_MEM], ACT.Copy), done, ff_last)
                free[i] = [km_got[c]]
            else:
                for q in range(NM):
                    terms = [(mn[0][k][:, q * P:(q + 1) * P], mn[1][k][:, q * P:(q + 1) * P], hi[:, k, :], lo[:, k, :], mn_got[k])
                             for k in range(DT)]
                    split_free[slot] = done = product(b[:, q * P:(q + 1) * P], terms, [was, wgot])
                t = act.op(lambda e, c=c, b=b: e.activation(vm[:, :, (c - NH) * P:(c - NH + 1) * P],
                           b[:, 0:NM * P].rearrange("p (q d) -> p q d", q=NM), ACT.Copy), done, ff_last)
                vm_got.append(t)
                free[i] = [t]

        kv_last = done
        y1, y1_got = x1, [[None, None] for _ in range(DT)]
        for half in range(2):
            i, b, done = spread(0, r1, half)
            for j in range(DT):
                y1_got[j][half] = dve.op(lambda e, j=j, b=b, half=half: e.scalar_tensor_tensor(y1[j][:, cut(half)], x1[j][:, cut(half)],
                                         C("g_final", j), b[:], ALU.mult, ALU.mult), done, h3_got[j][half])
            free[i] = [y1_got[DT - 1][half]]

        row = [sb(f"row{n}", "g", (8 + 17 + 8) * KB + 4096 * n, [P, SEQ]) for n in range(5)]
        bias = small[:, 80:82]
        l_bias = landing("bias")
        bias_got = sp.dma(lambda e: e.dma_start(bias[0:NH, 0:1], A["b_gates_2"][:, 0:NH].rearrange("l n -> n l")), l_bias)
        bias_got = sp.dma(lambda e: e.dma_start(bias[32:32 + NH, 0:1], A["b_gates_2"][:, NH:2 * NH].rearrange("l n -> n l")), l_bias)
        gate_evac = []

        def take(c, half, b, done):
            a = act.op(lambda e: e.activation(row[0][0:NH, cut(half)], b[0:NH, :], ACT.Identity, bias=bias[0:NH, 0:1]), done, bias_got,
                       ff_last)
            f = act.op(lambda e: e.activation(row[1][32:32 + NH, cut(half)], b[32:32 + NH, :], ACT.Identity, bias=bias[32:32 + NH, 0:1]),
                       done, bias_got)
            gate_evac.extend([a, f])
            return [a, f]
        outputs(("gates",), DT, P, h3, h3_got, take)
        R = lambda n: row[n][0:NH, :]
        chunks = lambda n: row[n][0:NH, :].rearrange("p (c t) -> p c t", t=P)
        t = act.op(lambda e: e.activation(R(2), row[1][32:32 + NH, :], ACT.Copy), gate_evac)
        f_got = t
        t = dve.op(lambda e: e.scalar_tensor_tensor(R(3), R(2), -1.0, R(2), ALU.mult, ALU.min), t)
        t = act.op(lambda e: e.activation(R(3), R(3), ACT.Exp), t)
        t = act.op(lambda e: e.activation(R(3), R(3), ACT.Ln, bias=1.0), t)
        t = dve.op(lambda e: e.scalar_tensor_tensor(R(2), R(2), 0.0, R(3), ALU.min, ALU.subtract), t)
        u = dve.op(lambda e: e.memset(R(4), 1.0), ff_last)
        u = dve.op(lambda e: e.memset(chunks(4)[:, :, 0:1], 0.0), u)
        t = dve.op(lambda e: e.tensor_tensor_scan(R(3), R(4), R(2), 0.0, ALU.mult, ALU.add), t, u)
        x_got = dve.op(lambda e: e.tensor_tensor(R(0), R(0), R(3), ALU.subtract), t, gate_evac)
        u = dve.op(lambda e: e.memset(R(4), BIG), t)
        u = dve.op(lambda e: e.memset(chunks(4)[:, :, 0:1], -BIG), u)
        t = dve.op(lambda e: e.tensor_tensor_scan(R(2), R(4), R(0), -BIG, ALU.min, ALU.max), x_got, u)
        mm4, mp4 = small[0:NH, 84:92], small[0:NH, 92:100]
        t = dve.op(lambda e: e.tensor_tensor_scan(mm4, chunks(2)[:, :, P - 1], chunks(3)[:, :, P - 1], 0.0, ALU.max, ALU.add), t)
        u = dve.op(lambda e: e.memset(mp4, 0.0))
        t = dve.op(lambda e: e.tensor_copy(mp4[:, 1:NT], mm4[:, 0:NT - 1]), t, u)
        m_row = dve.op(lambda e: e.tensor_tensor(chunks(1), chunks(2), mp4.unsqueeze(2).broadcast_to([NH, NT, P]), ALU.max), t, f_got)
        nb_row = dve.op(lambda e: e.scalar_tensor_tensor(R(4), R(3), -1.0, R(1), ALU.mult, ALU.subtract), m_row)
        rows_dram = nc.dram_tensor("rows_dram", (2, NH, SEQ), F32).ap()
        mp_dram = nc.dram_tensor("mp_dram", (NH, NT), F32).ap()
        sz_dram = nc.dram_tensor("sz_dram", (NH, P, SEQ), F32).ap()
        l_rowout, l_mb, l_nb, l_mp = landing("rowout"), landing("mb"), landing("nb"), landing("mp")
        rows_out = [sp.dma(lambda e: e.dma_start(rows_dram[0], R(1)), l_rowout, m_row),
                    sp.dma(lambda e: e.dma_start(rows_dram[1], R(4)), l_rowout, nb_row),
                    sp.dma(lambda e: e.dma_start(mp_dram, mp4), l_rowout, m_row)][-1]
        mp_got = sp.dma(lambda e: e.dma_start(mprev[:].rearrange("p (h c) -> p h c", h=NH), mp_dram.partition_broadcast(P)), l_mp, rows_out)

        def silu2(dst, b, done, over, scratch, scratch_read):
            t = act.op(lambda e: e.activation(scratch, b, ACT.Tanh, scale=0.5), done, scratch_read)
            return dve.op(lambda e: e.scalar_tensor_tensor(dst, scratch, 1.0, b, ALU.add, ALU.mult), t, over)

        def add_outputs(key, hl, got):
            for c4 in range(4):
                def take(c, half, b, done, c4=c4):
                    j = c4 * 2 + c
                    y1_got[j][half] = dve.op(lambda e: e.tensor_tensor(y1[j][:, cut(half)], y1[j][:, cut(half)], b[:], ALU.add), done,
                                             y1_got[j][half])
                    return y1_got[j][half]
                last = outputs((key, c4), NH, 2 * P, hl, got, take)
            return last

        PAD_U = 16
        uw = [sb(f"uw{n}", "g", 8 * KB + 4224 * n, [P, PAD_U + SEQ]) for n in range(3)]
        zb = sb("zb", "g", 8 * KB + 4224 * 3, [P, SEQ])
        yp = pair("yp", "g", 25 * KB, NH)
        l_rcnt = landing("rcnt")
        rcnt_got = sp.dma(lambda e: e.dma_start(rcnt[:], A["rcnt"]), l_rcnt)
        yp_got = [[None, None] for _ in range(NH)]
        uw_read = [dve.op(lambda e, n=n: e.memset(uw[n][:, 0:PAD_U], 0.0), kv_last) for n in range(3)]
        zb_read = [kv_last]
        for g, window in enumerate(WINDOWS):
            evac = []

            def take(c, half, b, done):
                evac.append(act.op(lambda e: e.activation(uw[0][:, PAD_U + half * HALF:PAD_U + (half + 1) * HALF], b[:], ACT.Copy), done,
                                   uw_read))
                return evac[-1]
            outputs(("u", g), DT, P, h3, h3_got, take)
            if g == 0:
                i, b, was = bank()
                for c in range(NT):
                    done = pe.op(lambda e, c=c, b=b: e.transpose(b[:, c * NH:(c + 1) * NH], row[0][0:NH, c * P:(c + 1) * P],
                                 ident[0:NH, 0:NH]), x_got, was, inc=c == NT - 1)
                xcol_got = dve.op(lambda e, b=b: e.tensor_copy(xcol[:], b[:, 0:NH * NT]), done)
                free[i] = [xcol_got]
                rows_read = [xcol_got, rows_out, nb_row]
            src, step, at = 0, 1, 1
            t = evac
            while step < window:
                dst = 1 if src != 1 else 2
                t = dve.op(lambda e, src=src, dst=dst, step=step, at=at: e.tensor_tensor(uw[dst][:, at:], uw[src][:, at:],
                           uw[src][:, at - step:PAD_U + SEQ - step], ALU.add), t, uw_read)
                src, step = dst, step * 2
                at += step
            t = dve.op(lambda e, src=src, g=g, w=window: e.tensor_tensor(uw[src][:, PAD_U:PAD_U + w], uw[src][:, PAD_U:PAD_U + w],
                       rcnt[:, 16 * g:16 * g + w], ALU.mult), t, rcnt_got)
            t = dve.op(lambda e, src=src, w=window: e.scalar_tensor_tensor(uw[src][:, PAD_U:], uw[src][:, PAD_U:], 1.0 / w,
                       uw[0][:, PAD_U:], ALU.mult, ALU.subtract), t)
            s = split_value(yp[0][g][:], yp[1][g][:], uw[src][:, PAD_U:], [t], [rows_read, ff_last])
            uw_read = s

            def take(c, half, b, done):
                n, tt, was = temporary()
                t = silu2(zb[:, cut(half)], b[:], done, zb_read, tt[:], was)
                tmp_read[n] = t
                zb_got.append(t)
                return t
            zb_got = []
            outputs(("zb", g), DT, P, h3, h3_got, take)
            (hi, lo, wgot), slot = weights(("pw", g))
            held = []
            for half in range(2):
                i, b, was = bank()
                done = product(b[:], [(hi[:, 0, :], lo[:, 0, :], yp[0][g][:, cut(half)], yp[1][g][:, cut(half)], s)], [was, wgot])
                held.append((i, b, done))
            split_free[slot] = done
            zb_read = []
            for half, (i, b, done) in enumerate(held):
                n, tt, was = temporary()
                t = dve.op(lambda e, g=g, tt=tt, b=b, half=half: e.scalar_tensor_tensor(tt[:], b[:], CH("pool_scale_2", g), zb[:, cut(half)],
                           ALU.mult, ALU.mult), done, was, zb_got)
                free[i] = [t]
                zb_read.append(t)
                yp_got[g][half] = split_value(yp[0][g][:, cut(half)], yp[1][g][:, cut(half)], tt[:], [t], [done])
                tmp_read[n] = yp_got[g][half]
        yp_last = add_outputs("ob", yp, yp_got)

        qc = sb("qc", "g", 8 * KB, [P, SEQ])
        zc = sb("zc", "g", 12 * KB, [P, SEQ])
        pr = [sb(f"pr{n}", "g", 16 * KB + 2048 * n, [P, 2, N_MEM]) for n in range(NT // 2)]
        pt = sb("pt", "g", 24 * KB, [P, NM, SEQ])
        yc = pair("yc", "g", 32 * KB, NH)
        yc_got = [[None, None] for _ in range(NH)]
        SCALE = float(HD) ** -0.5
        qc_read = zc_read = pt_read = [uw_read, zb_read]
        pr_read, pr_got = [[uw_read, zb_read]] * (NT // 2), [None] * (NT // 2)
        for g in range(NH):
            q_got = []

            def take(c, half, b, done):
                q_got.append(act.op(lambda e: e.activation(qc[:, cut(half)], b[:], ACT.Copy), done, qc_read))
                return q_got[-1]
            outputs(("qc", g), DT, P, h3, h3_got, take)
            for tp in range(NT // 2):
                i, b, was = bank()
                for q in range(2):
                    done = pe.op(lambda e, q=q, tp=tp, g=g, b=b: e.matmul(b[:, q * N_MEM:(q + 1) * N_MEM], qc[:, (2 * tp + q) * P:(2 * tp + q + 1) * P],
                                 km[:, g, :], start=True, stop=True), was, q_got, km_got[g], inc=q == 1)
                scores = b[:].rearrange("p (q m) -> p q m", q=2)
                top, total = small[:, 100 + 4 * tp:102 + 4 * tp], small[:, 102 + 4 * tp:104 + 4 * tp]
                t = dve.op(lambda e, s=scores, top=top: e.tensor_reduce(top, s, mybir.AxisListType.X, ALU.max), done, pr_read[tp])
                t = dve.op(lambda e, top=top: e.tensor_scalar(top, top, -SCALE, None, ALU.mult), t)
                for q in range(2):
                    t2 = act.op(lambda e, q=q, tp=tp, s=scores, top=top, total=total: e.activation(pr[tp][:, q, :], s[:, q, :], ACT.Exp,
                                bias=top[:, q:q + 1], scale=SCALE, accum_out=total[:, q:q + 1]), t, pr_read[tp])
                free[i] = [t2]
                t = dve.op(lambda e, total=total: e.reciprocal(total, total), t2)
                for q in range(2):
                    t = dve.op(lambda e, q=q, tp=tp, total=total: e.tensor_scalar(pr[tp][:, q, :], pr[tp][:, q, :], total[:, q:q + 1], None,
                                                                                ALU.mult), t, t2)
                pr_got[tp] = t
            qc_read = done
            zc_got, pt_got = [], []

            def take(c, half, b, done):
                n, tt, was = temporary()
                zc_got.append(silu2(zc[:, cut(half)], b[:], done, zc_read, tt[:], was))
                tmp_read[n] = zc_got[-1]
                return zc_got[-1]
            outputs(("zc", g), DT, P, h3, h3_got, take)
            for tp in range(NT // 2):
                i, b, was = bank()
                for mt in range(NM):
                    for q in range(2):
                        done = pe.op(lambda e, mt=mt, q=q, tp=tp, b=b: e.transpose(b[:, (mt * 2 + q) * P:(mt * 2 + q + 1) * P],
                                     pr[tp][:, q, mt * P:(mt + 1) * P], ident[:]), was, pr_got[tp], inc=(mt, q) == (NM - 1, 1))
                pr_read[tp] = done
                pt_got.append(act.op(lambda e, b=b, tp=tp: e.activation(pt[:, :, tp * 2 * P:(tp + 1) * 2 * P],
                              b[:].rearrange("p (m t) -> p m t", m=NM), ACT.Copy), done, pt_read))
                free[i] = [pt_got[-1]]
            zc_read = []
            for half in range(2):
                i, b, was = bank()
                for mt in range(NM):
                    done = pe.op(lambda e, mt=mt, g=g, b=b, half=half: e.matmul(b[:], vm[:, mt, g * P:(g + 1) * P], pt[:, mt, cut(half)],
                                 start=mt == 0, stop=mt == NM - 1), was, pt_got, vm_got, inc=mt == NM - 1)
                n, tt, was = temporary()
                t = dve.op(lambda e, tt=tt, b=b, half=half: e.scalar_tensor_tensor(tt[:], b[:], 0.5, zc[:, cut(half)], ALU.mult, ALU.mult),
                           done, was, zc_got)
                free[i] = [t]
                zc_read.append(t)
                yc_got[g][half] = split_value(yc[0][g][:, cut(half)], yc[1][g][:, cut(half)], tt[:], [t], [yp_last])
                tmp_read[n] = yc_got[g][half]
            pt_read = done
        yc_last = add_outputs("oc", yc, yc_got)

        q_all = sb("q_all", "g", 0, [P, NH, SEQ])
        k_all = sb("k_all", "g", 16 * KB, [P, NH, SEQ])
        v_tok = sb("v_tok", "g", 32 * KB, [P, NT, NH, P])
        o_all = sb("o_all", "g", 48 * KB, [P, NH, SEQ])
        work = [sb(f"work{n}", "g", 64 * KB + 4224 * n, [P, SEQ + 8]) for n in range(2)]
        before = [yc_last, pt_read, zc_read, yc_got[NH - 1], tmp_read]
        PAD_C = TAPS_C - 1
        work_read = [[dve.op(lambda e, n=n: e.memset(work[n][:, 0:PAD_C], 0.0), before)] for n in range(2)]
        q_got, k_got = [None] * NH, [None] * NH
        for j in range(2 * NH):
            dst = (q_all if j < NH else k_all)[:, j % NH, :]
            evac, w0 = [], work[0]

            def take(c, half, b, done, w0=w0):
                evac.append(act.op(lambda e: e.activation(w0[:, PAD_C + half * HALF:PAD_C + (half + 1) * HALF], b[:], ACT.Copy), done,
                                   work_read[0]))
                return evac[-1]
            outputs(("qk", j), DT, P, h3, h3_got, take)
            t = evac
            for m in range(TAPS_C):
                w, s = CH("conv_w_2", m * 2 * NH + j), w0[:, m:m + SEQ]
                if m == 0:
                    t = dve.op(lambda e, w=w, s=s, j=j, dst=dst: e.tensor_scalar(dst, s, w, CH("conv_b_2", j), ALU.mult, ALU.add), t, before)
                else:
                    t = dve.op(lambda e, w=w, s=s, dst=dst: e.scalar_tensor_tensor(dst, s, w, dst, ALU.mult, ALU.add), t)
            work_read[0] = [t]
            s = act.op(lambda e, dst=dst: e.activation(work[1][:, PAD_C:PAD_C + SEQ], dst, ACT.Tanh), t, work_read[1])
            t = dve.op(lambda e, dst=dst: e.scalar_tensor_tensor(dst, work[1][:, PAD_C:PAD_C + SEQ], 1.0, dst, ALU.add, ALU.mult), s)
            work_read[1] = [t]
            if j >= NH:
                t = dve.op(lambda e, dst=dst: e.tensor_scalar(dst, dst, SCALE, None, ALU.mult), t)
            (q_got if j < NH else k_got)[j % NH] = t
        v_got = []
        for g in range(NH):
            w0, evac, n = work[g % 2], [], g % 2

            def take(c, half, b, done, w0=w0):
                evac.append(act.op(lambda e: e.activation(w0[:, cut(half)], b[:], ACT.Copy), done, work_read[n]))
                return evac[-1]
            outputs(("v", g), DT, P, h3, h3_got, take)
            for half in range(2):
                i, b, was = bank()
                for q in range(4):
                    done = pe.op(lambda e, q=q, b=b, w0=w0, half=half: e.transpose(b[:, q * P:(q + 1) * P],
                                 w0[:, (half * 4 + q) * P:(half * 4 + q + 1) * P], ident[:]), was, evac, inc=q == 3)
                v_got.append(dve.op(lambda e, b=b, g=g, half=half: e.tensor_copy(v_tok[:, half * 4:half * 4 + 4, g, :],
                             b[:].rearrange("p (c d) -> p c d", c=4)), done, before))
                free[i] = [v_got[-1]]
            work_read[n] = [done]
        o_got = []
        for g in range(NH):
            def take(c, half, b, done):
                o_got.append(act.op(lambda e, g=g: e.activation(o_all[:, g, cut(half)], b[:], ACT.Tanh, scale=0.5), done, before))
                return o_got[-1]
            outputs(("o", g), DT, P, h3, h3_got, take)
        l_sz, l_szin = landing("sz"), landing("szin")
        sz_out = None
        for g in range(NH):
            w0, n, parts = work[g % 2], g % 2, []

            def take(c, half, b, done, w0=w0):
                t = act.op(lambda e: e.activation(w0[:, cut(half)], b[:], ACT.Tanh, scale=0.5), done, work_read[n])
                parts.append(dve.op(lambda e: e.scalar_tensor_tensor(w0[:, cut(half)], w0[:, cut(half)], 1.0, b[:], ALU.add, ALU.mult), t))
                return parts[-1]
            h3_last = outputs(("za", g), DT, P, h3, h3_got, take)
            sz_out = sp.dma(lambda e, g=g, w0=w0: e.dma_start(sz_dram[g], w0[:, 0:SEQ]), l_sz, parts)
            work_read[n] = [sz_out]

        NP, PAIR = NT // 2, 2 * P
        both = lambda p: slice(p * PAIR, (p + 1) * PAIR)
        mb = sb("mb", "h", 0, [P, NH, SEQ])
        nb = sb("nb", "h", 16 * KB, [P, NH, SEQ])
        mb_got, nb_got, wa_got = [], [], []
        for p in range(NP):
            mb_got.append(sp.dma(lambda e, p=p: e.dma_start(mb[:, :, both(p)], rows_dram[0, :, both(p)].partition_broadcast(P)),
                                 landing(f"mb{p}"), h3_last, rows_out))
            nb_got.append(sp.dma(lambda e, p=p: e.dma_start(nb[:, :, both(p)], rows_dram[1, :, both(p)].partition_broadcast(P)),
                                 landing(f"nb{p}"), h3_last, rows_out))
        o = 32 * KB
        buf = {}
        for name in ("dec", "qa", "pts", "kts"):
            for n in range(2):
                buf[name, n] = sb(f"{name}{n}", "h", o, [P, NH, P]); o += 2048
        dens = sb("dens", "h", o, [P, NH, P]); o += 2048
        sqs = sb("sqs", "h", o, [P, NH, P]); o += 2048
        ones_sq = sb("ones_sq", "h", o, [P, P]); o += 512
        mean_sq = sb("mean_sq", "h", o, [P, P]); o += 512
        x3 = [sb(f"x3_{n}", "h", o + 4096 * n, [P, D]) for n in range(2)]
        state = sb("state", "g", 64 * KB, [P, NH, P])
        nstate = sb("nstate", "g", 66 * KB, [P, 8])
        grow = sb("grow", "g", 66 * KB + 64, [P, D])
        sz = sb("sz", "g", 16 * KB, [P, NH, SEQ])
        ya_hi = sb("ya_hi", "g", 32 * KB, [P, NP, NH, PAIR], F32R)
        ya_lo = sb("ya_lo", "g", 0, [P, NH, SEQ], F32R)
        ones_got = dve.op(lambda e: e.memset(ones_sq[:], 1.0), h3_last)
        mean_got = dve.op(lambda e: e.memset(mean_sq[:], 1.0 / HD), h3_last)

        last_blocks = [weights(("oa", c))[0] for c in range(3)]
        last_raw = sb("last_raw", "h", o, [P, NH, PAIR])
        last_hi, last_lo = (sb(f"last_{n}", "raw", 4096 * m, [P, NH, PAIR], F32R) for m, n in enumerate(("hi", "lo")))
        late = {}

        def late_loads():
            t = sp.dma(lambda e: e.dma_start(last_raw[:], w_out2[0:GROUP, 3 * PAIR:4 * PAIR].rearrange("(k p) c -> p k c", p=P)),
                       landing("last_raw"), h3_last)
            late["gain"] = sp.dma(lambda e: e.dma_start(grow[:], A["final_norm_g_2"].partition_broadcast(P)), landing("grow"), sz_out,
                                  work_read)
            t = split_value(last_hi[:], last_lo[:], last_raw[:], [t], raw_free)
            last_blocks.append((last_hi, last_lo, t))
            x3_read[:] = t, t

        xc_view = xcol[:].rearrange("p (c h) -> p h c", h=NH)
        w_view, a_view = wcol[:].rearrange("p (h c) -> p h c", h=NH), acol[:].rearrange("p (h c) -> p h c", h=NH)
        mp_view = mprev[:].rearrange("p (h c) -> p h c", h=NH)
        flat2 = lambda t: t[:].rearrange("p h t -> p (h t)")
        read = {k: [] for k in buf}
        dens_read, sqs_read = [None], [None]
        state_got, state_read = [[]], [sz_out, work_read]
        ready_front, v2_got, sn_got, keys_read, values_read = [None] * NT, [None] * NT, [None] * NT, [None] * NT, [None] * NT

        def front(c):
            n, p, tok = c % 2, c // 2, slice(c * P, (c + 1) * P)
            mbc = mb[:, :, tok]
            dec, qa, pts, kts = (buf[name, n] for name in ("dec", "qa", "pts", "kts"))
            if c % 2 == 0:
                cs, ends = slice(c, c + 2), mb[:, :, c * P + P - 1:(c + 2) * P:P]
                t = dve.op(lambda e: e.tensor_tensor(w_view[:, :, cs], xc_view[:, :, cs], ends, ALU.subtract), mb_got[p], xcol_got)
                w = act.op(lambda e: e.activation(w_view[:, :, cs], w_view[:, :, cs], ACT.Exp), t)
                t = dve.op(lambda e: e.tensor_tensor(a_view[:, :, cs], mp_view[:, :, cs], ends, ALU.subtract), mb_got[p], mp_got)
                wa_got.append([w, act.op(lambda e: e.activation(a_view[:, :, cs], a_view[:, :, cs], ACT.Exp), t)])
            t = dve.op(lambda e: e.tensor_tensor(dec[:], mask[:].unsqueeze(1).broadcast_to([P, NH, P]), mbc, ALU.subtract),
                       mask_got, mb_got[p], read["dec", n])
            for g in range(NH):
                dec_got = act.op(lambda e, g=g: e.activation(dec[:, g, :], dec[:, g, :], ACT.Exp, bias=xcol[:, c * NH + g:c * NH + g + 1]),
                                 t, xcol_got)
            i, b, was = bank()
            for g in range(NH):
                done = pe.op(lambda e, g=g: e.matmul(b[:, g * P:(g + 1) * P], k_all[:, g, tok], q_all[:, g, tok], start=True,
                                                     stop=True), was, q_got, k_got, inc=g == NH - 1)
            p_got = dve.op(lambda e: e.tensor_tensor(flat2(pts), b[:], flat2(dec), ALU.mult), done, dec_got, read["pts", n])
            free[i] = [p_got]
            read["dec", n] = [p_got]
            i, b2, was = bank()
            for g in range(NH):
                done = pe.op(lambda e, g=g: e.transpose(b2[:, g * P:(g + 1) * P], k_all[:, g, tok], ident[:]), was, k_got, inc=g == NH - 1)
            keys_read[c] = done
            for g in range(NH):
                kt_got = act.op(lambda e, g=g: e.activation(kts[:, g, :], b2[:, g * P:(g + 1) * P], ACT.Copy,
                                scale=wcol[:, g * NT + c:g * NT + c + 1]), done, wa_got[p], read["kts", n])
            free[i] = [kt_got]
            qa_got = None
            if c:
                for g in range(NH):
                    t = act.op(lambda e, g=g: e.activation(qa[:, g, :], mbc[:, g, :], ACT.Exp, scale=-1.0,
                               bias=mprev[:, g * NT + c:g * NT + c + 1]), mb_got[p], mp_got, read["qa", n])
                qa_got = dve.op(lambda e: e.tensor_tensor(qa[:], qa[:], q_all[:, :, tok], ALU.mult), t, q_got)
            ready_front[c] = (p_got, kt_got, qa_got)

        def back(c):
            n, p, tok = c % 2, c // 2, slice(c * P, (c + 1) * P)
            qa, pts, kts = (buf[name, n] for name in ("qa", "pts", "kts"))
            p_got, kt_got, qa_got = ready_front[c]
            o_view = o_all[:, :, tok]
            i, b, was = bank()
            for g in range(NH):
                done = pe.op(lambda e, g=g: e.matmul(b[:, g * P:(g + 1) * P], v_tok[:, c, g, :], pts[:, g, :], start=True, stop=c == 0,
                                                     skip_group_check=True), was, p_got, v_got, inc=g == NH - 1)
                if c:
                    done = pe.op(lambda e, g=g: e.matmul(b[:, g * P:(g + 1) * P], state[:, g, :], qa[:, g, :], start=False, stop=True,
                                                         skip_group_check=True), qa_got, state_got[0], inc=g == NH - 1)
            sn = dve.op(lambda e: e.scalar_tensor_tensor(o_view, o_view, 1.0, b[:].rearrange("p (h t) -> p h t", h=NH), ALU.add,
                                                         ALU.mult), done, o_got)
            free[i] = [sn]
            i, b2, was = bank()
            done = pe.op(lambda e: e.matmul(b2[:], ones_sq[:], flat2(pts), start=True, stop=c == 0, skip_group_check=True), was, p_got,
                         ones_got)
            if c:
                for g in range(NH):
                    done = pe.op(lambda e, g=g: e.matmul(b2[:, g * P:(g + 1) * P], nstate[:, g:g + 1].broadcast_to([P, P]), qa[:, g, :],
                                                         start=False, stop=g == NH - 1, skip_group_check=True), qa_got, state_got[0])
            den_done, den_i = done, i
            read["pts", n] = read["qa", n] = [done]
            i, b3, was = bank()
            for g in range(NH):
                done = pe.op(lambda e, g=g: e.matmul(b3[:, g * P:(g + 1) * P], kts[:, g, :], v_tok[:, c, g, :], start=True, stop=True),
                             was, kt_got, v_got)
            for g in range(NH):
                done = pe.op(lambda e, g=g: e.matmul(stat_bank[:, g:g + 1], kts[:, g, :], ones[:, 0:1], start=True, stop=True),
                             stat_free[0], inc=g == NH - 1)
            read["kts", n] = [done]
            values_read[c] = done
            updates = []
            for g in range(NH):
                if c == 0:
                    updates.append(dve.op(lambda e, g=g: e.tensor_copy(state[:, g, :], b3[:, g * P:(g + 1) * P]), done, state_read))
                    updates.append(dve.op(lambda e, g=g: e.tensor_copy(nstate[:, g:g + 1], stat_bank[:, g:g + 1]), done, state_read))
                else:
                    col = acol[:, g * NT + c:g * NT + c + 1]
                    updates.append(dve.op(lambda e, g=g, col=col: e.scalar_tensor_tensor(state[:, g, :], state[:, g, :], col,
                                   b3[:, g * P:(g + 1) * P], ALU.mult, ALU.add), done, wa_got[p], state_got[0]))
                    updates.append(dve.op(lambda e, g=g, col=col: e.scalar_tensor_tensor(nstate[:, g:g + 1], nstate[:, g:g + 1], col,
                                   stat_bank[:, g:g + 1], ALU.mult, ALU.add), done, wa_got[p], state_got[0]))
            free[i] = [updates]
            state_got[0] = updates
            stat_free[0] = [updates]
            t = act.op(lambda e: e.activation(dens[:], nb[:, :, tok], ACT.Exp), nb_got[p], dens_read[0])
            s = act.op(lambda e: e.activation(sqs[:], o_view, ACT.Square), sn, sqs_read[0])
            a = act.op(lambda e: e.activation(b2[:], b2[:], ACT.Abs), den_done)
            t = dve.op(lambda e: e.tensor_tensor(flat2(dens), b2[:], flat2(dens), ALU.max), t, a)
            free[den_i] = [t]
            t = act.op(lambda e: e.activation(dens[:], dens[:], ACT.Square, scale=2.0 * EPS ** 0.5), t)
            i, b4, was = bank()
            done = pe.op(lambda e: e.matmul(b4[:], mean_sq[:], flat2(sqs), start=True, stop=True), was, s, mean_got)
            sqs_read[0] = done
            v2 = dve.op(lambda e: e.tensor_tensor(q_all[:, :, tok], b4[:].rearrange("p (h t) -> p h t", h=NH), dens[:], ALU.add), done, t,
                        keys_read[c], qa_got)
            free[i] = [v2]
            dens_read[0] = v2
            v2_got[c], sn_got[c] = v2, sn

        l_out = landing("out")
        out_rows = out.rearrange("b (t p) d -> p (b t) d", p=P)
        sz_got, sums_got, x3_read, stores = [None] * NP, [None] * NT, [None, None], []
        part = small[:, 120:120 + 2 * NT].rearrange("p (t c) -> p t c", c=2)
        l_szs = [l_szin] + [landing(f"szin{p}") for p in range(1, NP)]

        def gate_load(p):
            sz_got[p] = sp.dma(lambda e: e.dma_start(sz[:, :, both(p)], sz_dram[:, :, both(p)].rearrange("h p t -> p h t")), l_szs[p],
                               sz_out, keys_read[2 * p], keys_read[2 * p + 1])

        l_outs = [l_out, landing("out1")]

        def norm_rows(tiles):
            v = stat[:, tiles[0]:tiles[-1] + 1]
            t = dve.op(lambda e: e.tensor_tensor(v, part[:, tiles[0]:tiles[-1] + 1, 0], part[:, tiles[0]:tiles[-1] + 1, 1], ALU.add),
                       [sums_got[t] for t in tiles])
            r = rstd_of(slice(tiles[0], tiles[-1] + 1), 1.0 / D, t)
            for t in tiles:
                z = dve.op(lambda e, t=t: e.scalar_tensor_tensor(x3[t % 2][:], x3[t % 2][:], stat[:, t:t + 1], grow[:], ALU.mult,
                                                                 ALU.mult), r, late["gain"])
                stores.append(sp.dma(lambda e, t=t: e.dma_start(out_rows[:, t, :], x3[t % 2][:]), l_outs[t % 2], z))
                x3_read[t % 2] = stores[-1]

        def heads_rms(tiles):
            qv = q_all[:, :, tiles[0] * P:(tiles[-1] + 1) * P]
            t = act.op(lambda e: e.activation(qv, qv, ACT.Sqrt), v2_got[tiles[0]:tiles[-1] + 1])
            return dve.op(lambda e: e.reciprocal(qv, qv), t)

        def gate_heads(tiles, t):
            tok, p = slice(tiles[0] * P, (tiles[-1] + 1) * P), tiles[0] // 2
            own = slice(tiles[0] % 2 * P, (tiles[-1] % 2 + 1) * P)
            ov, qv = o_all[:, :, tok], q_all[:, :, tok]
            for g in range(NH):
                t = dve.op(lambda e, g=g: e.scalar_tensor_tensor(ov[:, g, :], ov[:, g, :], CH("mlstm_norm_g_2", g), qv[:, g, :], ALU.mult,
                                                                 ALU.mult), t, sn_got[tiles[0]:tiles[-1] + 1])
            t = dve.op(lambda e: e.tensor_tensor(ov, ov, sz[:, :, tok], ALU.mult), t, sz_got[p])
            t = split_value(ya_hi[:, p, :, own], ya_lo[:, :, tok], ov, [t], [values_read[2 * p:2 * p + 2]])
            for tile in tiles:
                ya_got[tile] = t

        ya_got = [None] * NT

        def multiply_out(t):
            half, tok, own = t // 4, slice(t * P, (t + 1) * P), slice((t % 2) * P, (t % 2 + 1) * P)
            sums_got[t] = []
            for m in range(2):
                i, b, was = bank()
                for c in (2 * m, 2 * m + 1):
                    w_hi, w_lo, w_got = last_blocks[c]
                    terms = [(ya_hi[:, t // 2, g, own], ya_lo[:, g, tok], w_hi[:, g, :], w_lo[:, g, :], ya_got[t]) for g in range(NH)]
                    product(b[:, (c % 2) * PAIR:(c % 2 + 1) * PAIR], terms, [was, w_got], start=c % 2 == 0, stop=False)
                for q in range(4):
                    j = 4 * m + q
                    done = pe.op(lambda e, q=q, j=j, b=b: e.matmul(b[:, q * P:(q + 1) * P], y1[j][:, tok], ident[:],
                                 start=False, stop=q == 3, skip_group_check=True), y1_got[j][half], inc=q == 3)
                a = act.op(lambda e, b=b, m=m: e.activation(x3[t % 2][:, m * HALF:(m + 1) * HALF], b[:], ACT.Copy), done,
                           x3_read[t % 2])
                a = act.op(lambda e, b=b, m=m: e.activation(b[:], b[:], ACT.Square, accum_out=part[:, t, m:m + 1]), a)
                sums_got[t].append(a)
                free[i] = [a]

        front(0)
        for c in range(NT):
            if c + 1 < NT:
                front(c + 1)
                if c % 2 == 0:
                    gate_load(c // 2)
            back(c)
            if c == 0:
                late_loads()
            if c % 2 == 1:
                last = c == NT - 1
                if c >= 5:
                    norm_rows([c - 5, c - 4])
                rms = [heads_rms([c - 1]), heads_rms([c])] if last else [heads_rms([c - 1, c])]
                if last:
                    gate_heads([c - 1], rms[0])
                if c >= 3:
                    multiply_out(c - 3)
                    multiply_out(c - 2)
                gate_heads([c] if last else [c - 1, c], rms[-1])
        norm_rows([NT - 4, NT - 3])
        multiply_out(NT - 2)
        multiply_out(NT - 1)
        norm_rows([NT - 2])
        norm_rows([NT - 1])
        sp.wait(stores[-2:])
        finish(nc, ctx, pe, act, dve, pool, sp)


def finish(nc, ctx, pe, act, dve, pool, sp):
    block = ctx.enter_context(nc.Block())
    block.sync(lambda e: sp.play(e))
    block.tensor(lambda e: pe.play(e))
    block.scalar(lambda e: act.play(e))
    block.vector(lambda e: dve.play(e))
    block.gpsimd(lambda e: pool.play(e))


def kernel(**inputs):
    import numpy as np
    import concourse.bacc as bacc
    from concourse.bass_utils import run_bass_kernel_spmd

    nc = bacc.Bacc("TRN2", target_bir_lowering=False, num_devices=1)
    arrays, A = {}, {}
    tokens = np.arange(P)
    rcnt = np.ones((P, 16 * NH), np.float32)
    for g, w in enumerate(WINDOWS):
        rcnt[:, 16 * g:16 * g + w] = w / np.arange(1, w + 1, dtype=np.float32)
    constants = {"ident": np.eye(P, dtype=np.float32),
                 "mask": np.where(tokens[:, None] <= tokens[None, :], 0.0, -1.0e30).astype(np.float32),
                 "rcnt": rcnt}
    for name, a in [*inputs.items(), *constants.items()]:
        a = np.ascontiguousarray(a)
        arrays[f"in_{name}"] = a
        A[name] = nc.dram_tensor(f"in_{name}", a.shape, mybir.dt.from_np(a.dtype), kind="ExternalInput").ap()
    out = nc.dram_tensor("out_0", (1, SEQ, D), F32, kind="ExternalOutput").ap()
    build_program(nc, A, out)
    result = run_bass_kernel_spmd(nc, [arrays], core_ids=[0])
    return result.results[0]["out_0"]
```

```python
import concourse.bass as bass
from concourse import mybir
from contextlib import ExitStack

F32 = mybir.dt.float32
F32R = mybir.dt.float32r
ALU = mybir.AluOpType
ACT = mybir.ActivationFunctionType

P = 128
HALF = 512
KB = 1024

SEQ = 1024
D = 1024
D_RNN = 1536
HEAD = 96
TAPS_A, TAPS_B = 31, 4
LAG = 1
D_FF = 4096
EPS = 1e-6
LRU_C = 8.0
GROUP = 512
HD = 128
NH = GROUP // HD
TAPS_C = 4
N_MEM = 256
WINDOWS = (2, 4, 8, 16)
NT = SEQ // P
DT = D // P
BIG = 3.0e38

Z_VA, Z_GA, Z_XB, Z_GB, Z_SA, Z_SB = 0, D, 2 * D, 2 * D + D_RNN, 2 * D + 2 * D_RNN, 3 * D + 2 * D_RNN
Y_QK, Y_V, Y_O, Y_ZA = 0, 2 * GROUP, 3 * GROUP, 4 * GROUP
Y_G = 5 * GROUP
Y_U = Y_G + 2 * NH
Y_ZB, Y_QC, Y_ZC = Y_U + GROUP, Y_U + 2 * GROUP, Y_U + 3 * GROUP

PARAMS = [("g_mix", 8), ("b_in", 56), ("conv_a_b", 8), ("ln_g", 8), ("ln_b", 8), ("conv_b_b", 12),
          ("b_rg_a", 12), ("b_rg_x", 12), ("lam", 12), ("conv_b_w", 48), ("conv_a_w", 248), ("g_mlp", 8),
          ("g_final", 8), ("norm_g_2", 8), ("conv_w_2", 32), ("conv_b_2", 8), ("mlstm_norm_g_2", 4),
          ("pool_scale_2", 4), ("mem_norm_g_2", 8)]
ROWS = sum(n for _, n in PARAMS)
assert ROWS == 4 * P


class Queue:

    def __init__(self, sem):
        self.sem, self.count, self.program = sem, 0, []

    def op(self, make, *waits, inc=True):
        self.program.append((list(flat(waits)), make, (self.sem, 1) if inc else None))
        self.count += inc
        return self.sem, self.count

    def dma(self, make, landing, *waits):
        landing.count += 16
        self.program.append((list(flat(waits)), make, (landing.sem, 16)))
        return landing.sem, landing.count

    def wait(self, *waits):
        self.program.append((list(flat(waits)), None, None))

    def play(self, engine):
        passed = {}
        for waits, make, signal in self.program:
            for sem, value in waits:
                if passed.get(id(sem), 0) < value:
                    engine.wait_ge(sem, value)
                    passed[id(sem)] = value
            if make is None:
                continue
            instruction = make(engine)
            if signal:
                instruction.then_inc(*signal)


class Landing:

    def __init__(self, sem):
        self.sem, self.count = sem, 0


def flat(waits):
    for w in waits:
        if isinstance(w, list):
            yield from flat(w)
        elif w is not None:
            yield w


def build_program(nc, A, out):
    ctx = ExitStack()
    with ctx:
        sem = lambda name: ctx.enter_context(nc.semaphore(name))
        pe, act, dve, pool, sp = (Queue(sem(f"{n}_done")) for n in ("pe", "act", "dve", "pool", "sp"))
        landing = lambda name: Landing(sem(f"landed_{name}"))

        base = (nc.sbuf_base + 31) // 32 * 32
        sizes = [("const", 7552), ("raw", 8 * KB), ("split", 24 * KB), ("h", 64 * KB), ("y", 32 * KB), ("g", 73984)]
        region, at = {}, base
        for name, size in sizes:
            region[name] = at
            at += size
        assert at <= nc.sbuf_usable_end, (at, nc.sbuf_usable_end)
        ends = dict(zip([n for n, _ in sizes], [region[n] + s for n, s in sizes]))

        def sb(name, where, offset, shape, dt=F32):
            n = 4
            for s in shape[1:]:
                n *= s
            assert region[where] + offset + n <= ends[where], name
            return nc.alloc_sbuf_tensor_at(name, shape, dt, offset=region[where] + offset)

        par = sb("par", "const", 0, [P, ROWS])
        parh = sb("parh", "const", 2048, [P, ROWS])
        ident = sb("ident", "const", 4096, [P, P])
        ones = sb("ones", "const", 4608, [P, 8])
        sp4 = sb("sp4", "const", 4640, [P, 16])
        nsp4 = sb("nsp4", "const", 4704, [P, 16])
        stat = sb("stat", "const", 4768, [P, 32])
        small = sb("small", "const", 4896, [P, 192])
        xcol = sb("xcol", "const", 5664, [P, 32])
        mprev = sb("mprev", "const", 5792, [P, 32])
        wcol = sb("wcol", "const", 5920, [P, 32])
        acol = sb("acol", "const", 6048, [P, 32])
        gcol = sb("gcol", "const", 6176, [P, 16])
        rcnt = sb("rcnt", "const", 6240, [P, 64])
        ones_sq = sb("ones_sq", "const", 7040, [P, P])
        mask = sb("mask", "const", 6528, [P, P])

        offsets, at = {}, 0
        for name, rows in PARAMS:
            offsets[name] = at
            at += rows
        C = lambda name, j: par[:, offsets[name] + j:offsets[name] + j + 1]
        CH = lambda name, j: parh[:, offsets[name] + j:offsets[name] + j + 1]

        banks = [ctx.enter_context(nc.psum_tensor(f"bank{i}", [P, HALF], F32)) for i in range(8)]
        ring = [8]
        free = [[] for _ in range(8)]
        turn = [0]

        def bank():
            i = turn[0] % ring[0]
            turn[0] += 1
            was = free[i]
            assert was is not None, "the bank's reader isn't known yet"
            free[i] = None
            return i, banks[i], was

        sum_banks, sum_free = banks[6:8], [None, None]

        def set_ring(n):
            for i in range(6, 8):
                if ring[0] > i >= n:
                    sum_free[i - 6] = free[i]
                elif ring[0] <= i < n:
                    free[i] = [sum_free[i - 6]]
            ring[0], turn[0] = n, 0

        stat_bank = sum_banks[1]

        raw = [sb(f"raw{i}", "raw", 4096 * i, [P, 1024]) for i in range(2)]
        whi = [sb(f"whi{i}", "split", 8192 * i, [P, 1024], F32R) for i in range(3)]
        wlo = [sb(f"wlo{i}", "split", 8192 * i + 4096, [P, 1024], F32R) for i in range(3)]
        raw_landed = [landing(f"raw{i}") for i in range(2)]
        raw_free = [None, None]
        split_free = [None, None, None]
        plan = []
        ready = {}
        at_use = [0]
        eager = [True]

        def load(i):
            key, pieces, kt, cols, clear = plan[i]
            r, n = i % 2, kt * cols
            waits = [raw_free[r]]
            if clear:
                waits = [pool.op(lambda e: e.memset(raw[r][:], 0.0), waits)]
            view = raw[r][:, 0:n].rearrange("p (k c) -> p k c", k=kt)
            for where, src in pieces:
                got = sp.dma(lambda e, d=view[:, :, where[0]:where[1]], s=src: e.dma_start(d, s), raw_landed[r], waits)
            return got

        loads = {}

        def split(i):
            key, pieces, kt, cols, clear = plan[i]
            r, s, n = i % 2, i % 3, kt * cols
            if i not in loads:
                loads[i] = load(i)
            hi = act.op(lambda e: e.activation(whi[s][:, 0:n], raw[r][:, 0:n], ACT.Copy), loads[i], split_free[s])
            lo = dve.op(lambda e: e.tensor_tensor(wlo[s][:, 0:n], raw[r][:, 0:n], whi[s][:, 0:n].bitcast(F32),
                                                  ALU.subtract), hi, split_free[s])
            raw_free[r] = [hi, lo]
            ready[i] = (whi[s][:, 0:n].rearrange("p (k c) -> p k c", k=kt),
                        wlo[s][:, 0:n].rearrange("p (k c) -> p k c", k=kt), [hi, lo])
            if i + 1 < len(plan) and i + 1 not in loads:
                loads[i + 1] = load(i + 1)

        def prefetch():
            for j in range(2):
                split(j)

        def split_ahead(i=None):
            i = at_use[0] if i is None else i
            for j in range(i, min(i + 3, len(plan))):
                if j not in ready:
                    if j >= 3 and split_free[j % 3] is None:
                        break
                    split(j)

        def weights(key):
            i = at_use[0]
            assert plan[i][0] == key, (plan[i][0], key)
            at_use[0] += 1
            split_ahead(i)
            assert i in ready
            split_free[i % 3] = None
            return ready[i], i % 3

        def need(key, src, row0, kt, col0, cols):
            piece = src[row0:row0 + kt * P, col0:col0 + cols].rearrange("(k p) c -> p k c", p=P)
            plan.append((key, [((0, cols), piece)], kt, cols, False))

        def product(target, terms, waits, start=True, stop=True):
            last = len(terms) - 1
            done = None
            for n, (lh, ll, rh, rl, tokens) in enumerate(terms):
                for m, (l, r) in enumerate(((lh, rh), (lh, rl), (ll, rh))):
                    first, end = start and n == 0 and m == 0, n == last and m == 2
                    done = pe.op(lambda e, l=l, r=r, a=first, b=end and stop: e.matmul(target, l, r, start=a, stop=b,
                                                                                skip_group_check=True),
                                 waits if n == 0 and m == 0 else [], tokens if m == 0 else [], inc=end)
            return done

        def pair(name, where, offset, n, width=SEQ):
            return ([sb(f"{name}_hi{i}", where, offset + 8 * width * i, [P, width], F32R) for i in range(n)],
                    [sb(f"{name}_lo{i}", where, offset + 8 * width * i + 4 * width, [P, width], F32R) for i in range(n)])

        cut = lambda half: slice(half * HALF, (half + 1) * HALF)

        def split_value(hi, lo, value, waits, over=()):
            a = act.op(lambda e: e.activation(hi, value, ACT.Copy), waits, list(over))
            b = dve.op(lambda e: e.tensor_tensor(lo, value, hi.bitcast(F32), ALU.subtract), a, waits, list(over))
            return [a, b]

        def outputs(key, kt, cols, rhs, tokens, consume, k0=0):
            (hi, lo, got), slot = weights(key)
            for c in range(cols // P):
                for half in range(2):
                    i, b, was = bank()
                    terms = [(hi[:, k, c * P:(c + 1) * P], lo[:, k, c * P:(c + 1) * P], rhs[0][k0 + k][:, cut(half)],
                              rhs[1][k0 + k][:, cut(half)], tokens[k0 + k][half]) for k in range(kt)]
                    done = product(b[:], terms, [was, got])
                    split_free[slot] = done
                    read = consume(c, half, b, done)
                    free[i] = None if read is None else [read]
            if eager[0]:
                split_ahead()
            return done

        def outputs_by_half(keys, kt, rhs, tokens, consume):
            blocks = [weights(key) for key in keys]
            for half in range(2):
                for n, ((hi, lo, got), slot) in enumerate(blocks):
                    i, b, was = bank()
                    terms = [(hi[:, k, :], lo[:, k, :], rhs[0][k][:, cut(half)], rhs[1][k][:, cut(half)], tokens[k][half])
                             for k in range(kt)]
                    done = product(b[:], terms, [was, got])
                    if half:
                        split_free[slot] = done
                    free[i] = [consume(n, half, b, done)]
                    if half:
                        split_ahead()
            return done

        x_rows = A["x"].rearrange("b (t p) d -> p (b t) d", p=P)
        x_in = sb("x_in", "g", 0, [P, NT, D])
        square_out = sb("square_out", "g", 32 * KB, [P, D])
        rows_in = [sb(f"rows_in{i}", "g", 36 * KB + 512 * i, [P, P]) for i in range(4)]
        l_rows, l_x, l_const = [landing(f"rows{n}") for n in range(4)], [landing(f"x{t}") for t in range(NT)], landing("const")
        got_ident = sp.dma(lambda e: e.dma_start(ident[:], A["ident"]), l_const)
        load_x = lambda t: sp.dma(lambda e: e.dma_start(x_in[:, t, :], x_rows[:, t, :]), l_x[t])
        row_pieces = [[] for _ in range(4)]
        for name, rows in PARAMS:
            a = A[name]
            flat_rows = a.rearrange("l (k p) -> (l k) p", p=P) if len(a.shape) == 2 else (
                a.rearrange("(k p) -> k p", p=P) if len(a.shape) == 1 else a.rearrange("l t (k p) -> (l t k) p", p=P))
            done = 0
            while done < rows:
                at = offsets[name] + done
                n = min(rows - done, P - at % P)
                row_pieces[at // P].append((rows_in[at // P][at % P:at % P + n, :], flat_rows[done:done + n, :]))
                done += n

        def load_rows(s):
            for dst, src in row_pieces[s]:
                got = sp.dma(lambda e, dst=dst, src=src: e.dma_start(dst, src), l_rows[s])
            return got

        got_x = [load_x(0), load_x(1)]
        got_rows = [load_rows(0)]
        got_x += [load_x(t) for t in range(2, NT)]
        dve.op(lambda e: e.memset(ones[:], 1.0))
        got_ones = dve.op(lambda e: e.memset(ones_sq[:], 1.0))

        def turn_rows(s, waits):
            i, b, was = bank()
            block = slice(s * P, (s + 1) * P)
            turned = pe.op(lambda e: e.transpose(b[:, 0:P], rows_in[s][:], ident[:]), waits, got_ident, was)
            t = dve.op(lambda e: e.tensor_copy(par[:, block], b[:, 0:P]), turned)
            free[i] = [t]
            return [t, dve.op(lambda e: e.tensor_scalar(parh[:, block], par[:, block], 0.5, None, ALU.mult), t)]

        got_par = turn_rows(0, got_rows[0])
        got_parh = got_par

        def rstd_of(columns, inv_n, waits):
            v = stat[:, columns]
            t = dve.op(lambda e: e.tensor_scalar(v, v, inv_n, EPS, ALU.mult, ALU.add), waits)
            t = act.op(lambda e: e.activation(v, v, ACT.Sqrt), t)
            return dve.op(lambda e: e.reciprocal(v, v), t)

        h = pair("h", "h", 0, DT)
        h_got = [[None, None] for _ in range(DT)]
        normed = []
        for half in range(2):
            for t in range(half * 4, half * 4 + 4):
                s = act.op(lambda e, t=t: e.activation(square_out[:], x_in[:, t, :], ACT.Square, accum_out=stat[:, t:t + 1]),
                           got_x[t], (act.sem, act.count) if t else None)
            r = rstd_of(slice(half * 4, half * 4 + 4), 1.0 / D, s)
            for t in range(half * 4, half * 4 + 4):
                normed.append(dve.op(lambda e, t=t: e.tensor_scalar(x_in[:, t, :], x_in[:, t, :], stat[:, t:t + 1], None,
                                                                    ALU.mult), r))
        def evacuate_split(hi, lo, source, scale, waits):
            a = act.op(lambda e: e.activation(hi, source, ACT.Copy, scale=scale), waits)
            b = dve.op(lambda e: e.scalar_tensor_tensor(lo, source, scale, hi.bitcast(F32), ALU.mult, ALU.subtract), a, waits)
            return [a, b]

        w_in = A["w_in"][0]
        w_b_out, w_a_out, w_o = A["w_b_out"][0], A["w_a_out"][0], A["w_o"][0]
        NG, GT = D_RNN // (3 * P), 3

        def plan_xb(g):
            for t in range(GT):
                need(("xb", g, t), w_in, 0, DT, Z_XB + (g * GT + t) * P, P)

        def plan_gb(g, tiles):
            for t in tiles:
                need(("gb", g, t), w_in, 0, DT, Z_GB + (g * GT + t) * P, P)

        def plan_a(names, j):
            for name, col in (("va", Z_VA), ("ga", Z_GA), ("sb", Z_SB), ("sa", Z_SA)):
                if name in names:
                    need((name, j), w_in, 0, DT, col + j * P, P)

        plan_xb(0)
        plan_gb(0, [0])
        for g in range(NG):
            plan_gb(g, range(1, GT))
            if g + 1 < NG:
                plan_xb(g + 1)
                plan_gb(g + 1, [0])
            else:
                plan_a(("va", "ga"), 0)
                plan_a(("va", "ga"), 1)
            for c in range(4):
                need(("yb", g, c), w_b_out, g * GT * P, GT, c * 2 * P, 2 * P)
        for j in range(DT + LAG):
            if 2 <= j < DT:
                plan_a(("va", "ga"), j)
            if j >= LAG:
                plan_a(("sb", "sa"), j - LAG)
        for j in range(DT):
            need(("ya", j), w_a_out, 0, DT, j * P, P)
        for j in range(DT):
            need(("wo", j), w_o, 0, DT, j * P, P)
        w_1, w_2 = A["w_1"][0], A["w_2"][0]
        FC = D_FF // D
        for f in range(FC):
            for j in range(DT):
                need(("w1", f, j), w_1, 0, DT, (f * DT + j) * P, P)
            for j in range(DT):
                need(("w2", f, j), w_2, f * D, DT, j * P, P)

        loads[0], loads[1] = load(0), load(1)
        got_rows += [load_rows(s) for s in range(1, 4)]
        mask_got = sp.dma(lambda e: e.dma_start(mask[:], A["mask"]), landing("mask"))
        for half in range(2):
            for j in range(DT):
                i, b, was = bank()
                for q in range(4):
                    t = half * 4 + q
                    turned = pe.op(lambda e, t=t, q=q, j=j, b=b: e.transpose(b[:, q * P:(q + 1) * P],
                                   x_in[:, t, j * P:(j + 1) * P], ident[:]), normed[t], was, got_ident)
                h_got[j][half] = evacuate_split(h[0][j][:, cut(half)], h[1][j][:, cut(half)], b[:], C("g_mix", j),
                                                [turned, got_par])
                free[i] = h_got[j][half]
            if half == 0:
                prefetch()
        x_in_read = turned

        got_par = got_parh = [turn_rows(s, got_rows[s]) for s in range(1, 4)] + [got_par]
        yb = [sb(f"yb{j}", "y", 4096 * j, [P, SEQ]) for j in range(DT)]
        o = 0
        xb_in = sb("xb_in", "g", o, [P, SEQ + 32]); o += 4 * (SEQ + 32)
        v = [sb(f"v{t}", "g", o + 4096 * t, [P, SEQ]) for t in range(GT)]; o += 4096 * GT
        G = [sb(f"gelu{t}", "g", o + 4096 * t, [P, SEQ]) for t in range(GT)]; o += 4096 * GT
        vg = pair("vg", "g", o, GT); o += 8192 * GT
        T1, T2, T3 = (sb(f"lru{i}", "g", o + 4096 * i, [P, SEQ]) for i in range(3)); o += 3 * 4096
        PAD_B, NR = TAPS_B - 1, D_RNN // P

        PAIRS = [(0, 0), (1, 0), (0, 1), (1, 1), (2, 1), (1, 2), (2, 2)]
        gate_w = [sb(f"gate_w{n}", "g", o + 3584 * n, [P, len(PAIRS), P]) for n in range(2)]
        l_gate = [landing(f"gate{n}") for n in range(2)]
        gate_read = [[None], [None]]
        start_gates = [pool.op(lambda e, n=n: e.memset(gate_w[n][:], 0.0), x_in_read) for n in range(2)]

        def load_gates(g):
            got = []
            for n, w in enumerate((A["w_rg_a"][0], A["w_rg_x"][0])):
                for a, c in PAIRS:
                    for q in range(4):
                        r0, r1 = max(q * HEAD, a * P), min((q + 1) * HEAD, (a + 1) * P)
                        c0, c1 = max(q * HEAD, c * P), min((q + 1) * HEAD, (c + 1) * P)
                        if r0 < r1 and c0 < c1:
                            t = sp.dma(lambda e, n=n, a=a, c=c, w=w, q=q, r0=r0, r1=r1, c0=c0, c1=c1: e.dma_start(
                                gate_w[n][r0 - a * P:r1 - a * P, PAIRS.index((a, c)), c0 - c * P:c1 - c * P],
                                w[4 * g + q, r0 - q * HEAD:r1 - q * HEAD, c0 - q * HEAD:c1 - q * HEAD]),
                                l_gate[n], start_gates[n], gate_read[n])
                got.append(t)
            return got

        v_got, v_read = [None] * GT, [[x_in_read]] * GT
        xb_read = [dve.op(lambda e: e.memset(xb_in[:, 0:PAD_B], 0.0), x_in_read)]

        def xb_tile(g, t):
            if g == NG:
                return
            j = g * GT + t
            evac = []

            def take(c, half, b, done, j=j, evac=evac):
                evac.append(act.op(lambda e: e.activation(xb_in[:, PAD_B + half * HALF:PAD_B + (half + 1) * HALF], b[:],
                                                          ACT.Identity, bias=C("b_in", Z_XB // P + j)), done, xb_read[0], got_par))
                return evac[-1]

            outputs(("xb", g, t), DT, P, h, h_got, take)
            for m in range(TAPS_B):
                w, src = C("conv_b_w", m * NR + j), xb_in[:, m:m + SEQ]
                if m == 0:
                    d = dve.op(lambda e, w=w, src=src, t=t, j=j: e.tensor_scalar(v[t][:], src, w, C("conv_b_b", j),
                               ALU.mult, ALU.add), evac, v_read[t])
                else:
                    d = dve.op(lambda e, w=w, src=src, t=t: e.scalar_tensor_tensor(v[t][:], src, w, v[t][:], ALU.mult,
                               ALU.add), d)
            xb_read[0], v_got[t] = d, d

        G_got, G_read, T1_read = [None] * GT, [[x_in_read]] * GT, [x_in_read]

        def gb_tiles(g, tiles):
            for t in tiles:
                j = g * GT + t
                evac = []

                def take(c, half, b, done, j=j, t=t, evac=evac):
                    evac.append(act.op(lambda e: e.activation(G[t][:, cut(half)], b[:], ACT.Identity,
                                                              bias=C("b_in", Z_GB // P + j)), done, G_read[t], got_par))
                    return evac[-1]

                outputs(("gb", g, t), DT, P, h, h_got, take)
                s = act.op(lambda e, t=t: e.activation(T1[:], G[t][:], ACT.Square), evac, T1_read[0])
                s = dve.op(lambda e: e.tensor_scalar(T1[:], T1[:], 0.044715, 1.0, ALU.mult, ALU.add), s)
                s = dve.op(lambda e, t=t: e.tensor_tensor(T1[:], T1[:], G[t][:], ALU.mult), s)
                s = act.op(lambda e: e.activation(T1[:], T1[:], ACT.Tanh, scale=0.7978845608028654), s)
                s = dve.op(lambda e, t=t: e.scalar_tensor_tensor(G[t][:], T1[:], 1.0, G[t][:], ALU.add, ALU.mult), s)
                G_got[t], T1_read[0] = s, s

        vg_got, vg_read = [[None, None] for _ in range(GT)], [x_in_read]
        v_scaled = [None] * GT
        T2_read, T3_read = [x_in_read], [x_in_read]

        got_sp4 = []

        def gate_tile(g, c, got_w):
            j = g * GT + c
            out_banks = {}
            for n in range(2):
                rows = [a for a, cc in PAIRS if cc == c]
                for half in range(2):
                    i, b, was = bank()
                    for m, a in enumerate(rows):
                        done = pe.op(lambda e, n=n, a=a, c=c, m=m, half=half, b=b, rows=rows: e.matmul(
                            b[:], gate_w[n][:, PAIRS.index((a, c)), :], v[a][:, cut(half)], start=m == 0,
                            stop=m == len(rows) - 1), was, got_w[n], v_got[a], inc=m == len(rows) - 1)
                    out_banks[n, half] = (i, b, done)
                    gate_read[n] = done
            tr, ti = [], []
            for half in range(2):
                i, b, done = out_banks[0, half]
                tr.append(act.op(lambda e, half=half, b=b, j=j: e.activation(T1[:, cut(half)], b[:], ACT.Tanh,
                          bias=CH("b_rg_a", j), scale=0.5), done, T1_read[0], got_parh))
            for half in range(2):
                i, b, done = out_banks[1, half]
                ti.append(act.op(lambda e, half=half, b=b, j=j: e.activation(T3[:, cut(half)], b[:], ACT.Tanh,
                          bias=CH("b_rg_x", j), scale=0.5), done, T3_read[0], got_parh))
                free[i] = [ti[-1]]
            a_got = act.op(lambda e, j=j: e.activation(T2[:], T1[:], ACT.Exp, scale=nsp4[:, j:j + 1], bias=nsp4[:, j:j + 1]),
                           tr, T2_read[0], got_sp4)
            th = act.op(lambda e, j=j: e.activation(T1[:], T1[:], ACT.Tanh, scale=sp4[:, j:j + 1], bias=sp4[:, j:j + 1]), a_got)
            mm = []
            for half in range(2):
                i, b, done = out_banks[0, half]
                q = dve.op(lambda e, half=half, b=b: e.tensor_tensor(b[:], T2[:, cut(half)], T2[:, cut(half)], ALU.mult),
                           a_got, tr)
                q = dve.op(lambda e, half=half, b=b: e.scalar_tensor_tensor(T1[:, cut(half)], b[:], 1.0, T1[:, cut(half)],
                           ALU.add, ALU.mult), q, th)
                free[i] = [q]
                mm.append(q)
            s = act.op(lambda e: e.activation(T1[:], T1[:], ACT.Sqrt), mm)
            s = dve.op(lambda e: e.memset(T1[:, 0:1], 1.0), s)
            q = dve.op(lambda e, c=c: e.scalar_tensor_tensor(T3[:], T3[:], 1.0, v[c][:], ALU.add, ALU.mult), ti)
            v_scaled[c] = q
            q = dve.op(lambda e: e.scalar_tensor_tensor(T3[:], T1[:], 0.5, T3[:], ALU.mult, ALU.mult), s, q)
            q = dve.op(lambda e: e.tensor_tensor_scan(T1[:], T2[:], T3[:], 0.0, ALU.mult, ALU.add), q)
            T2_read[0] = T3_read[0] = q
            q = dve.op(lambda e, c=c: e.scalar_tensor_tensor(T1[:], T1[:], 0.5, G[c][:], ALU.mult, ALU.mult), q, G_got[c])
            G_read[c] = q
            s = split_value(vg[0][c][:], vg[1][c][:], T1[:], [q], [vg_read[0]])
            vg_got[c] = [s, s]
            T1_read[0] = s

        yb_got = [[None, None] for _ in range(DT)]

        def yb_tiles(g):
            for c4 in range(4):
                def take(c, half, b, done, c4=c4):
                    j = c4 * 2 + c
                    dst = yb[j][:, cut(half)]
                    if g == 0:
                        yb_got[j][half] = dve.op(lambda e: e.tensor_copy(dst, b[:]), done)
                    else:
                        yb_got[j][half] = dve.op(lambda e: e.tensor_tensor(dst, dst, b[:], ALU.add), done, yb_got[j][half])
                    taps(2)
                    return yb_got[j][half]
                vg_read[0] = outputs(("yb", g, c4), GT, 2 * P, vg, vg_got, take)

        stage_b = []
        over_uc = [stage_b] * DT
        EDGE = [0, 4224 + 16 * 4096]
        uc = [sb(f"uc{j}", "g", 4224 + 4096 * j, [P, SEQ]) for j in range(DT)]
        sa = [sb(f"sa{j}", "g", 4224 + 4096 * (DT + j), [P, SEQ]) for j in range(DT)]
        PAD_A = TAPS_A - 1
        u_in = [sb(f"u_in{n}", "g", EDGE[n], [P, PAD_A + SEQ + 2]) for n in range(2)]
        u_read = [None, None]
        uc_got = [None] * DT

        def conv_a(j, got):
            src = u_in[j % 2]
            if j < 2:
                odd, over_odd = uc[j + GT][:], [G_read[j]]
            elif j + 2 < DT:
                odd, over_odd = sa[j + 1][:], [stage_b]
            elif j + 2 == DT:
                odd, over_odd = None, None
            else:
                odd, over_odd = u_in[(j + 1) % 2][:, 0:SEQ], [u_read[(j + 1) % 2]]
            sums, last = (uc[j][:], odd), [got, got]
            for m in range(TAPS_A):
                n = m % 2 if odd is not None else 0
                w, s, to = C("conv_a_w", m * DT + j), src[:, m:m + SEQ], sums[n]
                if m == 0:
                    d = dve.op(lambda e, w=w, s=s, to=to: e.tensor_scalar(to, s, w, C("conv_a_b", j), ALU.mult, ALU.add), last[0])
                elif m == 1 and odd is not None:
                    d = dve.op(lambda e, w=w, s=s, to=to: e.tensor_scalar(to, s, w, None, ALU.mult), last[1], over_odd)
                else:
                    d = dve.op(lambda e, w=w, s=s, to=to: e.scalar_tensor_tensor(to, s, w, to, ALU.mult, ALU.add), last[n])
                last[n] = d
                yield
            if odd is not None:
                d = dve.op(lambda e: e.tensor_tensor(uc[j][:], uc[j][:], odd, ALU.add), last)
            uc_got[j] = d
            u_read[j % 2] = [d]

        todo = []

        def taps(n):
            while n and todo:
                try:
                    next(todo[0])
                    n -= 1
                except StopIteration:
                    todo.pop(0)

        m_got = [[None, None] for _ in range(DT)]
        sa_got = [[None, None] for _ in range(DT)]

        def conv_input(j):
            n, u_half, u_got = j % 2, [], []

            def take(c, half, b, done):
                u_half.append(act.op(lambda e: e.activation(u_in[n][:, PAD_A + half * HALF:PAD_A + (half + 1) * HALF], b[:], ACT.Identity,
                                     bias=CH("b_in", Z_VA // P + j), scale=0.5), done, u_read[n], got_parh))
                return u_half[-1]
            outputs(("va", j), DT, P, h, h_got, take)

            def take(c, half, b, done):
                t = act.op(lambda e: e.activation(uc[j][:, cut(half)], b[:], ACT.Tanh, bias=CH("b_in", Z_GA // P + j), scale=0.5),
                           done, over_uc[j], got_parh)
                at = u_in[n][:, PAD_A + half * HALF:PAD_A + (half + 1) * HALF]
                u_got.append(dve.op(lambda e: e.scalar_tensor_tensor(at, uc[j][:, cut(half)], 1.0, at, ALU.add, ALU.mult), t,
                                    u_half[half]))
                return t
            outputs(("ga", j), DT, P, h, h_got, take)
            return u_got

        def mix_gates(j):
            def take(c, half, b, done):
                t = act.op(lambda e: e.activation(sa[j][:, cut(half)], b[:], ACT.Tanh, bias=CH("b_in", Z_SB // P + j), scale=0.5),
                           done, stage_b, uc_got[j - 1] if j else None)
                m_got[j][half] = dve.op(lambda e: e.scalar_tensor_tensor(yb[j][:, cut(half)], sa[j][:, cut(half)], 1.0,
                                        yb[j][:, cut(half)], ALU.add, ALU.mult), t, yb_got[j][half])
                return t
            outputs(("sb", j), DT, P, h, h_got, take)
            taps(8)

            def take(c, half, b, done):
                sa_got[j][half] = act.op(lambda e: e.activation(sa[j][:, cut(half)], b[:], ACT.Tanh, bias=CH("b_in", Z_SA // P + j),
                                         scale=0.5), done, m_got[j][half])
                return sa_got[j][half]
            last = outputs(("sa", j), DT, P, h, h_got, take)
            taps(8)
            return last

        def start_branch_a(j):
            u_read[j] = [dve.op(lambda e: e.memset(u_in[j][:, 0:PAD_A], 0.0), gate_read if j else xb_read[0])]
            over_uc[j] = [v_read[j]]
            todo.append(conv_a(j, conv_input(j)))

        for t in range(GT):
            xb_tile(0, t)

        lam = par[:, offsets["lam"]:offsets["lam"] + NR]
        la, lb, lc, ld = (small[:, 16 * n:16 * n + NR] for n in range(4))
        t = dve.op(lambda e: e.tensor_scalar(la, lam, -1.0, None, ALU.mult), got_par)
        t = dve.op(lambda e: e.tensor_tensor(lb, la, lam, ALU.min), t)
        t = act.op(lambda e: e.activation(lc, lb, ACT.Exp), t)
        t = dve.op(lambda e: e.tensor_scalar(lb, lc, 2.0, None, ALU.add), t)
        t = dve.op(lambda e: e.reciprocal(lb, lb), t)
        t = dve.op(lambda e: e.tensor_tensor(lb, lb, lc, ALU.mult), t)
        t = dve.op(lambda e: e.tensor_tensor(lc, lb, lb, ALU.mult), t)
        t = dve.op(lambda e: e.memset(ld, 1.0 / 17), t)
        for m in (15, 13, 11, 9, 7, 5, 3, 1):
            t = dve.op(lambda e: e.tensor_tensor(ld, ld, lc, ALU.mult), t)
            t = dve.op(lambda e, m=m: e.tensor_scalar(ld, ld, 1.0 / m, None, ALU.add), t)
        t = dve.op(lambda e: e.tensor_tensor(ld, ld, lb, ALU.mult), t)
        t = dve.op(lambda e: e.tensor_scalar(la, la, 0.0, None, ALU.max), t)
        t = dve.op(lambda e: e.scalar_tensor_tensor(la, ld, 2.0, la, ALU.mult, ALU.add), t)
        t = dve.op(lambda e: e.tensor_scalar(sp4[:, 0:NR], la, LRU_C / 2, None, ALU.mult), t)
        got_sp4.append(dve.op(lambda e: e.tensor_scalar(nsp4[:, 0:NR], la, -LRU_C / 2, None, ALU.mult), t))

        gb_tiles(0, [0])
        for g in range(NG):
            got_w = load_gates(g)
            gb_tiles(g, range(1, GT))
            gate_tile(g, 0, got_w)
            gate_tile(g, 1, got_w)
            v_read[0] = [v_scaled[0], gate_read]
            xb_tile(g + 1, 0)
            if g == NG - 1:
                start_branch_a(0)
            gate_tile(g, 2, got_w)
            v_read[1:] = [v_scaled[1], gate_read], [v_scaled[2], gate_read]
            xb_tile(g + 1, 1)
            xb_tile(g + 1, 2)
            if g == NG - 1:
                start_branch_a(1)
            else:
                gb_tiles(g + 1, [0])
            yb_tiles(g)

        stage_b.extend([(dve.sem, dve.count), (act.sem, act.count), (pe.sem, pe.count)])
        for j in range(1, DT + LAG):
            if 2 <= j < DT:
                while uc_got[j - 2] is None:
                    taps(1)
                if GT <= j < GT + 2:
                    over_uc[j] = [stage_b, uc_got[j - GT]]
                todo.append(conv_a(j, conv_input(j)))
                taps(8)
            if j >= LAG:
                h_last = mix_gates(j - LAG)
        while todo:
            taps(1)
        split_ahead()

        def add_sums(j, half, data, waits):
            return sum_into(sum_banks[half], j, data, [waits, sum_free[half] if j == 0 else None])

        def sum_into(b, j, data, waits):
            return pe.op(lambda e: e.matmul(b[:], ones_sq[:], data, start=j == 0, stop=j == DT - 1, skip_group_check=True), waits,
                         got_ones)

        def spread_rms(half, dst, waits):
            t = dve.op(lambda e: e.tensor_scalar(dst, sum_banks[half][:], 1.0 / D, EPS, ALU.mult, ALU.add), waits)
            sum_free[half] = [t]
            t = act.op(lambda e: e.activation(dst, dst, ACT.Sqrt), t)
            return dve.op(lambda e: e.reciprocal(dst, dst), t)

        def spread(column, waits, half):
            i, b, was = bank()
            for q in range(4):
                t = half * 4 + q
                done = pe.op(lambda e, t=t, q=q: e.matmul(b[:, q * P:(q + 1) * P], stat[:, column + t:column + t + 1].broadcast_to([P, P]),
                             ident[:], start=True, stop=True), waits, was, inc=q == 3)
            return i, b, done

        eager[0] = False
        set_ring(6)
        centred = [[None, None] for _ in range(DT)]
        means = [bank(), bank()]
        for j in range(DT):
            summed = [sum_into(means[half][1], j, uc[j][:, cut(half)], [uc_got[j], means[half][2]]) for half in range(2)]
        for j in range(DT):
            for half in range(2):
                i, b, was = means[half]
                centred[j][half] = dve.op(lambda e, j=j, half=half, b=b: e.scalar_tensor_tensor(uc[j][:, cut(half)], b[:], -1.0 / D,
                                          uc[j][:, cut(half)], ALU.mult, ALU.add), summed[half])
                free[i] = [centred[j][half]]
        sq = [sb(f"sq{n}", "g", EDGE[n // 2] + 2048 * (n % 2), [P, HALF]) for n in range(4)]
        sq_read = [uc_got] * 4
        for j in range(DT):
            for half in range(2):
                n = (2 * j + half) % 4
                s = act.op(lambda e, j=j, n=n, half=half: e.activation(sq[n][:], uc[j][:, cut(half)], ACT.Square), centred[j][half],
                           sq_read[n])
                sq_read[n] = add_sums(j, half, sq[n][:], s)
                summed[half] = sq_read[n]
        un = pair("un", "h", 0, DT)
        un_got = [[None, None] for _ in range(DT)]
        lnt = [sb(f"lnt{n}", "g", EDGE[0] + 2048 * n, [P, HALF]) for n in range(2)]
        ln_r = [sb(f"ln_r{half}", "g", EDGE[1] + 2048 * half, [P, HALF]) for half in range(2)]
        lnt_read = [sq_read] * 2
        for half in range(2):
            r_got = spread_rms(half, ln_r[half][:], [summed[half], sq_read])
            z_got, s_got = [None] * DT, [None] * DT
            for j in range(DT):
                z_got[j] = dve.op(lambda e, j=j, half=half: e.scalar_tensor_tensor(uc[j][:, cut(half)], uc[j][:, cut(half)],
                                  C("ln_g", j), ln_r[half][:], ALU.mult, ALU.mult), r_got, sq_read)
            for j in range(DT + 1):
                if j < DT:
                    n = j % 2
                    t = act.op(lambda e, j=j, n=n, half=half: e.activation(lnt[n][:], uc[j][:, cut(half)], ACT.Tanh, bias=CH("ln_b", j),
                               scale=0.5), z_got[j], lnt_read[n])
                    z = act.op(lambda e, j=j, half=half: e.activation(uc[j][:, cut(half)], uc[j][:, cut(half)], ACT.Identity,
                               bias=CH("ln_b", j), scale=0.5), t)
                    s_got[j] = dve.op(lambda e, j=j, n=n, half=half: e.scalar_tensor_tensor(uc[j][:, cut(half)], lnt[n][:], 1.0,
                                      uc[j][:, cut(half)], ALU.add, ALU.mult), z)
                    lnt_read[n] = [s_got[j]]
                if j:
                    un_got[j - 1][half] = split_value(un[0][j - 1][:, cut(half)], un[1][j - 1][:, cut(half)], uc[j - 1][:, cut(half)],
                                                      [s_got[j - 1]], [h_last])

        mx = pair("mx", "g", 0, DT)
        mx_got = [[None, None] for _ in range(DT)]
        uc_done = [un_got[j][half] for j in range(DT) for half in range(2)]
        gated = []

        def mix(j, half, b, done):
            s = dve.op(lambda e: e.scalar_tensor_tensor(sa[j][:, cut(half)], sa[j][:, cut(half)], 1.0, b[:], ALU.add, ALU.mult), done,
                       sa_got[j][half])
            s2 = dve.op(lambda e: e.tensor_tensor(yb[j][:, cut(half)], yb[j][:, cut(half)], sa[j][:, cut(half)], ALU.add), s,
                        m_got[j][half])
            gated.append(s2)
            mixed[j][half] = s2
            return s

        def split_mix(j):
            t = act.op(lambda e: e.activation(mx[0][j][:], yb[j][:], ACT.Copy, scale=0.5), mixed[j], gated, uc_done)
            t = [t, dve.op(lambda e: e.scalar_tensor_tensor(mx[1][j][:], yb[j][:], 0.5, mx[0][j][:].bitcast(F32), ALU.mult,
                                                            ALU.subtract), t)]
            mx_got[j] = [t, t]

        mixed = [[None, None] for _ in range(DT)]
        outputs_by_half([("ya", j) for j in range(3)], DT, un, un_got, mix)
        for j in range(3):
            split_mix(j)
        for j in range(3, DT):
            un_last = outputs(("ya", j), DT, P, un, un_got, lambda c, half, b, done, j=j: mix(j, half, b, done))
            split_mix(j)

        x1 = [sb(f"x1_{j}", "y", 4096 * j, [P, SEQ]) for j in range(DT)]
        x1_got = [[None, None] for _ in range(DT)]
        xcols = [sb(f"xcols{n}", "g", 64 * KB + 2048 * n, [P, NT // 2, P]) for n in range(2)]
        l_xc = [landing(f"xc{n}") for n in range(2)]
        xc_read = [gated, gated]
        squares = [sb(f"squares{n}", "g", 68 * KB + 2048 * n, [P, HALF]) for n in range(2)]
        squares_read, squares_got = [gated, gated], [None, None]

        h2 = pair("h2", "h", 0, DT)
        h2_got = [[None, None] for _ in range(DT)]
        for j in range(DT):
            (hi, lo, wgot), slot = weights(("wo", j))
            for half in range(2):
                n = half
                got = sp.dma(lambda e, n=n, j=j, half=half: e.dma_start(xcols[n][:], x_rows[:, half * 4:half * 4 + 4, j * P:(j + 1) * P]),
                             l_xc[n], xc_read[n], uc_done)
                i, b, was = bank()
                terms = [(hi[:, k, :], lo[:, k, :], mx[0][k][:, cut(half)], mx[1][k][:, cut(half)], mx_got[k][half])
                         for k in range(DT)]
                split_free[slot] = product(b[:], terms, [was, wgot], stop=False)
                for q in range(4):
                    done = pe.op(lambda e, q=q, b=b, n=n: e.matmul(b[:, q * P:(q + 1) * P], xcols[n][:, q, :],
                                 ident[:], start=False, stop=q == 3, skip_group_check=True), got, inc=q == 3)
                xc_read[n] = done
                x1_got[j][half] = act.op(lambda e, b=b, j=j, half=half: e.activation(x1[j][:, cut(half)], b[:], ACT.Copy), done, mx_got[j])
                free[i] = [x1_got[j][half]]
                h2_got[j][half] = evacuate_split(h2[0][j][:, cut(half)], h2[1][j][:, cut(half)], x1[j][:, cut(half)], C("g_mlp", j),
                                                 [x1_got[j][half], un_last])
                if j:
                    squares_read[half] = add_sums(j - 1, half, squares[half][:], squares_got[half])
                squares_got[half] = act.op(lambda e, j=j, half=half: e.activation(squares[half][:], x1[j][:, cut(half)], ACT.Square),
                                           x1_got[j][half], squares_read[half])
        mx_last = done
        factor = sb("factor", "g", 64 * KB, [P, SEQ])
        tmp = [sb(f"tmp{n}", "g", 68 * KB + 2048 * n, [P, HALF]) for n in range(2)]
        tmp_read, turns, factor_got = [None, None], [0], [None, None]

        def temporary():
            n = turns[0] % len(tmp)
            turns[0] += 1
            return n, tmp[n], tmp_read[n]

        def find_factor():
            for half in range(2):
                squares_read[half] = add_sums(DT - 1, half, squares[half][:], squares_got[half])
                factor_got[half] = spread_rms(half, factor[:, cut(half)], [squares_read[half], xc_read])
            tmp_read[:] = squares_read

        def scaled(hl, got, source, source_got, column, gain, r, over):
            held = [spread(column, r, half) for half in range(2)]
            for half, (i, b, done) in enumerate(held):
                for j in range(DT):
                    if j % 4 == 0:
                        yield
                    n, tt, was = temporary()
                    z = dve.op(lambda e, j=j, tt=tt, b=b, half=half: e.scalar_tensor_tensor(tt[:], source[j][:, cut(half)], gain(j), b[:],
                               ALU.mult, ALU.mult), done, was, source_got[j][half])
                    got[j][half] = split_value(hl[0][j][:, cut(half)], hl[1][j][:, cut(half)], tt[:], [z], over)
                    tmp_read[n] = got[j][half]
                free[i] = [z]

        ff = pair("ff", "g", 0, DT)
        ff_got = [[None, None] for _ in range(DT)]
        ff_read = [mx_last]
        GG, GF2 = small[:, 64:72], gcol[:, :].rearrange("p (j n) -> p j n", n=2)
        g_final, norm_g = (par[:, offsets[n]:offsets[n] + DT] for n in ("g_final", "norm_g_2"))
        t = dve.op(lambda e: e.memset(gcol[:], 1.0))
        gf_got = dve.op(lambda e: e.tensor_tensor(GF2[:, :, 1], g_final, g_final, ALU.mult), t)
        gg_got = dve.op(lambda e: e.tensor_tensor(GG, g_final, norm_g, ALU.mult), got_par)
        NM = N_MEM // P
        mem_in = sb("mem_in", "h", 0, [P, NM, D])
        mem_sq = sb("mem_sq", "h", 8 * KB, [P, D])
        mn = pair("mn", "g", 8 * KB, DT, N_MEM)
        km = sb("km", "g", 0, [P, NH, N_MEM])
        vm = sb("vm", "g", 4 * KB, [P, NM, GROUP])
        l_mem = landing("mem")
        sqm = [sb(f"sqm{n}", "h", 32 * KB + 4096 * n, [P, SEQ]) for n in range(2)]
        sqm_read = [None, None]
        w_in2, w_kv, w_out2 = A["w_in_2"][0], A["w_mem_kv_2"][0], A["w_out_2"][0]
        for c in range(2 * GROUP // P):
            need(("kv", c), w_kv, 0, DT, c * P, P)
        gate_cols = lambda c: w_in2[:, c:c + NH].rearrange("(k p) c -> p k c", p=P)
        plan.append((("gates",), [((0, NH), gate_cols(Y_G)), ((32, 32 + NH), gate_cols(Y_G + NH))], DT, P, True))
        for g in range(NH):
            need(("u", g), w_in2, 0, DT, Y_U + g * P, P)
            need(("zb", g), w_in2, 0, DT, Y_ZB + g * P, P)
            need(("pw", g), A["pool_w_2"][0, g], 0, 1, 0, P)
        for c in range(4):
            need(("ob", c), w_out2, GROUP, NH, c * 2 * P, 2 * P)
        for g in range(NH):
            need(("qc", g), w_in2, 0, DT, Y_QC + g * P, P)
            need(("zc", g), w_in2, 0, DT, Y_ZC + g * P, P)
        for c in range(4):
            need(("oc", c), w_out2, 2 * GROUP, NH, c * 2 * P, 2 * P)
        for j in range(2 * NH):
            need(("qk", j), w_in2, 0, DT, Y_QK + j * P, P)
        for g in range(NH):
            need(("v", g), w_in2, 0, DT, Y_V + g * P, P)
        for g in range(NH):
            need(("o", g), w_in2, 0, DT, Y_O + g * P, P)
        for g in range(NH):
            need(("za", g), w_in2, 0, DT, Y_ZA + g * P, P)
        for c in range(3):
            need(("oa", c), w_out2, 0, NH, c * 2 * P, 2 * P)

        def stat_tile(j, n_last, rhs, width, buffer, over, got):
            s = act.op(lambda e: e.activation(buffer[:], x1[j][:], ACT.Square), got, over)
            for t in range(NT):
                done = pe.op(lambda e, t=t: e.matmul(stat_bank[:, width * t:width * (t + 1)], buffer[:, t * P:(t + 1) * P], rhs,
                             start=j == 0 and t == 0, stop=j == n_last, skip_group_check=True), s,
                             sum_free[1] if j == 0 else [], gf_got, inc=t == NT - 1)
            return done

        def inner(j, half, b, done):
            n, tt, was = temporary()
            z = dve.op(lambda e: e.scalar_tensor_tensor(tt[:], b[:], 0.0, factor[:, cut(half)], ALU.max, ALU.mult), done, was,
                       factor_got[half])
            z2 = act.op(lambda e: e.activation(tt[:], tt[:], ACT.Square), z)
            ff_got[j][half] = split_value(ff[0][j][:, cut(half)], ff[1][j][:, cut(half)], tt[:], [z2], [ff_read[0]])
            tmp_read[n] = ff_got[j][half]
            return z

        for f in range(FC):
            for j in range(DT):
                if (f, j) == (0, 0):
                    first, held = turn[0], []
                    outputs(("w1", f, j), DT, P, h2, h2_got, lambda c, half, b, done: held.append((half, b, done)))
                    find_factor()
                    for half, b, done in held:
                        free[(first + half) % ring[0]] = [inner(j, half, b, done)]
                else:
                    h2_last = outputs(("w1", f, j), DT, P, h2, h2_got, lambda c, half, b, done, j=j: inner(j, half, b, done))
            if f == FC - 1:
                mem_got = sp.dma(lambda e: e.dma_start(mem_in[:], A["mem_2"][0].rearrange("(t p) d -> p t d", p=P)), l_mem, h2_last)
            for j in range(DT):
                def take(c, half, b, done, j=j):
                    x1_got[j][half] = dve.op(lambda e: e.tensor_tensor(x1[j][:, cut(half)], x1[j][:, cut(half)], b[:], ALU.add), done,
                                             x1_got[j][half])
                    return x1_got[j][half]
                last = outputs(("w2", f, j), DT, P, ff, ff_got, take)
                if f == FC - 1 and j:
                    sqm_read[(j - 1) % 2] = stat_tile(j - 1, DT - 1, GF2[:, j - 1, :], 2, sqm[(j - 1) % 2], [sqm_read[(j - 1) % 2], h2_last],
                                                      x1_got[j - 1])
                if f == FC - 1 and j in (1, 2):
                    t = j - 1
                    s = act.op(lambda e, t=t: e.activation(mem_sq[:], mem_in[:, t, :], ACT.Square, accum_out=stat[:, 16 + t:17 + t]),
                               mem_got, (act.sem, act.count), h2_last)
                    r = rstd_of(slice(16 + t, 17 + t), 1.0 / D, s)
                    mem_normed = dve.op(lambda e, t=t: e.tensor_scalar(mem_in[:, t, :], mem_in[:, t, :], stat[:, 16 + t:17 + t], None,
                                                                       ALU.mult), r)
            ff_read[0] = last
        ff_last = last

        tmp[:] = [sb(f"tmp_2_{n}", "g", 64 * KB + 2048 * n, [P, HALF]) for n in range(4)]
        tmp_read[:] = [[ff_last, ff_got]] * 4
        mn_got = [[None, None] for _ in range(DT)]
        for j in range(0, DT, 2):
            i, b, was = bank()
            for q in range(4):
                turned = done = pe.op(lambda e, q=q, j=j, b=b: e.transpose(b[:, q * P:(q + 1) * P], mem_in[:, q % 2, (j + q // 2) * P:(j + q // 2 + 1) * P],
                             ident[:]), mem_normed, was, inc=q == 3)
            for q in range(2):
                was = evacuate_split(mn[0][j + q][:], mn[1][j + q][:], b[:, q * N_MEM:(q + 1) * N_MEM], C("mem_norm_g_2", j + q),
                                     [done, was if q else None, ff_last])
                mn_got[j + q] = [was, was]
            free[i] = [mn_got[j], mn_got[j + 1]]
        h3 = pair("h3", "h", 0, DT)
        h3_got = [[None, None] for _ in range(DT)]

        km_got = [None] * NH
        vm_got = []
        for c in range(2 * NH):
            if c == 1:
                done = stat_tile(DT - 1, DT - 1, GF2[:, DT - 1, :], 2, sqm[(DT - 1) % 2], [sqm_read[(DT - 1) % 2]], x1_got[DT - 1])
                sums = stat_bank[:, 0:2 * NT].rearrange("p (t n) -> p t n", n=2)
                mem_last = [done, turned]
                t = dve.op(lambda e: e.tensor_copy(stat[:, 0:NT], sums[:, :, 0]), done)
                t2 = dve.op(lambda e: e.tensor_copy(stat[:, 8:16], sums[:, :, 1]), done)
                sum_free[1] = [t, t2]
                set_ring(8)
                r1 = rstd_of(slice(0, 8), 1.0 / D, t)
                t = dve.op(lambda e: e.tensor_tensor(small[:, 72:80], stat[:, 0:8], stat[:, 0:8], ALU.mult), r1)
                t = dve.op(lambda e: e.tensor_tensor(stat[:, 8:16], stat[:, 8:16], small[:, 72:80], ALU.mult), t)
                r2 = rstd_of(slice(8, 16), 1.0 / D, t)
                r12 = dve.op(lambda e: e.tensor_tensor(stat[:, 8:16], stat[:, 8:16], stat[:, 0:8], ALU.mult), r2)

            if c >= NH:
                if c == NH:
                    scaling = scaled(h3, h3_got, x1, x1_got, 8, lambda j: GG[:, j:j + 1], [r12, gg_got], mem_last)
                    next(scaling)
                next(scaling, None)
            (hi, lo, wgot), slot = weights(("kv", c))
            i, b, was = bank()
            if c < NH:
                terms = [(hi[:, k, :], lo[:, k, :], mn[0][k][:], mn[1][k][:], mn_got[k]) for k in range(DT)]
                split_free[slot] = done = product(b[:, 0:N_MEM], terms, [was, wgot])
                km_got[c] = act.op(lambda e, c=c, b=b: e.activation(km[:, c, :], b[:, 0:N_MEM], ACT.Copy), done, ff_last)
                free[i] = [km_got[c]]
            else:
                for q in range(NM):
                    terms = [(mn[0][k][:, q * P:(q + 1) * P], mn[1][k][:, q * P:(q + 1) * P], hi[:, k, :], lo[:, k, :], mn_got[k])
                             for k in range(DT)]
                    split_free[slot] = done = product(b[:, q * P:(q + 1) * P], terms, [was, wgot])
                t = act.op(lambda e, c=c, b=b: e.activation(vm[:, :, (c - NH) * P:(c - NH + 1) * P],
                           b[:, 0:NM * P].rearrange("p (q d) -> p q d", q=NM), ACT.Copy), done, ff_last)
                vm_got.append(t)
                free[i] = [t]

        kv_last = done
        y1, y1_got = x1, [[None, None] for _ in range(DT)]
        for half in range(2):
            i, b, done = spread(0, r1, half)
            for j in range(DT):
                y1_got[j][half] = dve.op(lambda e, j=j, b=b, half=half: e.scalar_tensor_tensor(y1[j][:, cut(half)], x1[j][:, cut(half)],
                                         C("g_final", j), b[:], ALU.mult, ALU.mult), done, h3_got[j][half])
            free[i] = [y1_got[DT - 1][half]]

        row = [sb(f"row{n}", "g", (8 + 17 + 8) * KB + 4096 * n, [P, SEQ]) for n in range(5)]
        bias = small[:, 80:82]
        l_bias = landing("bias")
        bias_got = sp.dma(lambda e: e.dma_start(bias[0:NH, 0:1], A["b_gates_2"][:, 0:NH].rearrange("l n -> n l")), l_bias)
        bias_got = sp.dma(lambda e: e.dma_start(bias[32:32 + NH, 0:1], A["b_gates_2"][:, NH:2 * NH].rearrange("l n -> n l")), l_bias)
        gate_evac = []

        def take(c, half, b, done):
            a = act.op(lambda e: e.activation(row[0][0:NH, cut(half)], b[0:NH, :], ACT.Identity, bias=bias[0:NH, 0:1]), done, bias_got,
                       ff_last)
            f = act.op(lambda e: e.activation(row[1][32:32 + NH, cut(half)], b[32:32 + NH, :], ACT.Identity, bias=bias[32:32 + NH, 0:1]),
                       done, bias_got)
            gate_evac.extend([a, f])
            return [a, f]
        outputs(("gates",), DT, P, h3, h3_got, take)
        R = lambda n: row[n][0:NH, :]
        chunks = lambda n: row[n][0:NH, :].rearrange("p (c t) -> p c t", t=P)
        t = act.op(lambda e: e.activation(R(2), row[1][32:32 + NH, :], ACT.Copy), gate_evac)
        f_got = t
        t = dve.op(lambda e: e.scalar_tensor_tensor(R(3), R(2), -1.0, R(2), ALU.mult, ALU.min), t)
        t = act.op(lambda e: e.activation(R(3), R(3), ACT.Exp), t)
        t = act.op(lambda e: e.activation(R(3), R(3), ACT.Ln, bias=1.0), t)
        t = dve.op(lambda e: e.scalar_tensor_tensor(R(2), R(2), 0.0, R(3), ALU.min, ALU.subtract), t)
        u = dve.op(lambda e: e.memset(R(4), 1.0), ff_last)
        u = dve.op(lambda e: e.memset(chunks(4)[:, :, 0:1], 0.0), u)
        t = dve.op(lambda e: e.tensor_tensor_scan(R(3), R(4), R(2), 0.0, ALU.mult, ALU.add), t, u)
        x_got = dve.op(lambda e: e.tensor_tensor(R(0), R(0), R(3), ALU.subtract), t, gate_evac)
        u = dve.op(lambda e: e.memset(R(4), BIG), t)
        u = dve.op(lambda e: e.memset(chunks(4)[:, :, 0:1], -BIG), u)
        t = dve.op(lambda e: e.tensor_tensor_scan(R(2), R(4), R(0), -BIG, ALU.min, ALU.max), x_got, u)
        mm4, mp4 = small[0:NH, 84:92], small[0:NH, 92:100]
        t = dve.op(lambda e: e.tensor_tensor_scan(mm4, chunks(2)[:, :, P - 1], chunks(3)[:, :, P - 1], 0.0, ALU.max, ALU.add), t)
        u = dve.op(lambda e: e.memset(mp4, 0.0))
        t = dve.op(lambda e: e.tensor_copy(mp4[:, 1:NT], mm4[:, 0:NT - 1]), t, u)
        m_row = dve.op(lambda e: e.tensor_tensor(chunks(1), chunks(2), mp4.unsqueeze(2).broadcast_to([NH, NT, P]), ALU.max), t, f_got)
        nb_row = dve.op(lambda e: e.scalar_tensor_tensor(R(4), R(3), -1.0, R(1), ALU.mult, ALU.subtract), m_row)
        rows_dram = nc.dram_tensor("rows_dram", (2, NH, SEQ), F32).ap()
        mp_dram = nc.dram_tensor("mp_dram", (NH, NT), F32).ap()
        sz_dram = nc.dram_tensor("sz_dram", (NH, P, SEQ), F32).ap()
        l_rowout, l_mp = landing("rowout"), landing("mp")
        rows_out = [sp.dma(lambda e: e.dma_start(rows_dram[0], R(1)), l_rowout, m_row),
                    sp.dma(lambda e: e.dma_start(rows_dram[1], R(4)), l_rowout, nb_row),
                    sp.dma(lambda e: e.dma_start(mp_dram, mp4), l_rowout, m_row)][-1]
        mp_got = sp.dma(lambda e: e.dma_start(mprev[:].rearrange("p (h c) -> p h c", h=NH), mp_dram.partition_broadcast(P)), l_mp, rows_out)

        def silu2(dst, b, done, over, scratch, scratch_read):
            t = act.op(lambda e: e.activation(scratch, b, ACT.Tanh, scale=0.5), done, scratch_read)
            return dve.op(lambda e: e.scalar_tensor_tensor(dst, scratch, 1.0, b, ALU.add, ALU.mult), t, over)

        def add_outputs(key, hl, got):
            for c4 in range(4):
                def take(c, half, b, done, c4=c4):
                    j = c4 * 2 + c
                    y1_got[j][half] = dve.op(lambda e: e.tensor_tensor(y1[j][:, cut(half)], y1[j][:, cut(half)], b[:], ALU.add), done,
                                             y1_got[j][half])
                    return y1_got[j][half]
                last = outputs((key, c4), NH, 2 * P, hl, got, take)
            return last

        PAD_U = 16
        uw = [sb(f"uw{n}", "g", 8 * KB + 4224 * n, [P, PAD_U + SEQ]) for n in range(3)]
        zb = sb("zb", "g", 8 * KB + 4224 * 3, [P, SEQ])
        yp = pair("yp", "g", 25 * KB, NH)
        l_rcnt = landing("rcnt")
        rcnt_got = sp.dma(lambda e: e.dma_start(rcnt[:], A["rcnt"]), l_rcnt)
        yp_got = [[None, None] for _ in range(NH)]
        uw_read = [dve.op(lambda e, n=n: e.memset(uw[n][:, 0:PAD_U], 0.0), kv_last) for n in range(3)]
        zb_read = [kv_last]
        for g, window in enumerate(WINDOWS):
            evac = []

            def take(c, half, b, done):
                evac.append(act.op(lambda e: e.activation(uw[0][:, PAD_U + half * HALF:PAD_U + (half + 1) * HALF], b[:], ACT.Copy), done,
                                   uw_read))
                return evac[-1]
            outputs(("u", g), DT, P, h3, h3_got, take)
            if g == 0:
                i, b, was = bank()
                for c in range(NT):
                    done = pe.op(lambda e, c=c, b=b: e.transpose(b[:, c * NH:(c + 1) * NH], row[0][0:NH, c * P:(c + 1) * P],
                                 ident[0:NH, 0:NH]), x_got, was, inc=c == NT - 1)
                xcol_got = dve.op(lambda e, b=b: e.tensor_copy(xcol[:], b[:, 0:NH * NT]), done)
                free[i] = [xcol_got]
                rows_read = [xcol_got, rows_out, nb_row]
            src, step, at = 0, 1, 1
            t = evac
            while step < window:
                dst = 1 if src != 1 else 2
                t = dve.op(lambda e, src=src, dst=dst, step=step, at=at: e.tensor_tensor(uw[dst][:, at:], uw[src][:, at:],
                           uw[src][:, at - step:PAD_U + SEQ - step], ALU.add), t, uw_read)
                src, step = dst, step * 2
                at += step
            t = dve.op(lambda e, src=src, g=g, w=window: e.tensor_tensor(uw[src][:, PAD_U:PAD_U + w], uw[src][:, PAD_U:PAD_U + w],
                       rcnt[:, 16 * g:16 * g + w], ALU.mult), t, rcnt_got)
            t = dve.op(lambda e, src=src, w=window: e.scalar_tensor_tensor(uw[src][:, PAD_U:], uw[src][:, PAD_U:], 1.0 / w,
                       uw[0][:, PAD_U:], ALU.mult, ALU.subtract), t)
            s = split_value(yp[0][g][:], yp[1][g][:], uw[src][:, PAD_U:], [t], [rows_read, ff_last])
            uw_read = s

            def take(c, half, b, done):
                n, tt, was = temporary()
                t = silu2(zb[:, cut(half)], b[:], done, zb_read, tt[:], was)
                tmp_read[n] = t
                zb_got.append(t)
                return t
            zb_got = []
            outputs(("zb", g), DT, P, h3, h3_got, take)
            (hi, lo, wgot), slot = weights(("pw", g))
            held = []
            for half in range(2):
                i, b, was = bank()
                done = product(b[:], [(hi[:, 0, :], lo[:, 0, :], yp[0][g][:, cut(half)], yp[1][g][:, cut(half)], s)], [was, wgot])
                held.append((i, b, done))
            split_free[slot] = done
            zb_read = []
            for half, (i, b, done) in enumerate(held):
                n, tt, was = temporary()
                t = dve.op(lambda e, g=g, tt=tt, b=b, half=half: e.scalar_tensor_tensor(tt[:], b[:], CH("pool_scale_2", g), zb[:, cut(half)],
                           ALU.mult, ALU.mult), done, was, zb_got)
                free[i] = [t]
                zb_read.append(t)
                yp_got[g][half] = split_value(yp[0][g][:, cut(half)], yp[1][g][:, cut(half)], tt[:], [t], [done])
                tmp_read[n] = yp_got[g][half]
        yp_last = add_outputs("ob", yp, yp_got)

        qc = sb("qc", "g", 8 * KB, [P, SEQ])
        zc = sb("zc", "g", 12 * KB, [P, SEQ])
        pr = [sb(f"pr{n}", "g", 16 * KB + 2048 * n, [P, 2, N_MEM]) for n in range(NT // 2)]
        pt = sb("pt", "g", 24 * KB, [P, NM, SEQ])
        yc = pair("yc", "g", 32 * KB, NH)
        yc_got = [[None, None] for _ in range(NH)]
        SCALE = float(HD) ** -0.5
        qc_read = zc_read = pt_read = [uw_read, zb_read]
        pr_read, pr_got = [[uw_read, zb_read]] * (NT // 2), [None] * (NT // 2)
        for g in range(NH):
            q_got = []

            def take(c, half, b, done):
                q_got.append(act.op(lambda e: e.activation(qc[:, cut(half)], b[:], ACT.Copy), done, qc_read))
                return q_got[-1]
            outputs(("qc", g), DT, P, h3, h3_got, take)
            for tp in range(NT // 2):
                i, b, was = bank()
                for q in range(2):
                    done = pe.op(lambda e, q=q, tp=tp, g=g, b=b: e.matmul(b[:, q * N_MEM:(q + 1) * N_MEM], qc[:, (2 * tp + q) * P:(2 * tp + q + 1) * P],
                                 km[:, g, :], start=True, stop=True), was, q_got, km_got[g], inc=q == 1)
                scores = b[:].rearrange("p (q m) -> p q m", q=2)
                top, total = small[:, 100 + 4 * tp:102 + 4 * tp], small[:, 102 + 4 * tp:104 + 4 * tp]
                t = dve.op(lambda e, s=scores, top=top: e.tensor_reduce(top, s, mybir.AxisListType.X, ALU.max), done, pr_read[tp])
                t = dve.op(lambda e, top=top: e.tensor_scalar(top, top, -SCALE, None, ALU.mult), t)
                for q in range(2):
                    t2 = act.op(lambda e, q=q, tp=tp, s=scores, top=top, total=total: e.activation(pr[tp][:, q, :], s[:, q, :], ACT.Exp,
                                bias=top[:, q:q + 1], scale=SCALE, accum_out=total[:, q:q + 1]), t, pr_read[tp])
                free[i] = [t2]
                t = dve.op(lambda e, total=total: e.reciprocal(total, total), t2)
                for q in range(2):
                    t = dve.op(lambda e, q=q, tp=tp, total=total: e.tensor_scalar(pr[tp][:, q, :], pr[tp][:, q, :], total[:, q:q + 1], None,
                                                                                ALU.mult), t, t2)
                pr_got[tp] = t
            qc_read = done
            zc_got, pt_got = [], []

            def take(c, half, b, done):
                n, tt, was = temporary()
                zc_got.append(silu2(zc[:, cut(half)], b[:], done, zc_read, tt[:], was))
                tmp_read[n] = zc_got[-1]
                return zc_got[-1]
            outputs(("zc", g), DT, P, h3, h3_got, take)
            for tp in range(NT // 2):
                i, b, was = bank()
                for mt in range(NM):
                    for q in range(2):
                        done = pe.op(lambda e, mt=mt, q=q, tp=tp, b=b: e.transpose(b[:, (mt * 2 + q) * P:(mt * 2 + q + 1) * P],
                                     pr[tp][:, q, mt * P:(mt + 1) * P], ident[:]), was, pr_got[tp], inc=(mt, q) == (NM - 1, 1))
                pr_read[tp] = done
                pt_got.append(act.op(lambda e, b=b, tp=tp: e.activation(pt[:, :, tp * 2 * P:(tp + 1) * 2 * P],
                              b[:].rearrange("p (m t) -> p m t", m=NM), ACT.Copy), done, pt_read))
                free[i] = [pt_got[-1]]
            zc_read = []
            for half in range(2):
                i, b, was = bank()
                for mt in range(NM):
                    done = pe.op(lambda e, mt=mt, g=g, b=b, half=half: e.matmul(b[:], vm[:, mt, g * P:(g + 1) * P], pt[:, mt, cut(half)],
                                 start=mt == 0, stop=mt == NM - 1), was, pt_got, vm_got, inc=mt == NM - 1)
                n, tt, was = temporary()
                t = dve.op(lambda e, tt=tt, b=b, half=half: e.scalar_tensor_tensor(tt[:], b[:], 0.5, zc[:, cut(half)], ALU.mult, ALU.mult),
                           done, was, zc_got)
                free[i] = [t]
                zc_read.append(t)
                yc_got[g][half] = split_value(yc[0][g][:, cut(half)], yc[1][g][:, cut(half)], tt[:], [t], [yp_last])
                tmp_read[n] = yc_got[g][half]
            pt_read = done
        yc_last = add_outputs("oc", yc, yc_got)

        q_all = sb("q_all", "g", 0, [P, NH, SEQ])
        k_all = sb("k_all", "g", 16 * KB, [P, NH, SEQ])
        v_tok = sb("v_tok", "g", 32 * KB, [P, NT, NH, P])
        o_all = sb("o_all", "g", 48 * KB, [P, NH, SEQ])
        work = [sb(f"work{n}", "g", 64 * KB + 4224 * n, [P, SEQ + 8]) for n in range(2)]
        before = [yc_last, pt_read, zc_read, yc_got[NH - 1], tmp_read]
        PAD_C = TAPS_C - 1
        work_read = [[dve.op(lambda e, n=n: e.memset(work[n][:, 0:PAD_C], 0.0), before)] for n in range(2)]
        q_got, k_got = [None] * NH, [None] * NH
        for j in range(2 * NH):
            dst = (q_all if j < NH else k_all)[:, j % NH, :]
            evac, w0 = [], work[0]

            def take(c, half, b, done, w0=w0):
                evac.append(act.op(lambda e: e.activation(w0[:, PAD_C + half * HALF:PAD_C + (half + 1) * HALF], b[:], ACT.Copy), done,
                                   work_read[0]))
                return evac[-1]
            outputs(("qk", j), DT, P, h3, h3_got, take)
            t = evac
            for m in range(TAPS_C):
                w, s = CH("conv_w_2", m * 2 * NH + j), w0[:, m:m + SEQ]
                if m == 0:
                    t = dve.op(lambda e, w=w, s=s, j=j, dst=dst: e.tensor_scalar(dst, s, w, CH("conv_b_2", j), ALU.mult, ALU.add), t, before)
                else:
                    t = dve.op(lambda e, w=w, s=s, dst=dst: e.scalar_tensor_tensor(dst, s, w, dst, ALU.mult, ALU.add), t)
            work_read[0] = [t]
            s = act.op(lambda e, dst=dst: e.activation(work[1][:, PAD_C:PAD_C + SEQ], dst, ACT.Tanh), t, work_read[1])
            t = dve.op(lambda e, dst=dst: e.scalar_tensor_tensor(dst, work[1][:, PAD_C:PAD_C + SEQ], 1.0, dst, ALU.add, ALU.mult), s)
            work_read[1] = [t]
            if j >= NH:
                t = dve.op(lambda e, dst=dst: e.tensor_scalar(dst, dst, SCALE, None, ALU.mult), t)
            (q_got if j < NH else k_got)[j % NH] = t
        v_got = []
        for g in range(NH):
            w0, evac, n = work[g % 2], [], g % 2

            def take(c, half, b, done, w0=w0):
                evac.append(act.op(lambda e: e.activation(w0[:, cut(half)], b[:], ACT.Copy), done, work_read[n]))
                return evac[-1]
            outputs(("v", g), DT, P, h3, h3_got, take)
            for half in range(2):
                i, b, was = bank()
                for q in range(4):
                    done = pe.op(lambda e, q=q, b=b, w0=w0, half=half: e.transpose(b[:, q * P:(q + 1) * P],
                                 w0[:, (half * 4 + q) * P:(half * 4 + q + 1) * P], ident[:]), was, evac, inc=q == 3)
                v_got.append(dve.op(lambda e, b=b, g=g, half=half: e.tensor_copy(v_tok[:, half * 4:half * 4 + 4, g, :],
                             b[:].rearrange("p (c d) -> p c d", c=4)), done, before))
                free[i] = [v_got[-1]]
            work_read[n] = [done]
        o_got = []
        for g in range(NH):
            def take(c, half, b, done):
                o_got.append(act.op(lambda e, g=g: e.activation(o_all[:, g, cut(half)], b[:], ACT.Tanh, scale=0.5), done, before))
                return o_got[-1]
            outputs(("o", g), DT, P, h3, h3_got, take)
        l_sz, l_szin = [landing("sz0"), landing("sz1")], landing("szin")
        sz_out = [None, None]
        for g in range(NH):
            w0, n, parts = work[g % 2], g % 2, []

            def take(c, half, b, done, w0=w0):
                t = act.op(lambda e: e.activation(w0[:, cut(half)], b[:], ACT.Tanh, scale=0.5), done, work_read[n])
                parts.append(dve.op(lambda e: e.scalar_tensor_tensor(w0[:, cut(half)], w0[:, cut(half)], 1.0, b[:], ALU.add, ALU.mult), t))
                return parts[-1]
            h3_last = outputs(("za", g), DT, P, h3, h3_got, take)
            sz_out[n] = sp.dma(lambda e, g=g, w0=w0: e.dma_start(sz_dram[g], w0[:, 0:SEQ]), l_sz[n], parts)
            work_read[n] = [sz_out[n]]

        NP, PAIR = NT // 2, 2 * P
        both = lambda p: slice(p * PAIR, (p + 1) * PAIR)
        mb = sb("mb", "h", 0, [P, NH, SEQ])
        nb = sb("nb", "h", 16 * KB, [P, NH, SEQ])
        set_ring(7)
        mb_got, nb_got, wa_got = [], [], []
        for p in range(NP):
            mb_got.append(sp.dma(lambda e, p=p: e.dma_start(mb[:, :, both(p)], rows_dram[0, :, both(p)].partition_broadcast(P)),
                                 landing(f"mb{p}"), h3_last, rows_out))
            nb_got.append(sp.dma(lambda e, p=p: e.dma_start(nb[:, :, both(p)], rows_dram[1, :, both(p)].partition_broadcast(P)),
                                 landing(f"nb{p}"), h3_last, rows_out))
        o = 32 * KB
        buf = {}
        for name in ("dec", "qa", "pts", "kts"):
            for n in range(2):
                buf[name, n] = sb(f"{name}{n}", "h", o, [P, NH, P]); o += 2048
        dens = sb("dens", "h", o, [P, NH, P]); o += 2048
        sqs = sb("sqs", "h", o, [P, NH, P]); o += 2048
        mean_sq = sb("mean_sq", "h", o, [P, P]); o += 512
        x3 = [sb(f"x3_{n}", "h", o + 4096 * n, [P, D]) for n in range(2)]
        state = sb("state", "g", 64 * KB, [P, NH, P])
        nstate = sb("nstate", "g", 66 * KB, [P, 8])
        grow = sb("grow", "g", 66 * KB + 64, [P, D])
        sz = sb("sz", "g", 16 * KB, [P, NH, SEQ])
        ya_hi = sb("ya_hi", "g", 32 * KB, [P, NP, NH, PAIR], F32R)
        ya_lo = sb("ya_lo", "g", 0, [P, NH, SEQ], F32R)
        mean_got = dve.op(lambda e: e.memset(mean_sq[:], 1.0 / HD), h3_last)

        last_blocks = [weights(("oa", c))[0] for c in range(3)]
        last_raw = sb("last_raw", "h", o, [P, NH, PAIR])
        last_hi, last_lo = (sb(f"last_{n}", "raw", 4096 * m, [P, NH, PAIR], F32R) for m, n in enumerate(("hi", "lo")))
        late = {}

        def late_loads():
            t = sp.dma(lambda e: e.dma_start(last_raw[:], w_out2[0:GROUP, 3 * PAIR:4 * PAIR].rearrange("(k p) c -> p k c", p=P)),
                       landing("last_raw"), h3_last)
            late["gain"] = sp.dma(lambda e: e.dma_start(grow[:], A["final_norm_g_2"].partition_broadcast(P)), landing("grow"), sz_out,
                                  work_read)
            t = split_value(last_hi[:], last_lo[:], last_raw[:], [t], raw_free)
            last_blocks.append((last_hi, last_lo, t))
            x3_read[:] = t, t

        xc_view = xcol[:].rearrange("p (c h) -> p h c", h=NH)
        w_view, a_view = wcol[:].rearrange("p (h c) -> p h c", h=NH), acol[:].rearrange("p (h c) -> p h c", h=NH)
        mp_view = mprev[:].rearrange("p (h c) -> p h c", h=NH)
        flat2 = lambda t: t[:].rearrange("p h t -> p (h t)")
        read = {k: [] for k in buf}
        dens_read, sqs_read = [None], [None]
        state_got, state_read = [[]], [sz_out, work_read]
        ready_front, v2_got, sn_got, keys_read, values_read = [None] * NT, [None] * NT, [None] * NT, [None] * NT, [None] * NT

        def front(c):
            n, p, tok = c % 2, c // 2, slice(c * P, (c + 1) * P)
            mbc = mb[:, :, tok]
            dec, qa, pts, kts = (buf[name, n] for name in ("dec", "qa", "pts", "kts"))
            if c % 2 == 0:
                cs, ends = slice(c, c + 2), mb[:, :, c * P + P - 1:(c + 2) * P:P]
                t = dve.op(lambda e: e.tensor_tensor(w_view[:, :, cs], xc_view[:, :, cs], ends, ALU.subtract), mb_got[p], xcol_got)
                w = act.op(lambda e: e.activation(w_view[:, :, cs], w_view[:, :, cs], ACT.Exp), t)
                t = dve.op(lambda e: e.tensor_tensor(a_view[:, :, cs], mp_view[:, :, cs], ends, ALU.subtract), mb_got[p], mp_got)
                wa_got.append([w, act.op(lambda e: e.activation(a_view[:, :, cs], a_view[:, :, cs], ACT.Exp), t)])
            t = dve.op(lambda e: e.tensor_tensor(dec[:], mask[:].unsqueeze(1).broadcast_to([P, NH, P]), mbc, ALU.subtract),
                       mask_got, mb_got[p], read["dec", n])
            for g in range(NH):
                dec_got = act.op(lambda e, g=g: e.activation(dec[:, g, :], dec[:, g, :], ACT.Exp, bias=xcol[:, c * NH + g:c * NH + g + 1]),
                                 t, xcol_got)
            i, b, was = bank()
            for g in range(NH):
                done = pe.op(lambda e, g=g: e.matmul(b[:, g * P:(g + 1) * P], k_all[:, g, tok], q_all[:, g, tok], start=True,
                                                     stop=True), was, q_got, k_got, inc=g == NH - 1)
            p_got = dve.op(lambda e: e.tensor_tensor(flat2(pts), b[:], flat2(dec), ALU.mult), done, dec_got, read["pts", n])
            free[i] = [p_got]
            read["dec", n] = [p_got]
            i, b2, was = bank()
            for g in range(NH):
                done = pe.op(lambda e, g=g: e.transpose(b2[:, g * P:(g + 1) * P], k_all[:, g, tok], ident[:]), was, k_got, inc=g == NH - 1)
            keys_read[c] = done
            for g in range(NH):
                kt_got = act.op(lambda e, g=g: e.activation(kts[:, g, :], b2[:, g * P:(g + 1) * P], ACT.Copy,
                                scale=wcol[:, g * NT + c:g * NT + c + 1]), done, wa_got[p], read["kts", n])
            free[i] = [kt_got]
            qa_got = None
            if c:
                for g in range(NH):
                    t = act.op(lambda e, g=g: e.activation(qa[:, g, :], mbc[:, g, :], ACT.Exp, scale=-1.0,
                               bias=mprev[:, g * NT + c:g * NT + c + 1]), mb_got[p], mp_got, read["qa", n])
                qa_got = dve.op(lambda e: e.tensor_tensor(qa[:], qa[:], q_all[:, :, tok], ALU.mult), t, q_got)
            ready_front[c] = (p_got, kt_got, qa_got)

        def back(c):
            n, p, tok = c % 2, c // 2, slice(c * P, (c + 1) * P)
            qa, pts, kts = (buf[name, n] for name in ("qa", "pts", "kts"))
            p_got, kt_got, qa_got = ready_front[c]
            o_view = o_all[:, :, tok]
            i, b, was = bank()
            for g in range(NH):
                done = pe.op(lambda e, g=g: e.matmul(b[:, g * P:(g + 1) * P], v_tok[:, c, g, :], pts[:, g, :], start=True, stop=c == 0,
                                                     skip_group_check=True), was, p_got, v_got, inc=g == NH - 1)
                if c:
                    done = pe.op(lambda e, g=g: e.matmul(b[:, g * P:(g + 1) * P], state[:, g, :], qa[:, g, :], start=False, stop=True,
                                                         skip_group_check=True), qa_got, state_got[0], inc=g == NH - 1)
            sn = dve.op(lambda e: e.scalar_tensor_tensor(o_view, o_view, 1.0, b[:].rearrange("p (h t) -> p h t", h=NH), ALU.add,
                                                         ALU.mult), done, o_got)
            free[i] = [sn]
            i, b2, was = bank()
            done = pe.op(lambda e: e.matmul(b2[:], ones_sq[:], flat2(pts), start=True, stop=c == 0, skip_group_check=True), was, p_got)
            if c:
                for g in range(NH):
                    done = pe.op(lambda e, g=g: e.matmul(b2[:, g * P:(g + 1) * P], nstate[:, g:g + 1].broadcast_to([P, P]), qa[:, g, :],
                                                         start=False, stop=g == NH - 1, skip_group_check=True), qa_got, state_got[0])
            den_done, den_i = done, i
            read["pts", n] = read["qa", n] = [done]
            i, b3, was = bank()
            for g in range(NH):
                done = pe.op(lambda e, g=g: e.matmul(b3[:, g * P:(g + 1) * P], kts[:, g, :], v_tok[:, c, g, :], start=True, stop=True),
                             was, kt_got, v_got)
            for g in range(NH):
                done = pe.op(lambda e, g=g: e.matmul(stat_bank[:, g:g + 1], kts[:, g, :], ones[:, 0:1], start=True, stop=True),
                             sum_free[1], inc=g == NH - 1)
            read["kts", n] = [done]
            values_read[c] = done
            updates = []
            for g in range(NH):
                if c == 0:
                    updates.append(dve.op(lambda e, g=g: e.tensor_copy(state[:, g, :], b3[:, g * P:(g + 1) * P]), done, state_read))
                    updates.append(dve.op(lambda e, g=g: e.tensor_copy(nstate[:, g:g + 1], stat_bank[:, g:g + 1]), done, state_read))
                else:
                    col = acol[:, g * NT + c:g * NT + c + 1]
                    updates.append(dve.op(lambda e, g=g, col=col: e.scalar_tensor_tensor(state[:, g, :], state[:, g, :], col,
                                   b3[:, g * P:(g + 1) * P], ALU.mult, ALU.add), done, wa_got[p], state_got[0]))
                    updates.append(dve.op(lambda e, g=g, col=col: e.scalar_tensor_tensor(nstate[:, g:g + 1], nstate[:, g:g + 1], col,
                                   stat_bank[:, g:g + 1], ALU.mult, ALU.add), done, wa_got[p], state_got[0]))
            free[i] = [updates]
            state_got[0] = updates
            sum_free[1] = [updates]
            t = act.op(lambda e: e.activation(dens[:], nb[:, :, tok], ACT.Exp), nb_got[p], dens_read[0])
            s = act.op(lambda e: e.activation(sqs[:], o_view, ACT.Square), sn, sqs_read[0])
            a = act.op(lambda e: e.activation(b2[:], b2[:], ACT.Abs), den_done)
            t = dve.op(lambda e: e.tensor_tensor(flat2(dens), b2[:], flat2(dens), ALU.max), t, a)
            free[den_i] = [t]
            t = act.op(lambda e: e.activation(dens[:], dens[:], ACT.Square, scale=2.0 * EPS ** 0.5), t)
            i, b4, was = bank()
            done = pe.op(lambda e: e.matmul(b4[:], mean_sq[:], flat2(sqs), start=True, stop=True), was, s, mean_got)
            sqs_read[0] = done
            v2 = dve.op(lambda e: e.tensor_tensor(q_all[:, :, tok], b4[:].rearrange("p (h t) -> p h t", h=NH), dens[:], ALU.add), done, t,
                        keys_read[c], qa_got)
            free[i] = [v2]
            dens_read[0] = v2
            v2_got[c], sn_got[c] = v2, sn

        l_out = landing("out")
        out_rows = out.rearrange("b (t p) d -> p (b t) d", p=P)
        sz_got, sums_got, x3_read, stores = [None] * NP, [None] * NT, [None, None], []
        part = small[:, 120:120 + 2 * NT].rearrange("p (t c) -> p t c", c=2)
        l_szs = [l_szin] + [landing(f"szin{p}") for p in range(1, NP)]

        def gate_load(p):
            sz_got[p] = sp.dma(lambda e: e.dma_start(sz[:, :, both(p)], sz_dram[:, :, both(p)].rearrange("h p t -> p h t")), l_szs[p],
                               sz_out, keys_read[2 * p], keys_read[2 * p + 1])

        l_outs = [l_out, landing("out1")]

        def norm_rows(tiles):
            v = stat[:, tiles[0]:tiles[-1] + 1]
            t = dve.op(lambda e: e.tensor_tensor(v, part[:, tiles[0]:tiles[-1] + 1, 0], part[:, tiles[0]:tiles[-1] + 1, 1], ALU.add),
                       [sums_got[t] for t in tiles])
            r = rstd_of(slice(tiles[0], tiles[-1] + 1), 1.0 / D, t)
            for t in tiles:
                z = dve.op(lambda e, t=t: e.scalar_tensor_tensor(x3[t % 2][:], x3[t % 2][:], stat[:, t:t + 1], grow[:], ALU.mult,
                                                                 ALU.mult), r, late["gain"])
                stores.append(sp.dma(lambda e, t=t: e.dma_start(out_rows[:, t, :], x3[t % 2][:]), l_outs[t % 2], z))
                x3_read[t % 2] = stores[-1]

        def heads_rms(tiles):
            qv = q_all[:, :, tiles[0] * P:(tiles[-1] + 1) * P]
            t = act.op(lambda e: e.activation(qv, qv, ACT.Sqrt), v2_got[tiles[0]:tiles[-1] + 1])
            return dve.op(lambda e: e.reciprocal(qv, qv), t)

        def gate_heads(tiles, t):
            tok, p = slice(tiles[0] * P, (tiles[-1] + 1) * P), tiles[0] // 2
            own = slice(tiles[0] % 2 * P, (tiles[-1] % 2 + 1) * P)
            ov, qv = o_all[:, :, tok], q_all[:, :, tok]
            for g in range(NH):
                t = dve.op(lambda e, g=g: e.scalar_tensor_tensor(ov[:, g, :], ov[:, g, :], CH("mlstm_norm_g_2", g), qv[:, g, :], ALU.mult,
                                                                 ALU.mult), t, sn_got[tiles[0]:tiles[-1] + 1])
            t = dve.op(lambda e: e.tensor_tensor(ov, ov, sz[:, :, tok], ALU.mult), t, sz_got[p])
            t = split_value(ya_hi[:, p, :, own], ya_lo[:, :, tok], ov, [t], [values_read[2 * p:2 * p + 2]])
            for tile in tiles:
                ya_got[tile] = t

        ya_got = [None] * NT

        def multiply_out(t):
            half, tok, own = t // 4, slice(t * P, (t + 1) * P), slice((t % 2) * P, (t % 2 + 1) * P)
            sums_got[t] = []
            for m in range(2):
                i, b, was = bank()
                for c in (2 * m, 2 * m + 1):
                    w_hi, w_lo, w_got = last_blocks[c]
                    terms = [(ya_hi[:, t // 2, g, own], ya_lo[:, g, tok], w_hi[:, g, :], w_lo[:, g, :], ya_got[t]) for g in range(NH)]
                    product(b[:, (c % 2) * PAIR:(c % 2 + 1) * PAIR], terms, [was, w_got], start=c % 2 == 0, stop=False)
                for q in range(4):
                    j = 4 * m + q
                    done = pe.op(lambda e, q=q, j=j, b=b: e.matmul(b[:, q * P:(q + 1) * P], y1[j][:, tok], ident[:],
                                 start=False, stop=q == 3, skip_group_check=True), y1_got[j][half], inc=q == 3)
                a = act.op(lambda e, b=b, m=m: e.activation(x3[t % 2][:, m * HALF:(m + 1) * HALF], b[:], ACT.Copy), done,
                           x3_read[t % 2])
                a = act.op(lambda e, b=b, m=m: e.activation(b[:], b[:], ACT.Square, accum_out=part[:, t, m:m + 1]), a)
                sums_got[t].append(a)
                free[i] = [a]

        front(0)
        for c in range(NT):
            if c + 1 < NT:
                front(c + 1)
                if c % 2 == 0:
                    gate_load(c // 2)
            back(c)
            if c == 0:
                late_loads()
            if c % 2 == 1:
                last = c == NT - 1
                if c >= 5:
                    norm_rows([c - 5, c - 4])
                rms = [heads_rms([c - 1]), heads_rms([c])] if last else [heads_rms([c - 1, c])]
                if last:
                    gate_heads([c - 1], rms[0])
                if c >= 3:
                    multiply_out(c - 3)
                    multiply_out(c - 2)
                gate_heads([c] if last else [c - 1, c], rms[-1])
        norm_rows([NT - 4, NT - 3])
        multiply_out(NT - 2)
        multiply_out(NT - 1)
        norm_rows([NT - 2])
        norm_rows([NT - 1])
        sp.wait(stores[-2:])
        finish(nc, ctx, pe, act, dve, pool, sp)


def finish(nc, ctx, pe, act, dve, pool, sp):
    block = ctx.enter_context(nc.Block())
    block.sync(lambda e: sp.play(e))
    block.tensor(lambda e: pe.play(e))
    block.scalar(lambda e: act.play(e))
    block.vector(lambda e: dve.play(e))
    block.gpsimd(lambda e: pool.play(e))


def kernel(**inputs):
    import numpy as np
    import concourse.bacc as bacc
    from concourse.bass_utils import run_bass_kernel_spmd

    nc = bacc.Bacc("TRN2", target_bir_lowering=False, num_devices=1)
    arrays, A = {}, {}
    tokens = np.arange(P)
    rcnt = np.ones((P, 16 * NH), np.float32)
    for g, w in enumerate(WINDOWS):
        rcnt[:, 16 * g:16 * g + w] = w / np.arange(1, w + 1, dtype=np.float32)
    constants = {"ident": np.eye(P, dtype=np.float32),
                 "mask": np.where(tokens[:, None] <= tokens[None, :], 0.0, -1.0e30).astype(np.float32),
                 "rcnt": rcnt}
    for name, a in [*inputs.items(), *constants.items()]:
        a = np.ascontiguousarray(a)
        arrays[f"in_{name}"] = a
        A[name] = nc.dram_tensor(f"in_{name}", a.shape, mybir.dt.from_np(a.dtype), kind="ExternalInput").ap()
    out = nc.dram_tensor("out_0", (1, SEQ, D), F32, kind="ExternalOutput").ap()
    build_program(nc, A, out)
    result = run_bass_kernel_spmd(nc, [arrays], core_ids=[0])
    return result.results[0]["out_0"]
```
